# Optimizing a Trainium2 kernel written in Bass

```python
import jax
import jax.numpy as jnp
from jax import lax
import numpy as np

D_MODEL = 1024
BATCH = 1
SEQ = 128
DEPTH = 2
DEC_BATCH = 1
DEC_SEQ = 512
PAST_LEN = 128

GRID_W = 64
N_EVEN = (DEPTH + 1) // 2
N_ODD = DEPTH // 2
D_FF = 2816
N_MOD = 9
CHUNK = 128
Q_BLOCK = 128
ROPE_BASE = 10000.0
H_A = 4
DK_A = 64
DV_A = 128
H_B = 8
HS_B = 64
LORA_W = 64
LORA_A = 64
LORA_G = 128
H_C = 4
DH_C = 128
HQ_D = 8
HKV_D = 2
HD_D = 64

WA = H_A * DV_A
WB = H_B * HS_B
WC = H_C * DH_C
WD = HQ_D * HD_D
P_A = 2 * H_A * DK_A + 2 * WA
P_B = 3 * WB + LORA_W + LORA_A + LORA_G
P_C = 3 * WC + 4 * H_C + WC
P_D = WD + 2 * HKV_D * HD_D

kernel_name = 'hybrid_bidir_diffusion_step'

def rms_norm(x, g, eps=1e-6):
    xf = x.astype(jnp.float32)
    y = xf * lax.rsqrt(jnp.mean(xf * xf, axis=-1, keepdims=True) + eps)
    return (y * g.astype(jnp.float32)).astype(x.dtype)

def head_layer_norm(y, eps):
    y = y.astype(jnp.float32)
    mu = jnp.mean(y, axis=-1, keepdims=True)
    var = jnp.mean(jnp.square(y - mu), axis=-1, keepdims=True)
    return (y - mu) * lax.rsqrt(var + eps)

def to_heads(p, h):
    b, l, w = p.shape
    return p.reshape(b, l, h, w // h).transpose(0, 2, 1, 3)

def from_heads(o):
    b, h, l, d = o.shape
    return o.transpose(0, 2, 1, 3).reshape(b, l, h * d)

def tflip(t):
    return jnp.flip(t, axis=2)

def center_shift(p):
    z = jnp.zeros_like(p[:, :1])
    prev = jnp.concatenate([z, p[:, :-1]], axis=1)
    nxt = jnp.concatenate([p[:, 1:], z], axis=1)
    return 0.5 * (prev + nxt)

def axial_rope(x):
    n, d = x.shape[-2], x.shape[-1]
    rows = n // GRID_W
    row = jnp.repeat(jnp.arange(rows), GRID_W).astype(jnp.float32)
    col = (jnp.arange(rows * GRID_W) % GRID_W).astype(jnp.float32)
    da = d // 2
    nf = da // 2
    inv = ROPE_BASE ** (-jnp.arange(nf, dtype=jnp.float32) / nf)

    def rot(xa, pos):
        ang = pos[:, None] * inv[None, :]
        cos = jnp.cos(ang).astype(x.dtype)
        sin = jnp.sin(ang).astype(x.dtype)
        x1, x2 = xa[..., :nf], xa[..., nf:]
        return jnp.concatenate([x1 * cos - x2 * sin, x1 * sin + x2 * cos], axis=-1)

    return jnp.concatenate([rot(x[..., :da], row), rot(x[..., da:], col)], axis=-1)

def to_chunks(x):
    b, h, l = x.shape[:3]
    x = x.reshape(b, h, l // CHUNK, CHUNK, *x.shape[3:])
    return jnp.moveaxis(x, 2, 0)

def from_chunks(x):
    x = jnp.moveaxis(x, 0, 2)
    b, h, nc, cl = x.shape[:4]
    return x.reshape(b, h, nc * cl, *x.shape[4:])

def retention_scan(q, k, v, log_g, s0):
    idx = jnp.arange(CHUNK, dtype=jnp.float32)
    diff = idx[:, None] - idx[None, :]
    causal = diff >= 0
    lg = log_g[:, None, None]
    d_intra = jnp.where(causal, jnp.exp(lg * jnp.where(causal, diff, 0.0)), 0.0)
    q_dec = jnp.exp(log_g[:, None] * (idx + 1.0))[:, :, None]
    k_dec = jnp.exp(log_g[:, None] * (CHUNK - 1.0 - idx))[:, :, None]
    c_dec = jnp.exp(log_g * CHUNK)[:, None, None]

    def step(s, inp):
        qc, kc, vc = inp
        att = jnp.einsum('bhid,bhjd->bhij', qc, kc) * d_intra
        o = jnp.einsum('bhij,bhje->bhie', att, vc) + jnp.einsum('bhid,bhde->bhie', qc * q_dec, s)
        s = s * c_dec + jnp.einsum('bhjd,bhje->bhde', kc * k_dec, vc)
        return s, o

    s_fin, o = lax.scan(step, s0, (to_chunks(q), to_chunks(k), to_chunks(v)))
    return from_chunks(o), s_fin

def mlstm_scan(q, k, v, ig, lf, c0, n0, m0):
    idx = jnp.arange(CHUNK)
    causal = idx[:, None] >= idx[None, :]

    def step(carry, inp):
        cm, nv, m = carry
        qc, kc, vc, igc, lfc = inp
        b = jnp.cumsum(lfc, axis=-1)
        a = b + m[..., None]
        dlog = jnp.where(causal, b[..., :, None] - b[..., None, :] + igc[..., None, :], -jnp.inf)
        mt = jnp.maximum(a, jnp.max(dlog, axis=-1))
        w = jnp.exp(dlog - mt[..., None])
        s = jnp.einsum('bhid,bhjd->bhij', qc, kc) * w
        inter = jnp.exp(a - mt)
        num = jnp.einsum('bhij,bhje->bhie', s, vc) + inter[..., None] * jnp.einsum('bhid,bhde->bhie', qc, cm)
        den = jnp.sum(s, axis=-1) + inter * jnp.einsum('bhid,bhd->bhi', qc, nv)
        h = num / jnp.maximum(jnp.abs(den), jnp.exp(-mt))[..., None]
        bl = b[..., -1]
        wl = bl[..., None] - b + igc
        m_new = jnp.maximum(bl + m, jnp.max(wl, axis=-1))
        wk = jnp.exp(wl - m_new[..., None])[..., None] * kc
        dec = jnp.exp(bl + m - m_new)
        cm = dec[..., None, None] * cm + jnp.einsum('bhjd,bhje->bhde', wk, vc)
        nv = dec[..., None] * nv + jnp.sum(wk, axis=2)
        return (cm, nv, m_new), h

    seqs = tuple(to_chunks(t) for t in (q, k, v, ig, lf))
    (c_f, n_f, m_f), h = lax.scan(step, (c0, n0, m0), seqs)
    return from_chunks(h), c_f, n_f, m_f

def rwkv_scan(r, w, k, v, a, b, s0):
    def step(s, inp):
        rt, wt, kt, vt, at, bt = inp
        sa = jnp.einsum('bhij,bhj->bhi', s, at)
        s = s * wt[..., None, :] + sa[..., :, None] * bt[..., None, :] + vt[..., :, None] * kt[..., None, :]
        return s, jnp.einsum('bhij,bhj->bhi', s, rt)

    seqs = tuple(jnp.moveaxis(t, 2, 0) for t in (r, w, k, v, a, b))
    s_fin, y = lax.scan(step, s0, seqs)
    return jnp.moveaxis(y, 0, 2), s_fin

def block_attention(q, k, v):
    b, hq, l, hd = q.shape
    hkv = k.shape[1]
    g = hq // hkv
    nb = l // Q_BLOCK
    qb = jnp.moveaxis(q.reshape(b, hkv, g, nb, Q_BLOCK, hd), 3, 0)
    scale = hd ** -0.5

    def one(qblk):
        s = jnp.einsum('bkgqd,bksd->bkgqs', qblk, k).astype(jnp.float32) * scale
        pr = jax.nn.softmax(s, axis=-1).astype(v.dtype)
        return jnp.einsum('bkgqs,bksd->bkgqd', pr, v)

    o = lax.map(one, qb)
    return jnp.moveaxis(o, 0, 3).reshape(b, hq, l, hd)

def retention_mixer(p, log_decay, gn_w, s0, latent):
    f32 = jnp.float32
    qk = H_A * DK_A
    q = to_heads(p[..., :qk], H_A)
    k = to_heads(p[..., qk:2 * qk], H_A)
    v = to_heads(p[..., 2 * qk:2 * qk + WA], H_A).astype(f32)
    g = p[..., 2 * qk + WA:]
    if latent:
        q = axial_rope(q)
        k = axial_rope(k)
    q = q.astype(f32)
    k = k.astype(f32) * DK_A ** -0.5
    s0 = s0.astype(f32)
    log_decay = log_decay.astype(f32)
    o_f, s_f = retention_scan(q, k, v, log_decay[0], s0[:, 0])
    o_b, s_b = retention_scan(tflip(q), tflip(k), tflip(v), log_decay[1], s0[:, 1])
    o = from_heads(head_layer_norm(o_f + tflip(o_b), 1e-5)) * gn_w
    out = jax.nn.silu(g) * o.astype(p.dtype)
    return out, jnp.stack([s_f, s_b], axis=1)

def rwkv_mixer(p, mu, w0, w2, a0, a2, g2, k_k, k_a, r_k, ln_w, ln_b, s0):
    f32 = jnp.float32
    p = p + mu * (center_shift(p) - p)
    r, k, v = p[..., :WB], p[..., WB:2 * WB], p[..., 2 * WB:3 * WB]
    o = 3 * WB
    wd = jnp.tanh(p[..., o:o + LORA_W])
    ad = p[..., o + LORA_W:o + LORA_W + LORA_A]
    gd = p[..., o + LORA_W + LORA_A:]
    g = jax.nn.sigmoid(gd) @ g2
    kk = to_heads(k * k_k, H_B).astype(f32)
    kk = kk / jnp.maximum(jnp.sqrt(jnp.sum(kk * kk, axis=-1, keepdims=True)), 1e-12)
    r_h = to_heads(r, H_B).astype(f32)
    k_h = to_heads(k, H_B).astype(f32)
    v_h = to_heads(v, H_B).astype(f32)
    ys, ss = [], []
    for d in range(2):
        w_log = -jax.nn.softplus(-(w0[d] + wd @ w2[d])) - 0.5
        decay = to_heads(jnp.exp(-jnp.exp(w_log.astype(f32))), H_B)
        a = jax.nn.sigmoid(a0[d] + ad @ a2[d])
        kd = to_heads(k * (1 + (a - 1) * k_a), H_B).astype(f32)
        a_h = to_heads(a, H_B).astype(f32)
        seqs = (r_h, decay, kd, v_h, -kk, kk * a_h)
        if d == 1:
            seqs = tuple(tflip(t) for t in seqs)
        y, s = rwkv_scan(*seqs, s0[:, d].astype(f32))
        ys.append(y if d == 0 else tflip(y))
        ss.append(s)
    y = from_heads(head_layer_norm(ys[0] + ys[1], 64e-5)) * ln_w + ln_b
    bonus = from_heads(jnp.sum(r_h * k_h * r_k[:, None, :].astype(f32), axis=-1, keepdims=True) * v_h)
    out = (y + bonus).astype(p.dtype) * g
    return out, jnp.stack(ss, axis=1)

def mlstm_mixer(p, i_bias, f_bias, norm_w, c0, n0, m0):
    f32 = jnp.float32
    bsz, seq = p.shape[0], p.shape[1]
    q = to_heads(p[..., :WC], H_C).astype(f32)
    k = to_heads(p[..., WC:2 * WC], H_C).astype(f32) * DH_C ** -0.5
    v = to_heads(p[..., 2 * WC:3 * WC], H_C).astype(f32)
    o = 3 * WC
    ig = p[..., o:o + 2 * H_C].reshape(bsz, seq, 2, H_C) + i_bias
    fg = p[..., o + 2 * H_C:o + 4 * H_C].reshape(bsz, seq, 2, H_C) + f_bias
    og = p[..., o + 4 * H_C:]
    ig = jnp.transpose(ig, (2, 0, 3, 1)).astype(f32)
    lf = jax.nn.log_sigmoid(jnp.transpose(fg, (2, 0, 3, 1)).astype(f32))
    c0 = c0.astype(f32)
    n0 = n0.astype(f32)
    m0 = m0.astype(f32)
    h_f, cf, nf, mf = mlstm_scan(q, k, v, ig[0], lf[0], c0[:, 0], n0[:, 0], m0[:, 0])
    h_b, cb, nb, mb = mlstm_scan(tflip(q), tflip(k), tflip(v), tflip(ig[1]), tflip(lf[1]),
                                 c0[:, 1], n0[:, 1], m0[:, 1])
    h = from_heads(head_layer_norm(h_f + tflip(h_b), 1e-5)) * norm_w
    out = jax.nn.sigmoid(og) * h.astype(p.dtype)
    return out, jnp.stack([cf, cb], axis=1), jnp.stack([nf, nb], axis=1), jnp.stack([mf, mb], axis=1)

def attention_mixer(p, qk_gain, ctx_k, ctx_v, latent):
    kvw = HKV_D * HD_D
    q = to_heads(p[..., :WD], HQ_D)
    k = to_heads(p[..., WD:WD + kvw], HKV_D)
    v = to_heads(p[..., WD + kvw:], HKV_D)
    q = rms_norm(q, qk_gain[0])
    k = rms_norm(k, qk_gain[1])
    if latent:
        q = axial_rope(q)
        k_lat = axial_rope(k)
        keys = jnp.concatenate([ctx_k.astype(k.dtype), k_lat], axis=2)
        vals = jnp.concatenate([ctx_v.astype(v.dtype), v], axis=2)
    else:
        keys, vals = k, v
    o = block_attention(q, keys, vals)
    return from_heads(o), k, v

def modulation(cond, ada_w, ada_b):
    m = jax.nn.silu(cond) @ ada_w + ada_b
    return jnp.split(m[:, None, :], N_MOD, axis=-1)

def swiglu(h, w1, w2):
    gate, up = jnp.split(h @ w1, 2, axis=-1)
    return (jax.nn.silu(gate) * up) @ w2

def setup_inputs(seed: int = 0) -> dict:
    key = jax.random.key(seed)
    ks = iter(jax.random.split(key, 48))
    f32 = jnp.float32

    def nrm(shape, scale=1.0):
        return jax.random.normal(next(ks), shape, f32) * scale

    d = D_MODEL
    ret_base = jnp.log1p(-(2.0 ** (-5.0 - jnp.arange(H_A, dtype=f32))))
    w0_base = jnp.repeat(jnp.linspace(-6.0, -0.5, HS_B)[None, :], H_B, axis=0).reshape(-1)
    return {
        'x_prompt': nrm((BATCH, SEQ, d)),
        'x_sample': nrm((DEC_BATCH, DEC_SEQ, d)),
        'state_ret': nrm((DEC_BATCH, N_EVEN, 2, H_A, DK_A, DV_A), 0.5),
        'state_rwkv': nrm((DEC_BATCH, N_EVEN, 2, H_B, HS_B, HS_B), 0.3),
        'state_mlstm_c': nrm((DEC_BATCH, N_ODD, 2, H_C, DH_C, DH_C), 0.3),
        'state_mlstm_n': nrm((DEC_BATCH, N_ODD, 2, H_C, DH_C), 0.3),
        'state_mlstm_m': nrm((DEC_BATCH, N_ODD, 2, H_C), 0.5),
        'cache_k': nrm((DEC_BATCH, N_ODD, HKV_D, PAST_LEN, HD_D)),
        'cache_v': nrm((DEC_BATCH, N_ODD, HKV_D, PAST_LEN, HD_D)),
        'c': nrm((DEC_BATCH, d)),
        'c_ctx': nrm((d,)),
        'ada_w': nrm((DEPTH, d, N_MOD * d), 0.5 * d ** -0.5),
        'ada_b': nrm((DEPTH, N_MOD * d), 0.02),
        'norm_g': 1.0 + nrm((DEPTH, 3, d), 0.02),
        'ffn_w1': nrm((DEPTH, 2, d, 2 * D_FF), d ** -0.5),
        'ffn_w2': nrm((DEPTH, 2, D_FF, d), D_FF ** -0.5),
        'w_in_even': nrm((N_EVEN, d, P_A + P_B), d ** -0.5),
        'w_out_even': nrm((N_EVEN, WA + WB, d), (WA + WB) ** -0.5),
        'ret_log_decay': ret_base[None, None, :] * (1.0 + nrm((N_EVEN, 2, H_A), 0.05)),
        'ret_gn_w': 1.0 + nrm((N_EVEN, WA), 0.02),
        'rwkv_mu': 0.5 + nrm((N_EVEN, P_B), 0.1),
        'rwkv_w0': w0_base[None, None, :] + nrm((N_EVEN, 2, WB), 0.1),
        'rwkv_w2': nrm((N_EVEN, 2, LORA_W, WB), 0.1 * LORA_W ** -0.5),
        'rwkv_a0': nrm((N_EVEN, 2, WB), 0.1),
        'rwkv_a2': nrm((N_EVEN, 2, LORA_A, WB), LORA_A ** -0.5),
        'rwkv_g2': nrm((N_EVEN, LORA_G, WB), LORA_G ** -0.5),
        'rwkv_k_k': 0.85 + nrm((N_EVEN, WB), 0.02),
        'rwkv_k_a': 1.0 + nrm((N_EVEN, WB), 0.02),
        'rwkv_r_k': nrm((N_EVEN, H_B, HS_B), 0.1),
        'rwkv_ln_w': 1.0 + nrm((N_EVEN, WB), 0.02),
        'rwkv_ln_b': nrm((N_EVEN, WB), 0.02),
        'w_in_odd': nrm((N_ODD, d, P_C + P_D), d ** -0.5),
        'w_out_odd': nrm((N_ODD, WC + WD, d), (WC + WD) ** -0.5),
        'mlstm_i_bias': nrm((N_ODD, 2, H_C), 0.1),
        'mlstm_f_bias': jnp.linspace(3.0, 6.0, H_C)[None, None, :] + nrm((N_ODD, 2, H_C), 0.1),
        'mlstm_norm_w': 1.0 + nrm((N_ODD, WC), 0.02),
        'attn_qk_norm': 1.0 + nrm((N_ODD, 2, HD_D), 0.02),
        'final_norm': 1.0 + nrm((d,), 0.02),
    }

def reference(x_prompt, x_sample, state_ret, state_rwkv, state_mlstm_c, state_mlstm_n, state_mlstm_m,
              cache_k, cache_v, c, c_ctx, ada_w, ada_b, norm_g, ffn_w1, ffn_w2, w_in_even, w_out_even,
              ret_log_decay, ret_gn_w, rwkv_mu, rwkv_w0, rwkv_w2, rwkv_a0, rwkv_a2, rwkv_g2, rwkv_k_k,
              rwkv_k_a, rwkv_r_k, rwkv_ln_w, rwkv_ln_b, w_in_odd, w_out_odd, mlstm_i_bias, mlstm_f_bias,
              mlstm_norm_w, attn_qk_norm, final_norm):
    f32 = jnp.float32

    def layer(x, cond, l, latent, st):
        sh1, sc1, gt1, sh2, sc2, gt2, sh3, sc3, gt3 = modulation(cond, ada_w[l], ada_b[l])
        h = rms_norm(x, norm_g[l, 0]) * (1 + sc1) + sh1
        x = x + 0.5 * gt1 * swiglu(h, ffn_w1[l, 0], ffn_w2[l, 0])
        h = rms_norm(x, norm_g[l, 1]) * (1 + sc2) + sh2
        if l % 2 == 0:
            e = l // 2
            p = h @ w_in_even[e]
            out_a, s_ret = retention_mixer(p[..., :P_A], ret_log_decay[e], ret_gn_w[e], st[0], latent)
            out_b, s_rwkv = rwkv_mixer(p[..., P_A:], rwkv_mu[e], rwkv_w0[e], rwkv_w2[e], rwkv_a0[e],
                                       rwkv_a2[e], rwkv_g2[e], rwkv_k_k[e], rwkv_k_a[e], rwkv_r_k[e],
                                       rwkv_ln_w[e], rwkv_ln_b[e], st[1])
            mix = jnp.concatenate([out_a, out_b], axis=-1) @ w_out_even[e]
            new = (s_ret, s_rwkv)
        else:
            o = l // 2
            p = h @ w_in_odd[o]
            out_c, s_c, s_n, s_m = mlstm_mixer(p[..., :P_C], mlstm_i_bias[o], mlstm_f_bias[o],
                                               mlstm_norm_w[o], st[0], st[1], st[2])
            out_d, k_ctx, v_ctx = attention_mixer(p[..., P_C:], attn_qk_norm[o], st[3], st[4], latent)
            mix = jnp.concatenate([out_c, out_d], axis=-1) @ w_out_odd[o]
            new = (s_c, s_n, s_m, k_ctx, v_ctx)
        x = x + gt2 * mix
        h = rms_norm(x, norm_g[l, 2]) * (1 + sc3) + sh3
        x = x + 0.5 * gt3 * swiglu(h, ffn_w1[l, 1], ffn_w2[l, 1])
        return x, new

    bp = x_prompt.shape[0]
    cond_ctx = c_ctx[None, :]
    xp, xs = x_prompt, x_sample
    ret_l, rwkv_l, mc_l, mn_l, mm_l, k_l, v_l = [], [], [], [], [], [], []
    for l in range(DEPTH):
        if l % 2 == 0:
            e = l // 2
            zeros = (jnp.zeros((bp, 2, H_A, DK_A, DV_A), f32), jnp.zeros((bp, 2, H_B, HS_B, HS_B), f32))
            xp, (s_ret, s_rwkv) = layer(xp, cond_ctx, l, False, zeros)
            ret_l.append(s_ret)
            rwkv_l.append(s_rwkv)
            xs, _ = layer(xs, c, l, True, (state_ret[:, e], state_rwkv[:, e]))
        else:
            o = l // 2
            zeros = (jnp.zeros((bp, 2, H_C, DH_C, DH_C), f32), jnp.zeros((bp, 2, H_C, DH_C), f32),
                     jnp.zeros((bp, 2, H_C), f32), None, None)
            xp, (s_c, s_n, s_m, k_ctx, v_ctx) = layer(xp, cond_ctx, l, False, zeros)
            mc_l.append(s_c)
            mn_l.append(s_n)
            mm_l.append(s_m)
            k_l.append(k_ctx)
            v_l.append(v_ctx)
            xs, _ = layer(xs, c, l, True, (state_mlstm_c[:, o], state_mlstm_n[:, o], state_mlstm_m[:, o],
                                           cache_k[:, o], cache_v[:, o]))
    y_prompt = rms_norm(xp, final_norm)
    y_sample = rms_norm(xs, final_norm)
    new_state_ret = jnp.stack(ret_l, axis=1)
    new_state_rwkv = jnp.stack(rwkv_l, axis=1)
    new_state_mlstm_c = jnp.stack(mc_l, axis=1)
    new_state_mlstm_n = jnp.stack(mn_l, axis=1)
    new_state_mlstm_m = jnp.stack(mm_l, axis=1)
    new_cache_k = jnp.stack(k_l, axis=1)
    new_cache_v = jnp.stack(v_l, axis=1)
    return (y_prompt, y_sample, new_state_ret, new_state_rwkv, new_state_mlstm_c, new_state_mlstm_n,
            new_state_mlstm_m, new_cache_k, new_cache_v)


_drawn_inputs = setup_inputs


def setup_inputs(seed=0):
    import zlib

    import numpy as np

    out = dict(_drawn_inputs(seed))
    spreads = {}
    factors = {'state_ret': 3.108,
     'state_rwkv': 8.0,
     'state_mlstm_c': 3.283,
     'state_mlstm_n': 6.895,
     'state_mlstm_m': 8.0,
     'cache_k': 8.0,
     'cache_v': 8.0,
     'ret_gn_w': 8.0,
     'rwkv_w2': 5.977,
     'rwkv_ln_w': 8.0,
     'rwkv_ln_b': 8.0,
     'mlstm_norm_w': 8.0,
     'attn_qk_norm': 2.749,
     'final_norm': 2.722}
    for name, (base, spread) in spreads.items():
        noise = np.random.default_rng([zlib.crc32(name.encode()), seed]).standard_normal(out[name].shape)
        drawn = base * np.exp(spread * noise) if base else spread * noise
        out[name] = jnp.asarray(drawn.astype(out[name].dtype))
    for name, factor in factors.items():
        out[name] = (out[name] * factor).astype(out[name].dtype)
    return out
```

```python
from contextlib import ExitStack

import numpy as np
import concourse.bass as bass
from concourse import mybir

F32 = mybir.dt.float32
ALU = mybir.AluOpType
ACT = mybir.ActivationFunctionType
AX = mybir.AxisListType

P = 128
D_MODEL, D_FF, N_MOD, DEPTH = 1024, 2816, 9, 2
SEQ, DEC_SEQ, PAST = 128, 512, 128
NT = SEQ + DEC_SEQ
NCH = NT // P
DB = D_MODEL // P
FB = D_FF // P
HALF_K = FB // 2
RING = 4
ARENA = 29900
SETS = 4
EPS = 1e-6
GRID_W, ROPE_BASE = 64, 10000.0
HS = 64
LEVELS = 7
DECAY_MAX = float(np.exp(-0.5))

PROMPT = slice(0, SEQ)
SAMPLE = slice(SEQ, NT)

PROJECTIONS = ("ret", "rwkv", "mlstm", "att")
RET_BLOCKS, RWKV_BLOCKS = 12, 14
MLSTM_BLOCKS, ATT_BLOCKS = 18, 7


def const_layout():
    r = np.arange(P)
    row, col = r[:, None], r[None, :]
    parts = {
        "ident": (row == col),
        "ones": np.ones((P, P)),
        "ones64": (row // HS == col // HS),
        "mask_f": np.concatenate([row < col, row <= col], 1),
        "mask_b": np.concatenate([row > col, row >= col], 1),
    }
    lv = []
    for b in (1 << n for n in range(LEVELS)):
        same = row // (2 * b) == col // (2 * b)
        lv.append(same & (row % (2 * b) < b) & (col % (2 * b) >= b))
    parts["merge_f"] = np.concatenate(lv, 1)
    parts["merge_b"] = np.concatenate([m.T for m in lv], 1)
    perm = np.zeros((P, P))
    for m in range(P):
        if m % 32 < 16:
            perm[m + 16, m] = -1.0
        else:
            perm[m - 16, m] = 1.0
    parts["turn"] = perm
    nf = HS // 4
    inv = (np.float32(ROPE_BASE) ** (-np.arange(nf, dtype=np.float32) / np.float32(nf))).astype(np.float32)
    t = np.arange(DEC_SEQ)
    pos = np.where((r % HS < HS // 2)[:, None], (t // GRID_W)[None, :], (t % GRID_W)[None, :]).astype(np.float32)
    ang = pos * inv[r % nf][:, None]
    parts["cos"] = np.cos(ang)
    parts["sin"] = np.sin(ang)
    parts["ahead"] = np.maximum(col - row, 0)
    parts["behind"] = np.maximum(row - col, 0)
    parts["from1"] = np.broadcast_to(col + 1, (P, P))
    parts["to1"] = np.broadcast_to(P - col, (P, P))
    parts["left_f"] = (P - 1) - row
    parts["left_b"] = row
    parts["neg_f"] = np.where(row <= col, 0.0, -1e30)
    parts["neg_b"] = np.where(row >= col, 0.0, -1e30)
    at, cols = {}, 0
    for k, v in parts.items():
        at[k] = (cols, cols + v.shape[1])
        cols += v.shape[1]
    return at, np.concatenate([np.asarray(v, np.float32) for v in parts.values()], 1)


PARAM_COLS = [("norm_g", DEPTH * 3 * DB), ("final", DB), ("ada_b", DEPTH * N_MOD * DB), ("gn_w", 4), ("mu", 14),
              ("w0", 8), ("a0", 8), ("k_k", 4), ("k_a", 4), ("r_k", 4), ("ln_w", 4), ("ln_b", 4), ("mn_w", 4),
              ("q_gain", 1), ("k_gain", 1), ("lg_head", 8), ("lg_part", 4), ("m_init", 1), ("i_bias", 1),
              ("f_bias", 1), ("cond", 2 * DB)]


def param_layout():
    at, cols = {}, 0
    for k, n in PARAM_COLS:
        at[k] = (cols, cols + n)
        cols += n
    return at, cols


def stages_of_layer(layer):
    mixers = [("ret", RET_BLOCKS, 1), ("rwkv", RWKV_BLOCKS, 1)] if layer == 0 else \
             [("mlstm", MLSTM_BLOCKS, 1), ("att", ATT_BLOCKS, 1)]
    return [("ada", N_MOD * DB, 1),
            ("norm0", 1, 0), ("up0", 2 * FB, 1), ("down0", DB, 2),
            ("norm1", 1, 0)] + mixers + [("out", DB, 1),
            ("norm2", 1, 0), ("up1", 2 * FB, 1), ("down1", DB, 2)]


def build(nc, w, x_in, consts_in, params_in, lora_in, st, outs, stop=None):
    cat, _ = const_layout()
    pat, npar = param_layout()

    tile0, blk0, free0 = {}, {}, {}
    tiles = blks = 0
    freed = {"dve": SETS, "act": SETS}
    for layer in range(DEPTH):
        for name, blocks, per in stages_of_layer(layer):
            tile0[layer, name], blk0[layer, name] = tiles, blks
            free0[layer, name] = dict(freed)
            freed["act" if name in PROJECTIONS else "dve"] += 1 if name == "ada" else blocks
            tiles += blocks * per
            blks += 1 if name == "ada" else blocks
    blk0[DEPTH, "norm"], free0[DEPTH, "norm"] = blks, dict(freed)

    with ExitStack() as ctx:
        def sb(name, shape):
            return ctx.enter_context(nc.sbuf_tensor(name, shape, F32))

        def sem(name):
            return ctx.enter_context(nc.semaphore(name))

        cst = sb("cst", [P, max(b for _, b in cat.values())])
        par = sb("par", [P, npar])
        x = sb("x", [P, DB, NT])
        h = sb("h", [P, DB, NT])
        ring = sb("ring", [P, RING, HALF_K * P])
        lora = sb("lora", [P, 3, 512])
        mod = sb("mod", [P, N_MOD * DB, 2])
        gs = sb("gs", [P, 3, DB, 2])
        scond = sb("scond", [P, DB, 2])
        rs = sb("rs", [P, NT])
        arena = sb("arena", [P, ARENA])
        ps = ctx.enter_context(nc.psum_tensor("ps", [P, 8 * 512], F32))

        def C(name, rows=P):
            a, b = cat[name]
            return cst[0:rows, a:b]

        def prm(name, i=0, n=1, rows=P):
            a, _ = pat[name]
            return par[0:rows, a + i:a + i + n]

        def over(ap, n):
            return ap.unsqueeze(2).to_broadcast([ap.shape[0], ap.shape[1], n])

        def each(ap, n):
            return ap.unsqueeze(1).to_broadcast([ap.shape[0], n, ap.shape[1]])

        def pair(s):
            at = 1024 * s
            return ps[:, at + 384:at + 512], ps[:, at + 512:at + 1024], ps[:, at + 384:at + 1024]

        def bank(b, lo=0, hi=512):
            return ps[:, 512 * b + lo:512 * b + hi]

        def grid(ap, *dims):
            names = "abcde"[:len(dims)]
            return ap.rearrange(f"p ({' '.join(names)}) -> p {' '.join(names)}",
                                **{k: d for k, d in zip(names[1:], dims[1:])})

        class Area:

            def __init__(self, at=0):
                self.at = at

            def take(self, *dims):
                n = int(np.prod(dims))
                v = arena[:, self.at:self.at + n]
                self.at += n
                assert self.at <= ARENA, self.at
                return grid(v, *dims) if len(dims) > 1 else v

        ff = Area()
        gated = ff.take(FB, NT)
        silu = ff.take(2, NT)

        def chunk(c):
            return slice(c * P, (c + 1) * P)

        ORDER = ([0, 1, 2, 3, 4], [0, 4, 3, 2, 1])

        loaded = sem("loaded")
        land = [sem(f"land{r}") for r in range(RING)]
        tiles_done = sem("tiles_done")
        norm_ready = sem("norm_ready")
        free_dve = sem("free_dve")
        free_act = sem("free_act")
        silu_ready = sem("silu_ready")
        gated_ready = sem("gated_ready")
        cond_ready = sem("cond_ready")
        mod_ready = sem("mod_ready")
        x_ready = sem("x_ready")
        sq_ready = sem("sq_ready")
        ms_ready = sem("ms_ready")
        root_ready = sem("root_ready")
        scaled = sem("scaled")
        h_ready = sem("h_ready")
        proj_ready = sem("proj_ready")
        mix_ready = sem("mix_ready")
        y_ready = sem("y_ready")
        stored = sem("stored")
        dve_chain = sem("dve_chain")
        act_chain = sem("act_chain")
        pool_chain = sem("pool_chain")

        class Order:

            def __init__(self, eng, s):
                self.eng, self.s, self.n = eng, s, 0

            def __call__(self, ins):
                self.n += 1
                ins.then_inc(self.s, 1)
                self.eng.wait_ge(self.s, self.n)

        def looped(eng, n, body):
            if n // 4 > 1:
                with eng.Fori(0, n // 4) as i:
                    for u in range(4):
                        body(i, u)
            elif n // 4:
                for u in range(4):
                    body(0, u)
            for u in range(n % 4):
                body(n // 4, u)

        mx = Area()
        mix = mx.take(DB, NT)
        saved = sem("saved")
        first = sem("first")

        hn_mean = sem("hn_mean")
        hn_cent = sem("hn_cent")
        hn_sq = sem("hn_sq")
        hn_var = sem("hn_var")
        hn_ms = sem("hn_ms")
        hn_root = sem("hn_root")

        def tensor_head_norm(pe, q, src, table, tmp):
            for stage, go, done in ((src, None, hn_mean), (tmp, hn_sq, hn_var)):
                for b in range(4):
                    if go is not None:
                        pe.wait_ge(go, 4 * q + b + 1)
                    pr, sa, _ = pair(b)
                    pe.matmul(pr, table, stage[:, b, PROMPT], start=True, stop=True)
                    pe.matmul(sa, table, stage[:, b, SAMPLE], start=True, stop=True).then_inc(done, 1)

        def scalar_head_norm(act, q, src, tmp):
            for b in range(4):
                act.wait_ge(hn_cent, 4 * q + b + 1)
                act.activation(tmp[:, b, :], src[:, b, :], ACT.Square).then_inc(hn_sq, 1)
            for b in range(4):
                act.wait_ge(hn_ms, 4 * q + b + 1)
                act.activation(tmp[:, b, :], tmp[:, b, :], ACT.Sqrt).then_inc(hn_root, 1)

        def vector_head_norm(dve, turn, q, src, tmp, n, eps, weight):
            for b in range(4):
                dve.wait_ge(hn_mean, 4 * q + b + 1)
                dve.scalar_tensor_tensor(out=src[:, b, :], in0=pair(b)[2], scalar=-1.0 / n, in1=src[:, b, :],
                                         op0=ALU.mult, op1=ALU.add).then_inc(hn_cent, 1)
            for b in range(4):
                dve.wait_ge(hn_var, 4 * q + b + 1)
                dve.tensor_scalar(tmp[:, b, :], pair(b)[2], 1.0 / n, eps, ALU.mult, ALU.add).then_inc(hn_ms, 1)
            for b in range(4):
                dve.wait_ge(hn_root, 4 * q + b + 1)
                turn(dve.reciprocal(tmp[:, b, :], tmp[:, b, :]))
                turn(dve.scalar_tensor_tensor(out=src[:, b, :], in0=src[:, b, :], scalar=prm(weight, b),
                                              in1=tmp[:, b, :], op0=ALU.mult, op1=ALU.mult))

        ra = Area(mx.at)
        rt_p = ra.take(RET_BLOCKS, NT)
        rt_v = ra.take(NCH, 512)
        rt_k = ra.take(2, NCH, 256)
        rt_decay = ra.take(4, P)
        rt_back = ra.take(4, P)
        rt_qdec = ra.take(4, P)
        rt_q = ra.take(2, 4, P)
        rt_att = ra.take(2, 4, P)
        rt_s = ra.take(2, NCH, 2, P)
        rt_end = ra.take(2, 2, P)
        rt_kdec = ra.take(8)
        rt_cdec = ra.take(4)
        rt_rope = ra.take(2, DEC_SEQ)

        rt_tab = sem("rt_tab")
        rt_turned = sem("rt_turned")
        rt_roped = sem("rt_roped")
        rt_vt = sem("rt_vt")
        rt_v_ready = sem("rt_v_ready")
        rt_kt = sem("rt_kt")
        rt_k_ready = sem("rt_k_ready")
        rt_zero = sem("rt_zero")
        rt_upd = sem("rt_upd")
        rt_state = sem("rt_state")
        rt_qs = sem("rt_qs")
        rt_score = sem("rt_score")
        rt_weighed = sem("rt_weighed")
        rt_o = sem("rt_o")
        rt_out = sem("rt_out")
        rt_silu = sem("rt_silu")
        RT_UPD = [(d, i) for d in range(2) for i in range(NCH - 1)]

        def pool_retention(pool):
            pool.wait_ge(x_ready, DB)
            for d in range(2):
                pool.memset(rt_s[:, d, 0, :, :], 0.0).then_inc(rt_zero, 1)
                pool.dma_start(rt_s[:, d, ORDER[d][1], :, :], st["s_ret"][d]).then_inc(first, 16)
            for d in range(2):
                pool.wait_ge(rt_state, (NCH - 1) * d + 1)
                pool.dma_start(outs["ret"][d], rt_end[:, d, :, :]).then_inc(saved, 16)

        def tensor_retention(pe):
            pe.wait_ge(proj_ready, RET_BLOCKS)
            for b in range(4):
                pe.matmul(bank(b), C("turn"), rt_p[:, b, SAMPLE], start=True, stop=True).then_inc(rt_turned, 1)
            for c in range(NCH):
                if c >= 2:
                    pe.wait_ge(rt_v_ready, c - 1)
                for b in range(4):
                    ins = pe.transpose(bank(4 + c % 2, b * P, b * P + P), rt_p[:, 4 + b, chunk(c)], C("ident"))
                ins.then_inc(rt_vt, 1)
            pe.wait_ge(rt_roped, 4)
            for c in range(NCH):
                if c >= 2:
                    pe.wait_ge(rt_k_ready, c - 1)
                for b in range(2):
                    ins = pe.transpose(bank(6 + c % 2, b * P, b * P + P), rt_p[:, 2 + b, chunk(c)], C("ident"))
                ins.then_inc(rt_kt, 1)
            pe.wait_ge(rt_v_ready, NCH)
            pe.wait_ge(rt_k_ready, NCH)
            for n, (d, i) in enumerate(RT_UPD):
                c = ORDER[d][i]
                for hd in range(4):
                    lo, b = HS * (hd % 2), hd // 2
                    ins = pe.matmul(bank(n, b * P, b * P + P)[lo:lo + HS], rt_k[:, d, c, hd * HS:hd * HS + HS],
                                    rt_v[:, c, hd * P:hd * P + P], start=True, stop=True)
                ins.then_inc(rt_upd, 1)
            pe.wait_ge(rt_state, 2 * (NCH - 1))
            pe.wait_ge(first, 32)
            pe.wait_ge(rt_zero, 2)

            def scores(c):
                if c >= 2:
                    pe.wait_ge(rt_weighed, c - 1)
                for hd in range(4):
                    lo, b = HS * (hd % 2), hd // 2
                    ins = pe.matmul(bank(4 * (c % 2) + hd % 2, b * P, b * P + P), rt_p[lo:lo + HS, 2 + b, chunk(c)],
                                    rt_p[lo:lo + HS, b, chunk(c)], start=True, stop=True)
                ins.then_inc(rt_score, 1)

            def output(c):
                if c >= 2:
                    pe.wait_ge(rt_out, c - 1)
                pe.wait_ge(rt_weighed, c + 1)
                pe.wait_ge(rt_qs, c + 1)
                for hd in (0, 2, 1, 3):
                    lo, b = HS * (hd % 2), hd // 2
                    out = bank(4 * (c % 2) + 2 + hd % 2, b * P, b * P + P)
                    pe.matmul(out, rt_v[:, c, hd * P:hd * P + P], rt_att[:, c % 2, 2 * (hd % 2) + b, :],
                              start=True, stop=False)
                    for d in range(2):
                        ins = pe.matmul(out, rt_s[lo:lo + HS, d, c, b, :], rt_q[lo:lo + HS, c % 2, 2 * d + b, :],
                                        start=False, stop=(d == 1))
                ins.then_inc(rt_o, 1)

            scores(0)
            for c in range(NCH):
                if c + 1 < NCH:
                    scores(c + 1)
                output(c)
            pe.wait_ge(rt_out, NCH)
            tensor_head_norm(pe, 0, mix[:, 0:4, :], C("ones"), rt_v.rearrange("p a b -> p (a b)")
                             .rearrange("p (a b) -> p a b", a=4))
            pe.wait_ge(hn_ms, 4)

        def scalar_retention(act, turn):
            for d, table in ((0, rt_decay), (1, rt_back)):
                for hd in range(4):
                    act.activation(table[:, 2 * (hd % 2) + hd // 2, :], C(("ahead", "behind")[d]), ACT.Exp,
                                   scale=prm("lg_head", 4 * d + hd))
                for b in range(2):
                    act.activation(rt_qdec[:, 2 * d + b, :], C(("from1", "to1")[d]), ACT.Exp,
                                   scale=prm("lg_part", 2 * d + b))
                act.activation(rt_kdec[:, 4 * d:4 * d + 4], prm("lg_head", 4 * d, 4), ACT.Exp,
                               scale=C(("left_f", "left_b")[d]))
            act.activation(rt_cdec[:, :], prm("lg_part", 0, 4), ACT.Exp, scale=float(P)).then_inc(rt_tab, 1)
            for c in range(NCH):
                act.wait_ge(rt_vt, c + 1)
                act.activation(rt_v[:, c, :], bank(4 + c % 2), ACT.Copy).then_inc(rt_v_ready, 1)
            act.activation(rt_p[:, 8:12, :], rt_p[:, 8:12, :], ACT.Silu).then_inc(rt_silu, 1)
            for c in range(NCH):
                act.wait_ge(rt_o, c + 1)
                for q in range(2):
                    ins = act.activation(mix[:, q:4:2, chunk(c)], grid(bank(4 * (c % 2) + 2 + q, 0, 256), 2, P), ACT.Copy)
                ins.then_inc(rt_out, 1)
            scalar_head_norm(act, 0, mix[:, 0:4, :], rt_v.rearrange("p a b -> p (a b)")
                             .rearrange("p (a b) -> p a b", a=4))

        def vector_retention(dve, turn):
            dve.wait_ge(rt_tab, 1)
            turn(dve.tensor_scalar(rt_kdec[:, :], rt_kdec[:, :], HS ** -0.5, None, ALU.mult))
            dve.tensor_tensor(rt_decay[:, :, :], rt_decay[:, :, :], each(C("mask_f")[:, P:2 * P], 4), ALU.mult)
            turn(dve.tensor_tensor(rt_back[:, :, :], rt_back[:, :, :], each(C("mask_b")[:, P:2 * P], 4), ALU.mult))
            turn(dve.tensor_tensor(rt_decay[:, :, :], rt_decay[:, :, :], rt_back[:, :, :], ALU.add))
            turn(dve.tensor_scalar(rt_decay[:, :, :], rt_decay[:, :, :], HS ** -0.5, None, ALU.mult))
            for b in range(4):
                rope(dve, turn, rt_p[:, b, SAMPLE], bank(b), rt_rope[:, b % 2, :], rt_turned, b + 1, rt_roped)
            for c in range(NCH):
                dve.wait_ge(rt_kt, c + 1)
                for d in range(2):
                    ins = dve.tensor_tensor(grid(rt_k[:, d, c, :], 4, HS), grid(bank(6 + c % 2, 0, 256), 4, HS),
                                            over(rt_kdec[:, 4 * d:4 * d + 4], HS), ALU.mult)
                ins.then_inc(rt_k_ready, 1)
            dve.wait_ge(rt_zero, 2)
            dve.wait_ge(first, 32)
            for n, (d, i) in enumerate(RT_UPD):
                dve.wait_ge(rt_upd, n + 1)
                old = rt_s[:, d, ORDER[d][i], :, :]
                new = rt_end[:, d, :, :] if i == 0 else rt_s[:, d, ORDER[d][i + 1], :, :]
                for b in range(2):
                    ins = dve.scalar_tensor_tensor(out=new[:, b, :], in0=old[:, b, :],
                                                   scalar=rt_cdec[:, 2 * d + b:2 * d + b + 1],
                                                   in1=bank(n, b * P, b * P + P), op0=ALU.mult, op1=ALU.add)
                ins.then_inc(rt_state, 1)
                dve.wait_ge(rt_state, n + 1)
            for c in range(NCH):
                dve.wait_ge(rt_score, c + 1)
                if c >= 2:
                    dve.wait_ge(rt_o, c - 1)
                two = grid(ps[:, 2048 * (c % 2):2048 * (c % 2) + 1024], 2, 512)[:, :, 0:256]
                dve.tensor_tensor(grid(rt_att[:, c % 2, :, :].rearrange("p a b -> p (a b)"), 2, 256), two,
                                  grid(rt_decay[:, :, :].rearrange("p a b -> p (a b)"), 2, 256), ALU.mult)\
                   .then_inc(rt_weighed, 1)
                for d in range(2):
                    ins = dve.tensor_tensor(rt_q[:, c % 2, 2 * d:2 * d + 2, :], rt_p[:, 0:2, chunk(c)],
                                            rt_qdec[:, 2 * d:2 * d + 2, :], ALU.mult)
                ins.then_inc(rt_qs, 1)
            tmp = rt_v.rearrange("p a b -> p (a b)").rearrange("p (a b) -> p a b", a=4)
            vector_head_norm(dve, turn, 0, mix[:, 0:4, :], tmp, P, 1e-5, "gn_w")
            dve.wait_ge(rt_silu, 1)
            turn(dve.tensor_tensor(mix[:, 0:4, :], mix[:, 0:4, :], rt_p[:, 8:12, :], ALU.mult))
            dve.sem_inc(mix_ready, 4)

        def rope(dve, turn, v, turned, tmp, go, count, done):
            dve.wait_ge(go, count)
            dve.tensor_tensor(tmp, turned, C("sin"), ALU.mult)
            turn(dve.tensor_tensor(v, v, C("cos"), ALU.mult))
            dve.tensor_tensor(v, v, tmp, ALU.add).then_inc(done, 1)
            dve.wait_ge(done, count)

        wa = Area(mx.at)
        rw_p = wa.take(RWKV_BLOCKS, NT)
        batch0 = wa.at
        rw_w = wa.take(4, P)
        rw_f = wa.take(4, P + 1)
        rw_up = wa.take(4, P + 1)
        rw_dn = wa.take(4, P + 1)
        rw_a = wa.take(4, P)
        rw_k = wa.take(4, P)
        rw_b = wa.take(4, P)
        rw_ar = wa.take(4, 2, P)
        rw_bn = wa.take(4, P)
        rw_kn = wa.take(4, P)
        rw_mb = wa.take(2, 4, 2, P)
        rw_mk = wa.take(2, 4, 2, P)
        rw_abt = wa.take(2, 4, P)
        rw_t = wa.take(2, 4, P)
        rw_tt = wa.take(2, 4, P)
        rw_q = wa.take(2, 4, P)
        rw_r = wa.take(8, HS)
        rw_u = wa.take(8, HS)
        rw_s = wa.take(2, 4, HS)
        shifted = Area(batch0).take(2, NT)
        rw_tmp = Area(batch0).take(4, NT)
        rw_kk = h[:, 0:4, :]
        rw_v = h[:, 4:8, :].rearrange("p a b -> p (a b)").rearrange("p (a b) -> p a b", a=NCH)
        rw_one_ka = rs[:, 0:4]

        rw_shift = sem("rw_shift")
        rw_tanh = sem("rw_tanh")
        rw_kraw = sem("rw_kraw")
        rw_ksq = sem("rw_ksq")
        rw_ksum = sem("rw_ksum")
        rw_kroot = sem("rw_kroot")
        rw_kk_ready = sem("rw_kk_ready")
        rw_vt = sem("rw_vt")
        rw_v_ready = sem("rw_v_ready")
        rw_lora = sem("rw_lora")
        rw_z = sem("rw_z")
        rw_th = sem("rw_th")
        rw_sum = sem("rw_sum")
        rw_exp = sem("rw_exp")
        rw_prep = sem("rw_prep")
        rw_mm = [sem(f"rw_mm{g}") for g in range(2)]
        rw_masked = [sem(f"rw_masked{g}") for g in range(2)]
        rw_tr = [sem(f"rw_tr{g}") for g in range(2)]
        rw_qm = [sem(f"rw_qm{g}") for g in range(2)]
        rw_qs = [sem(f"rw_qs{g}") for g in range(2)]
        rw_zm = [sem(f"rw_zm{g}") for g in range(2)]
        rw_tp = [sem(f"rw_tp{g}") for g in range(2)]
        rw_tt_ready = [sem(f"rw_tt_ready{g}") for g in range(2)]
        rw_natp = sem("rw_natp")
        rw_nat = sem("rw_nat")
        rw_s0 = sem("rw_s0")
        rw_rm = sem("rw_rm")
        rw_r_ready = sem("rw_r_ready")
        rw_um = sem("rw_um")
        rw_u_ready = sem("rw_u_ready")
        rw_y = sem("rw_y")
        rw_y_added = sem("rw_y_added")
        rw_sm = sem("rw_sm")
        rw_s_ready = sem("rw_s_ready")
        rw_zero = sem("rw_zero")
        rw_first = sem("rw_first")
        rw_bonus = sem("rw_bonus")
        rw_bsum = sem("rw_bsum")
        rw_badd = sem("rw_badd")
        rw_g = sem("rw_g")

        RW_BATCHES = [(d, i) for i in range(NCH) for d in range(2)]
        NB = len(RW_BATCHES)

        def where(hd):
            b, odd = hd // 2, hd % 2
            return b, HS * odd, b // 2, 2 * odd + b % 2

        def pool_rwkv(pool):
            pool.wait_ge(mix_ready, 4)
            pool.wait_ge(saved, 32)
            for d in range(2):
                pool.memset(rw_s[:, d, :, :], 0.0).then_inc(rw_zero, 1)
            for d in range(2):
                pool.wait_ge(rw_s_ready, d + 1)
                pool.dma_start(outs["rwkv"][d], rw_s[:, d, :, :]).then_inc(saved, 16)
                pool.wait_ge(saved, 16 * (d + 3))
                pool.dma_start(rw_s[:, d, :, :], st["s_rwkv"][d]).then_inc(rw_first, 16)

        def tensor_rwkv(pe):
            pe.wait_ge(proj_ready, RET_BLOCKS + RWKV_BLOCKS)
            pe.wait_ge(rw_shift, RWKV_BLOCKS)
            for b in range(4):
                pe.wait_ge(rw_ksq, b + 1)
                pr, sa, _ = pair(b)
                pe.matmul(pr, C("ones64"), rw_tmp[:, b, PROMPT], start=True, stop=True)
                pe.matmul(sa, C("ones64"), rw_tmp[:, b, SAMPLE], start=True, stop=True).then_inc(rw_ksum, 1)
            pe.wait_ge(rw_kroot, 4)
            for c in range(NCH):
                if c >= 2:
                    pe.wait_ge(rw_v_ready, c - 1)
                for b in range(4):
                    ins = pe.transpose(bank(c % 2, b * P, b * P + P), rw_p[:, 8 + b, chunk(c)], C("ident"))
                ins.then_inc(rw_vt, 1)
            pe.wait_ge(rw_v_ready, NCH)
            pe.wait_ge(rw_tanh, 1)
            for n, (d, i) in enumerate(RW_BATCHES):
                c = ORDER[d][i]
                if n:
                    pe.wait_ge(rw_u_ready, n)
                    pe.wait_ge(rw_r_ready, n)
                    pe.wait_ge(rw_y_added, n)
                    pe.wait_ge(rw_s_ready, n)
                    pe.wait_ge(rw_nat, 2 * n)
                for b in range(4):
                    pe.matmul(bank(0, b * P, b * P + P), lora[0:HS, d, b * P:(b + 1) * P],
                              rw_p[0:HS, 12, chunk(c)], start=True, stop=True)
                for b in range(4):
                    ins = pe.matmul(bank(1, b * P, b * P + P), lora[HS:P, d, b * P:(b + 1) * P],
                                    rw_p[HS:P, 12, chunk(c)], start=True, stop=True)
                ins.then_inc(rw_lora, 1)
                pe.wait_ge(rw_prep, n + 1)
                for g in range(2):
                    heads = [hd for hd in range(8) if where(hd)[2] == g]
                    for k, lhs in ((0, rw_b), (1, rw_k)):
                        for hd in heads:
                            b, lo, _, q = where(hd)
                            ins = pe.matmul(bank(4 * g + 2 * k + q // 2, 256 * (q % 2), 256 * (q % 2) + 256),
                                            lhs[lo:lo + HS, b, :], rw_ar[lo:lo + HS, b, :, :]
                                            .rearrange("p a b -> p (a b)"), start=True, stop=True)
                        ins.then_inc(rw_mm[g], 1)
                for g in range(2):
                    pe.wait_ge(rw_masked[g], 3 * n + 1)
                    for hd in [hd for hd in range(8) if where(hd)[2] == g]:
                        b, lo, _, q = where(hd)
                        ins = pe.matmul(bank(4 * g + q // 2, P * (q % 2), P * (q % 2) + P),
                                        rw_ar[lo:lo + HS, b, 0, :], rw_b[lo:lo + HS, b, :], start=True, stop=True)
                    ins.then_inc(rw_mm[g], 1)
                for lv in range(1, LEVELS):
                    for g in range(2):
                        pe.wait_ge(rw_tr[g], LEVELS * n + lv)
                        if lv == 1:
                            pe.wait_ge(rw_masked[g], 3 * n + 3)
                        for q in range(4):
                            ins = pe.matmul(bank(4 * g, q * P, q * P + P), rw_abt[:, g, q, :], rw_t[:, g, q, :],
                                            start=True, stop=True)
                        ins.then_inc(rw_qm[g], 1)
                    for g in range(2):
                        pe.wait_ge(rw_qs[g], (LEVELS - 1) * n + lv)
                        if lv > 1:
                            pe.wait_ge(rw_tt_ready[g], (LEVELS - 2) * n + lv - 1)
                        for q in range(4):
                            ins = pe.matmul(bank(4 * g + 1, q * P, q * P + P), rw_tt[:, g, q, :], rw_q[:, g, q, :],
                                            start=True, stop=True)
                        ins.then_inc(rw_zm[g], 1)
                    if lv < LEVELS - 1:
                        for g in range(2):
                            pe.wait_ge(rw_tr[g], LEVELS * n + lv + 1)
                            for q in range(4):
                                ins = pe.transpose(bank(4 * g + 2, q * P, q * P + P), rw_t[:, g, q, :], C("ident"))
                            ins.then_inc(rw_tp[g], 1)
                for g in range(2):
                    pe.wait_ge(rw_tr[g], LEVELS * (n + 1))
                for j, src in ((0, rw_b), (1, rw_k)):
                    for b in range(4):
                        ins = pe.transpose(bank(5 + j, b * P, b * P + P), src[:, b, :], C("ident"))
                    ins.then_inc(rw_natp, 1)
                pe.wait_ge(rw_s0, n + 1)
                for hd in (0, 2, 4, 6, 1, 3, 5, 7):
                    b, lo, g, q = where(hd)
                    out = bank(3 + 4 * (hd % 2), b * HS, b * HS + HS)
                    pe.matmul(out, rw_ar[lo:lo + HS, b, 0, :], rw_s[lo:lo + HS, d, b, :], start=True, stop=False)
                    ins = pe.matmul(out, rw_mk[:, g, q, 0, :], rw_v[:, c, hd * HS:hd * HS + HS],
                                    start=False, stop=True)
                ins.then_inc(rw_rm, 1)
                pe.wait_ge(rw_r_ready, n + 1)
                for hd in range(8):
                    b, lo, g, q = where(hd)
                    ins = pe.matmul(bank(0, hd * HS, hd * HS + HS), rw_t[:, g, q, :], rw_r[:, hd, :],
                                    start=True, stop=True)
                ins.then_inc(rw_um, 1)
                pe.wait_ge(rw_u_ready, n + 1)
                for hd in (0, 2, 4, 6, 1, 3, 5, 7):
                    b, lo, g, q = where(hd)
                    out = bank(1 + hd % 2, b * P, b * P + P)[lo:lo + HS]
                    pe.matmul(out, rw_s[lo:lo + HS, d, b, :], rw_ar[lo:lo + HS, b, 1, :], start=True, stop=False)
                    pe.matmul(out, rw_u[:, hd, :], rw_mb[:, g, q, 1, :], start=False, stop=False)
                    ins = pe.matmul(out, rw_v[:, c, hd * HS:hd * HS + HS], rw_mk[:, g, q, 1, :],
                                    start=False, stop=True)
                ins.then_inc(rw_y, 1)
                pe.wait_ge(rw_nat, 2 * (n + 1))
                for hd in range(8):
                    b, lo, g, q = where(hd)
                    out = bank(4, b * HS, b * HS + HS)[lo:lo + HS]
                    pe.matmul(out, rw_bn[:, b, lo:lo + HS], rw_u[:, hd, :], start=True, stop=False)
                    ins = pe.matmul(out, rw_kn[:, b, lo:lo + HS], rw_v[:, c, hd * HS:hd * HS + HS],
                                    start=False, stop=True)
                ins.then_inc(rw_sm, 1)
            pe.wait_ge(rw_y_added, NB)
            pe.wait_ge(rw_s_ready, NB)
            tensor_head_norm(pe, 1, mix[:, 4:8, :], C("ones64"), rw_tmp)
            for b in range(4):
                pe.wait_ge(rw_bonus, b + 1)
                pr, sa, _ = pair(b)
                pe.matmul(pr, C("ones64"), rw_p[:, b, PROMPT], start=True, stop=True)
                pe.matmul(sa, C("ones64"), rw_p[:, b, SAMPLE], start=True, stop=True).then_inc(rw_bsum, 1)
            for b in range(4):
                pe.wait_ge(rw_badd, b + 1)
                pr, sa, _ = pair(b)
                pe.matmul(pr, lora[:, 2, b * P:(b + 1) * P], rw_p[:, 13, PROMPT], start=True, stop=True)
                pe.matmul(sa, lora[:, 2, b * P:(b + 1) * P], rw_p[:, 13, SAMPLE], start=True, stop=True)\
                  .then_inc(rw_g, 1)

        def scalar_rwkv(act, turn):
            act.wait_ge(rw_shift, RWKV_BLOCKS)
            act.activation(rw_p[0:HS, 12, :], rw_p[0:HS, 12, :], ACT.Tanh)
            act.activation(rw_p[:, 13, :], rw_p[:, 13, :], ACT.Sigmoid).then_inc(rw_tanh, 1)
            for b in range(4):
                act.wait_ge(rw_kraw, b + 1)
                act.activation(rw_tmp[:, b, :], rw_kk[:, b, :], ACT.Square).then_inc(rw_ksq, 1)
            for b in range(4):
                act.wait_ge(rw_ksum, b + 1)
                act.activation(rw_tmp[:, b, :], pair(b)[2], ACT.Sqrt).then_inc(rw_kroot, 1)
            for c in range(NCH):
                act.wait_ge(rw_vt, c + 1)
                act.activation(rw_v[:, c, :], bank(c % 2), ACT.Copy).then_inc(rw_v_ready, 1)
            for n in range(NB):
                act.wait_ge(rw_z, 2 * n + 1)
                act.activation(rw_w[:, :, :], rw_w[:, :, :], ACT.Tanh, scale=0.5).then_inc(rw_th, 1)
                act.wait_ge(rw_z, 2 * n + 2)
                act.activation(rw_a[:, :, :], rw_a[:, :, :], ACT.Tanh, scale=0.5).then_inc(rw_th, 1)
                act.wait_ge(rw_sum, n + 1)
                act.activation(rw_dn[:, :, :], rw_up[:, :, :], ACT.Exp, scale=-1.0)
                act.activation(rw_up[:, :, :], rw_up[:, :, :], ACT.Exp).then_inc(rw_exp, 1)
                for lv in range(1, LEVELS - 1):
                    for g in range(2):
                        act.wait_ge(rw_tp[g], (LEVELS - 2) * n + lv)
                        act.activation(rw_tt[:, g, :, :].rearrange("p a b -> p (a b)"), bank(4 * g + 2), ACT.Copy)\
                           .then_inc(rw_tt_ready[g], 1)
                for j, dst in ((0, rw_bn), (1, rw_kn)):
                    act.wait_ge(rw_natp, 2 * n + j + 1)
                    act.activation(dst[:, :, :].rearrange("p a b -> p (a b)"), bank(5 + j), ACT.Copy)\
                       .then_inc(rw_nat, 1)
                act.wait_ge(rw_rm, n + 1)
                for odd in range(2):
                    ins = act.activation(rw_r[:, odd:8:2, :], grid(bank(3 + 4 * odd, 0, 256), 4, HS), ACT.Copy)
                ins.then_inc(rw_r_ready, 1)
                act.wait_ge(rw_um, n + 1)
                act.activation(rw_u[:, :, :].rearrange("p a b -> p (a b)"), bank(0), ACT.Copy).then_inc(rw_u_ready, 1)
            scalar_head_norm(act, 1, mix[:, 4:8, :], rw_tmp)

        def vector_rwkv(dve, turn):
            turn(dve.tensor_scalar(rw_one_ka, prm("k_a", 0, 4), -1.0, 1.0, ALU.mult, ALU.add))
            turn(dve.memset(rw_f[:, :, 0:1], 0.0))
            for b in range(RWKV_BLOCKS):
                dve.wait_ge(proj_ready, RET_BLOCKS + b + 1)
                s, v = shifted[:, b % 2, :], rw_p[:, b, :]
                for lo, hi in ((0, SEQ), (SEQ, NT)):
                    dve.tensor_tensor(s[:, lo + 1:hi - 1], v[:, lo:hi - 2], v[:, lo + 2:hi], ALU.add)
                    dve.tensor_copy(s[:, lo:lo + 1], v[:, lo + 1:lo + 2])
                    last = dve.tensor_copy(s[:, hi - 1:hi], v[:, hi - 2:hi - 1])
                turn(last)
                turn(dve.scalar_tensor_tensor(out=s, in0=s, scalar=0.5, in1=v, op0=ALU.mult, op1=ALU.subtract))
                dve.scalar_tensor_tensor(out=v, in0=s, scalar=prm("mu", b), in1=v, op0=ALU.mult, op1=ALU.add)\
                   .then_inc(rw_shift, 1)
            dve.wait_ge(rw_shift, RWKV_BLOCKS)
            for b in range(4):
                dve.tensor_scalar(rw_kk[:, b, :], rw_p[:, 4 + b, :], prm("k_k", b), None, ALU.mult)\
                   .then_inc(rw_kraw, 1)
            for b in range(4):
                dve.wait_ge(rw_kroot, b + 1)
                turn(dve.tensor_scalar(rw_tmp[:, b, :], rw_tmp[:, b, :], 1e-12, None, ALU.max))
                turn(dve.reciprocal(rw_tmp[:, b, :], rw_tmp[:, b, :]))
                dve.tensor_tensor(rw_kk[:, b, :], rw_kk[:, b, :], rw_tmp[:, b, :], ALU.mult).then_inc(rw_kk_ready, 1)
            dve.wait_ge(rw_kk_ready, 4)
            turn(dve.memset(rw_f[:, :, 0:1], 0.0))
            dve.wait_ge(rw_zero, 2)
            for n, (d, i) in enumerate(RW_BATCHES):
                c = ORDER[d][i]
                grow, shrink = (rw_dn, rw_up) if d == 0 else (rw_up, rw_dn)
                with_own = slice(1, P + 1) if d == 0 else slice(0, P)
                before = slice(0, P) if d == 0 else slice(1, P + 1)
                start, end = (0, P) if d == 0 else (P, 0)
                dve.wait_ge(rw_lora, n + 1)
                dve.tensor_tensor(rw_w[:, :, :], grid(bank(0), 4, P), over(prm("w0", 4 * d, 4), P), ALU.add)\
                   .then_inc(rw_z, 1)
                dve.tensor_tensor(rw_a[:, :, :], grid(bank(1), 4, P), over(prm("a0", 4 * d, 4), P), ALU.add)\
                   .then_inc(rw_z, 1)
                dve.wait_ge(rw_th, 2 * n + 1)
                turn(dve.tensor_scalar(rw_w[:, :, :], rw_w[:, :, :], -DECAY_MAX / 2, -DECAY_MAX / 2,
                                       ALU.mult, ALU.add))
                for b in range(4):
                    last = dve.tensor_tensor_scan(rw_f[:, b, 1:P + 1], C("ones"), rw_w[:, b, :], 0.0,
                                                  ALU.mult, ALU.add)
                turn(last)
                dve.tensor_tensor(rw_up[:, :, :], rw_f[:, :, :],
                                  rw_f[:, :, P // 2:P // 2 + 1].to_broadcast([P, 4, P + 1]), ALU.subtract)\
                   .then_inc(rw_sum, 1)
                dve.wait_ge(rw_th, 2 * n + 2)
                turn(dve.tensor_scalar(rw_a[:, :, :], rw_a[:, :, :], 0.5, 0.5, ALU.mult, ALU.add))
                dve.tensor_tensor(rw_b[:, :, :], rw_kk[:, :, chunk(c)], rw_a[:, :, :], ALU.mult)
                turn(dve.tensor_tensor(rw_k[:, :, :], rw_a[:, :, :], over(prm("k_a", 0, 4), P), ALU.mult))
                turn(dve.tensor_tensor(rw_k[:, :, :], rw_k[:, :, :], over(rw_one_ka, P), ALU.add))
                turn(dve.tensor_tensor(rw_k[:, :, :], rw_k[:, :, :], rw_p[:, 4:8, chunk(c)], ALU.mult))
                dve.wait_ge(rw_exp, n + 1)
                dve.tensor_tensor(rw_k[:, :, :], rw_k[:, :, :], grow[:, :, with_own], ALU.mult)
                dve.tensor_tensor(rw_b[:, :, :], rw_b[:, :, :], grow[:, :, with_own], ALU.mult)
                dve.scalar_tensor_tensor(out=rw_ar[:, :, 0, :], in0=rw_kk[:, :, chunk(c)], scalar=-1.0,
                                         in1=shrink[:, :, before], op0=ALU.mult, op1=ALU.mult)
                dve.tensor_tensor(rw_ar[:, :, 1, :], rw_p[:, 0:4, chunk(c)], shrink[:, :, with_own], ALU.mult)\
                   .then_inc(rw_prep, 1)
                mask, other = (C("mask_f"), C("mask_b")) if d == 0 else (C("mask_b"), C("mask_f"))
                merge, merge_t = (C("merge_f"), C("merge_b")) if d == 0 else (C("merge_b"), C("merge_f"))
                for k, dst in ((0, rw_mb), (1, rw_mk)):
                    for g in range(2):
                        dve.wait_ge(rw_mm[g], 3 * n + k + 1)
                        at = 2048 * g + 1024 * k
                        dve.tensor_tensor(dst[:, g, :, :, :].rearrange("p a b c -> p a (b c)"),
                                          grid(ps[:, at:at + 1024], 4, 256), each(mask, 4), ALU.mult)\
                           .then_inc(rw_masked[g], 1)
                for g in range(2):
                    dve.wait_ge(rw_mm[g], 3 * n + 3)
                    dve.tensor_tensor(rw_abt[:, g, :, :].rearrange("p (a b) c -> p a b c", a=2),
                                      grid(ps[:, 2048 * g:2048 * g + 1024], 2, 4, P)[:, :, 0:2, :],
                                      each(other[:, 0:P], 4).rearrange("p (a b) c -> p a b c", a=2), ALU.mult)\
                       .then_inc(rw_masked[g], 1)
                for g in range(2):
                    dve.wait_ge(rw_masked[g], 3 * n + 3)
                    dve.tensor_tensor(rw_t[:, g, :, :], rw_mb[:, g, :, 0, :], each(merge[:, 0:P], 4), ALU.mult)
                    turn(dve.tensor_tensor(rw_tt[:, g, :, :], rw_abt[:, g, :, :], each(merge_t[:, 0:P], 4), ALU.mult))
                    dve.tensor_tensor(rw_t[:, g, :, :], rw_t[:, g, :, :], each(C("ident"), 4), ALU.add)
                    dve.tensor_tensor(rw_tt[:, g, :, :], rw_tt[:, g, :, :], each(C("ident"), 4), ALU.add)\
                       .then_inc(rw_tr[g], 1)
                for lv in range(1, LEVELS):
                    for g in range(2):
                        dve.wait_ge(rw_qm[g], (LEVELS - 1) * n + lv)
                        dve.tensor_tensor(rw_q[:, g, :, :], grid(bank(4 * g), 4, P),
                                          each(merge[:, lv * P:(lv + 1) * P], 4), ALU.mult).then_inc(rw_qs[g], 1)
                    for g in range(2):
                        dve.wait_ge(rw_zm[g], (LEVELS - 1) * n + lv)
                        dve.wait_ge(rw_tr[g], LEVELS * n + lv)
                        dve.tensor_tensor(rw_t[:, g, :, :], rw_t[:, g, :, :], grid(bank(4 * g + 1), 4, P), ALU.add)\
                           .then_inc(rw_tr[g], 1)
                if n >= 2:
                    dve.wait_ge(rw_s_ready, n - 1)
                if i == 1:
                    dve.wait_ge(rw_first, 16 * (d + 1))
                S = rw_s[:, d, :, :]
                dve.tensor_tensor(S, S, grow[:, :, start:start + 1].to_broadcast([P, 4, HS]), ALU.mult)\
                   .then_inc(rw_s0, 1)
                dve.wait_ge(rw_y, n + 1)
                for odd in range(2):
                    lo = HS * odd
                    dst = mix[lo:lo + HS, 4:8, chunk(c)]
                    src = grid(bank(1 + odd), 4, P)[lo:lo + HS]
                    seen = [ORDER[e][j] for e, j in RW_BATCHES[:n]]
                    if c in seen:
                        last = dve.tensor_tensor(dst, dst, src, ALU.add)
                    else:
                        last = dve.tensor_copy(dst, src)
                last.then_inc(rw_y_added, 1)
                dve.wait_ge(rw_y_added, n + 1)
                dve.wait_ge(rw_sm, n + 1)
                turn(dve.tensor_tensor(S, S, grid(bank(4, 0, 256), 4, HS), ALU.add))
                dve.tensor_tensor(S, S, shrink[:, :, end:end + 1].to_broadcast([P, 4, HS]), ALU.mult)\
                   .then_inc(rw_s_ready, 1)
            vector_head_norm(dve, turn, 1, mix[:, 4:8, :], rw_tmp, HS, 64e-5, "ln_w")
            for b in range(4):
                dve.scalar_tensor_tensor(out=rw_p[:, b, :], in0=rw_p[:, b, :], scalar=prm("r_k", b),
                                         in1=rw_p[:, 4 + b, :], op0=ALU.mult, op1=ALU.mult).then_inc(rw_bonus, 1)
            for b in range(4):
                dve.wait_ge(rw_bsum, b + 1)
                turn(dve.tensor_tensor(rw_p[:, 8 + b, :], rw_p[:, 8 + b, :], pair(b)[2], ALU.mult))
                dve.scalar_tensor_tensor(out=mix[:, 4 + b, :], in0=mix[:, 4 + b, :], scalar=prm("ln_b", b),
                                         in1=rw_p[:, 8 + b, :], op0=ALU.add, op1=ALU.add).then_inc(rw_badd, 1)
            for b in range(4):
                dve.wait_ge(rw_g, b + 1)
                last = dve.tensor_tensor(mix[:, 4 + b, :], mix[:, 4 + b, :], pair(b)[2], ALU.mult)
            turn(last)
            dve.sem_inc(mix_ready, 4)

        la = Area(mx.at)
        ml_p = la.take(MLSTM_BLOCKS, NT)
        ml_v = la.take(NCH, 4, P + 1)
        ml_kn = la.take(NCH, 4, P)
        ml_b = la.take(NT)
        ml_top = la.take(NT)
        ml_share = la.take(NT)
        ml_floor = la.take(NT)
        ml_left = la.take(NT)
        ml_m = la.take(NCH)
        ml_last = la.take(NCH)
        ml_dec = la.take(NCH)
        ml_mend = la.take(1)
        ml_g = la.take(2, NCH, HS)
        ml_w = la.take(4, P)
        ml_sw = la.take(4, P)
        ml_q = la.take(4, P)
        ml_wk = la.take(4, P)
        ml_c = la.take(2, 4, P + 1)
        ml_decb = la.take(4)
        ml_bd = rs[:, 0:4 * P].rearrange("p (a b) -> p a b", a=4)
        R = HS

        ml_fg = sem("ml_fg")
        ml_soft = sem("ml_soft")
        ml_rows = sem("ml_rows")
        ml_exps = sem("ml_exps")
        ml_kscaled = sem("ml_kscaled")
        ml_vt = sem("ml_vt")
        ml_kt = sem("ml_kt")
        ml_nat = sem("ml_nat")
        ml_gt = sem("ml_gt")
        ml_g_ready = sem("ml_g_ready")
        ml_mm = sem("ml_mm")
        ml_arg = sem("ml_arg")
        ml_w_ready = sem("ml_w_ready")
        ml_bd_ready = sem("ml_bd_ready")
        ml_fed = sem("ml_fed")
        ml_nd = sem("ml_nd")
        ml_abs = sem("ml_abs")
        ml_done = sem("ml_done")
        ml_zero = sem("ml_zero")
        ml_first = sem("ml_first")
        ml_sig = sem("ml_sig")

        def run(d, c):
            lo, hi = c * P, (c + 1) * P
            return slice(lo, hi) if d == 0 else slice(hi - 1, lo - 1 if lo else None, -1)

        def pool_mlstm(pool):
            pool.wait_ge(x_ready, DB * 4)
            for d in range(2):
                pool.memset(ml_c[:, d, :, :], 0.0).then_inc(ml_zero, 1)
            pool.memset(ml_v[:, :, :, P:P + 1], 1.0).then_inc(ml_zero, 1)
            for d in range(2):
                pool.wait_ge(ml_done, d + 1)
                pool.dma_start(outs["mc"][d], ml_c[:, d, :, :]).then_inc(saved, 16)
                pool.wait_ge(saved, 16 * (5 + d))
                pool.dma_start(ml_c[:, d, :, :], st["s_mc"][d]).then_inc(ml_first, 16)
            for d in range(2):
                pool.dma_start(outs["m"][d], ml_mend[32 * d:32 * d + 4, :]).then_inc(saved, 16)

        def tensor_mlstm(pe):
            pe.wait_ge(proj_ready, RET_BLOCKS + RWKV_BLOCKS + MLSTM_BLOCKS)
            pe.wait_ge(ml_kscaled, 1)
            for c in range(NCH):
                if c >= 2:
                    pe.wait_ge(ml_nat, 2 * (c - 1))
                for j, go in ((8, ml_vt), (4, ml_kt)):
                    for b in range(4):
                        ins = pe.transpose(bank((j == 4) * 2 + c % 2, b * P, b * P + P), ml_p[:, j + b, chunk(c)],
                                           C("ident"))
                    ins.then_inc(go, 1)
            pe.wait_ge(ml_exps, 1)
            for j, row in ((0, ml_p[:, 12, :]), (1, ml_left)):
                for c in range(NCH):
                    ins = pe.transpose(bank(4 + j, c * HS, c * HS + HS), row[0:R, chunk(c)], C("ident", R)[:, 0:R])
            ins.then_inc(ml_gt, 1)
            pe.wait_ge(ml_nat, 2 * NCH)
            pe.wait_ge(ml_g_ready, 1)
            for n, (d, i) in enumerate(RW_BATCHES):
                c = ORDER[d][i]
                if n:
                    pe.wait_ge(ml_done, n)
                for hd in range(4):
                    pe.matmul(bank(0, hd * P, hd * P + P), ml_p[:, 4 + hd, chunk(c)], ml_p[:, hd, chunk(c)],
                              start=True, stop=True)
                for hd in range(4):
                    r = 32 * d + hd
                    unit = C("ident", R)[:, r:r + 1].to_broadcast([R, P])
                    for b, row in ((1, ml_top), (2, ml_share), (3, ml_floor)):
                        pe.matmul(bank(b, hd * P, hd * P + P), unit, row[0:R, chunk(c)], start=True, stop=True)
                    ins = pe.matmul(bank(7, hd, hd + 1), unit, ml_dec[0:R, c:c + 1], start=True, stop=True)
                ins.then_inc(ml_mm, 1)
                pe.wait_ge(ml_fed, n + 1)
                for hd in range(4):
                    pe.matmul(bank(4, hd * P, hd * P + P), ml_v[:, c, hd, 0:P], ml_sw[:, hd, :],
                              start=True, stop=False)
                    pe.matmul(bank(4, hd * P, hd * P + P), ml_c[:, d, hd, 0:P], ml_q[:, hd, :],
                              start=False, stop=True)
                for hd in range(4):
                    pe.matmul(bank(5, hd * P, hd * P + P), C("ones"), ml_sw[:, hd, :], start=True, stop=False)
                    pe.matmul(bank(5, hd * P, hd * P + P), ml_c[:, d, hd, P:P + 1].to_broadcast([P, P]),
                              ml_q[:, hd, :], start=False, stop=True)
                for hd in range(4):
                    at = (P + 1) * (hd % 2)
                    ins = pe.matmul(bank(6 + hd // 2, at, at + P + 1), ml_wk[:, hd, :], ml_v[:, c, hd, :],
                                    start=True, stop=True)
                ins.then_inc(ml_nd, 1)
            pe.wait_ge(ml_done, NB)
            tensor_head_norm(pe, 2, mix[:, 0:4, :], C("ones"), ml_kn.rearrange("p a b c -> p (a b c)")
                             .rearrange("p (a b) -> p a b", a=4))
            pe.wait_ge(hn_ms, 12)

        def scalar_mlstm(act, turn):
            act.activation(ml_p[:, 4:8, :], ml_p[:, 4:8, :], ACT.Copy, scale=float(P) ** -0.5).then_inc(ml_kscaled, 1)
            act.wait_ge(ml_fg, 1)
            t = ml_left[0:R, :]
            turn(act.activation(t, ml_p[0:R, 13, :], ACT.Abs))
            turn(act.activation(t, t, ACT.Exp, scale=-1.0))
            act.activation(t, t, ACT.Ln, bias=1.0).then_inc(ml_soft, 1)
            for c in range(NCH):
                for j, (go, src) in enumerate(((ml_vt, ml_v[:, c, :, 0:P]), (ml_kt, ml_kn[:, c, :, :]))):
                    act.wait_ge(go, c + 1)
                    act.activation(src, grid(bank(2 * j + c % 2), 4, P), ACT.Copy).then_inc(ml_nat, 1)
            act.wait_ge(ml_rows, 1)
            for c in range(NCH):
                act.activation(ml_share[0:R, chunk(c)], ml_top[0:R, chunk(c)], ACT.Exp, scale=-1.0,
                               bias=ml_m[0:R, c:c + 1])
            act.activation(ml_floor[0:R, :], ml_floor[0:R, :], ACT.Exp, scale=-1.0)
            act.activation(ml_dec[0:R, :], ml_dec[0:R, :], ACT.Exp)
            act.activation(ml_left[0:R, :], ml_left[0:R, :], ACT.Exp).then_inc(ml_exps, 1)
            act.wait_ge(ml_gt, 1)
            for j in range(2):
                ins = act.activation(ml_g[:, j, :, :].rearrange("p a b -> p (a b)"), bank(4 + j, 0, NCH * HS), ACT.Copy)
            ins.then_inc(ml_g_ready, 1)
            for n in range(NB):
                act.wait_ge(ml_mm, n + 1)
                act.activation(ml_bd, grid(bank(3), 4, P), ACT.Copy).then_inc(ml_bd_ready, 1)
                act.wait_ge(ml_arg, n + 1)
                act.activation(ml_w[:, :, :], ml_w[:, :, :], ACT.Exp).then_inc(ml_w_ready, 1)
                act.wait_ge(ml_nd, n + 1)
                act.activation(ml_w[:, :, :], grid(bank(5), 4, P), ACT.Abs).then_inc(ml_abs, 1)
            act.activation(ml_p[:, 14:18, :], ml_p[:, 14:18, :], ACT.Sigmoid).then_inc(ml_sig, 1)
            scalar_head_norm(act, 2, mix[:, 0:4, :], ml_kn.rearrange("p a b c -> p (a b c)")
                             .rearrange("p (a b) -> p a b", a=4))

        def vector_mlstm(dve, turn):
            dve.wait_ge(proj_ready, RET_BLOCKS + RWKV_BLOCKS + MLSTM_BLOCKS)
            ig, fg = ml_p[0:R, 12, :], ml_p[0:R, 13, :]
            dve.tensor_scalar(fg, fg, prm("f_bias", rows=R), None, ALU.add).then_inc(ml_fg, 1)
            dve.tensor_scalar(ig, ig, prm("i_bias", rows=R), None, ALU.add)
            dve.memset(ml_b[0:R, :], 0.0)
            dve.memset(ml_top[0:R, :], 0.0)
            dve.memset(ml_last[0:R, :], 0.0)
            turn(dve.memset(ml_m[0:R, :], 0.0))
            for d in range(2):
                rows = slice(32 * d, 32 * d + 4)
                c = ORDER[d][1]
                dve.tensor_copy(ml_m[rows, c:c + 1], par[rows, pat["m_init"][0]:pat["m_init"][1]])
            dve.wait_ge(ml_soft, 1)
            turn(dve.scalar_tensor_tensor(out=fg, in0=fg, scalar=0.0, in1=ml_left[0:R, :], op0=ALU.min,
                                          op1=ALU.subtract))
            for d in range(2):
                rows = slice(32 * d, 32 * d + 4)
                for c in range(NCH):
                    last = dve.tensor_tensor_scan(ml_b[rows, run(d, c)], C("ones")[rows, :],
                                                  ml_p[rows, 13, run(d, c)], 0.0, ALU.mult, ALU.add)
            turn(last)
            turn(dve.tensor_tensor(ig, ig, ml_b[0:R, :], ALU.subtract))
            for i in range(NCH):
                for d in range(2):
                    rows, c = slice(32 * d, 32 * d + 4), ORDER[d][i]
                    g = ml_p[rows, 12, run(d, c)]
                    last = dve.tensor_tensor_scan(ml_top[rows, run(d, c)], g, g, ml_m[rows, c:c + 1],
                                                  ALU.max, ALU.max)
                turn(last)
                for d in range(2):
                    rows, c = slice(32 * d, 32 * d + 4), ORDER[d][i]
                    e = c * P + (P - 1 if d == 0 else 0)
                    last = dve.tensor_copy(ml_last[rows, c:c + 1], ml_top[rows, e:e + 1])
                    if i + 1 < NCH:
                        m = ml_mend[rows, :] if i == 0 else ml_m[rows, ORDER[d][i + 1]:ORDER[d][i + 1] + 1]
                        last = dve.tensor_tensor(m, ml_top[rows, e:e + 1], ml_b[rows, e:e + 1], ALU.add)
                turn(last)
            dve.tensor_tensor(ml_floor[0:R, :], ml_b[0:R, :], ml_top[0:R, :], ALU.add)
            dve.tensor_tensor(ml_dec[0:R, :], ml_m[0:R, :], ml_last[0:R, :], ALU.subtract)
            dve.tensor_tensor(grid(ml_left[0:R, :], NCH, P), grid(ig, NCH, P), over(ml_last[0:R, :], P),
                              ALU.subtract).then_inc(ml_rows, 1)
            dve.wait_ge(ml_g_ready, 1)
            dve.wait_ge(ml_zero, 3)
            for n, (d, i) in enumerate(RW_BATCHES):
                c = ORDER[d][i]
                col = slice(32 * d, 32 * d + 4)
                dve.wait_ge(ml_mm, n + 1)
                turn(dve.scalar_tensor_tensor(out=ml_w[:, :, :], in0=grid(bank(1), 4, P), scalar=-1.0,
                                              in1=over(ml_g[:, 0, c, col], P), op0=ALU.mult, op1=ALU.add))
                dve.scalar_tensor_tensor(out=ml_w[:, :, :], in0=ml_w[:, :, :], scalar=0.0,
                                         in1=each(C(("neg_f", "neg_b")[d]), 4), op0=ALU.min, op1=ALU.add)\
                   .then_inc(ml_arg, 1)
                dve.tensor_tensor(ml_q[:, :, :], ml_p[:, 0:4, chunk(c)], grid(bank(2), 4, P), ALU.mult)
                dve.tensor_tensor(ml_wk[:, :, :], ml_kn[:, c, :, :], over(ml_g[:, 1, c, col], P), ALU.mult)
                dve.tensor_copy(ml_decb[:, :], bank(7, 0, 4))
                if i == 1:
                    dve.wait_ge(ml_first, 16 * (d + 1))
                dve.wait_ge(ml_w_ready, n + 1)
                dve.tensor_tensor(ml_sw[:, :, :], ml_w[:, :, :], grid(bank(0), 4, P), ALU.mult).then_inc(ml_fed, 1)
                dve.wait_ge(ml_fed, n + 1)
                dve.wait_ge(ml_nd, n + 1)
                dve.wait_ge(ml_bd_ready, n + 1)
                dve.wait_ge(ml_abs, n + 1)
                turn(dve.tensor_tensor(ml_w[:, :, :], ml_w[:, :, :], ml_bd, ALU.max))
                turn(dve.reciprocal(ml_w[:, :, :], ml_w[:, :, :]))
                dst = mix[:, 0:4, chunk(c)]
                if c in [ORDER[e][j] for e, j in RW_BATCHES[:n]]:
                    turn(dve.tensor_tensor(ml_w[:, :, :], ml_w[:, :, :], grid(bank(4), 4, P), ALU.mult))
                    dve.tensor_tensor(dst, dst, ml_w[:, :, :], ALU.add)
                else:
                    dve.tensor_tensor(dst, ml_w[:, :, :], grid(bank(4), 4, P), ALU.mult)
                s = ml_c[:, d, :, :]
                turn(dve.tensor_tensor(s, s, over(ml_decb[:, :], P + 1), ALU.mult))
                s = s.rearrange("p (a b) c -> p a (b c)", a=2)
                dve.tensor_tensor(s, s, grid(ps[:, 3072:4096], 2, 512)[:, :, 0:2 * (P + 1)], ALU.add)\
                   .then_inc(ml_done, 1)
                dve.wait_ge(ml_done, n + 1)
            tmp = ml_kn.rearrange("p a b c -> p (a b c)").rearrange("p (a b) -> p a b", a=4)
            vector_head_norm(dve, turn, 2, mix[:, 0:4, :], tmp, P, 1e-5, "mn_w")
            dve.wait_ge(ml_sig, 1)
            turn(dve.tensor_tensor(mix[:, 0:4, :], mix[:, 0:4, :], ml_p[:, 14:18, :], ALU.mult))
            dve.sem_inc(mix_ready, 4)

        aa = Area(mx.at)
        at_p = aa.take(ATT_BLOCKS, NT)
        at_ck = aa.take(2, PAST)
        at_cv = aa.take(2 * HS)
        at_v = aa.take(NCH, 2 * HS)
        at_tmp = aa.take(6, NT)
        at_rope = aa.take(2, DEC_SEQ)
        at_e = aa.take(2, NT)
        at_t = aa.take(2, NT)
        at_stat = aa.take(2, 4)

        at_sq = sem("at_sq")
        at_ss = sem("at_ss")
        at_ms = sem("at_ms")
        at_root = sem("at_root")
        at_normed = sem("at_normed")
        at_turned = sem("at_turned")
        at_roped = sem("at_roped")
        at_vt = sem("at_vt")
        at_v_ready = sem("at_v_ready")
        at_cached = sem("at_cached")
        at_score = sem("at_score")
        at_max = sem("at_max")
        at_exp = sem("at_exp")
        at_prob = sem("at_prob")
        at_pt = sem("at_pt")
        at_pt_ready = sem("at_pt_ready")
        at_o = sem("at_o")
        at_out = sem("at_out")
        AT_UNITS = [(c, hd) for c in range(NCH) for hd in range(8)]
        NU = len(AT_UNITS)

        def keys_of(c):
            return 1 if c == 0 else NCH

        def pool_attention(pool):
            pool.wait_ge(mix_ready, 12)
            pool.wait_ge(saved, 16 * 8)
            pool.dma_start(at_ck[:, :, :], st["s_ck"]).then_inc(at_cached, 16)
            pool.dma_start(grid(at_cv, 2, HS), st["s_cv"]).then_inc(at_cached, 16)
            pool.wait_ge(at_normed, 6)
            for g in range(2):
                pool.dma_start(outs["ck"][g], at_p[0:HS, 4 + g, PROMPT]).then_inc(saved, 16)
            pool.wait_ge(at_v_ready, 1)
            pool.dma_start(outs["cv"], at_v[:, 0, :]).then_inc(saved, 16)

        def tensor_attention(pe):
            pe.wait_ge(proj_ready, RET_BLOCKS + RWKV_BLOCKS + MLSTM_BLOCKS + ATT_BLOCKS)
            for b in range(6):
                pe.wait_ge(at_sq, b + 1)
                if b >= 3:
                    pe.wait_ge(at_ms, b - 2)
                pr, sa, _ = pair(b % 3)
                pe.matmul(pr, C("ones64"), at_tmp[:, b, PROMPT], start=True, stop=True)
                pe.matmul(sa, C("ones64"), at_tmp[:, b, SAMPLE], start=True, stop=True).then_inc(at_ss, 1)
            for c in range(NCH):
                ins = pe.transpose(bank(6 + c // 4, c % 4 * P, c % 4 * P + P), at_p[:, 6, chunk(c)], C("ident"))
            ins.then_inc(at_vt, 1)
            pe.wait_ge(at_ms, 6)
            for b in range(6):
                pe.wait_ge(at_normed, b + 1)
                pe.matmul(bank(b), C("turn"), at_p[:, b, SAMPLE], start=True, stop=True).then_inc(at_turned, 1)
            pe.wait_ge(at_roped, 6)
            pe.wait_ge(at_v_ready, 1)
            pe.wait_ge(at_cached, 32)

            def scores(n):
                c, hd = AT_UNITS[n]
                lo, g = HS * (hd % 2), hd // 4
                pr, sa, _ = pair(n % 2)
                q = at_p[lo:lo + HS, hd // 2, chunk(c)]
                if n >= 2:
                    pe.wait_ge(at_exp, n - 1)
                if c == 0:
                    pe.matmul(pr, q, at_p[lo:lo + HS, 4 + g, PROMPT], start=True, stop=True).then_inc(at_score, 1)
                else:
                    pe.matmul(pr, q, at_ck[lo:lo + HS, g, :], start=True, stop=True)
                    pe.matmul(sa, q, at_p[lo:lo + HS, 4 + g, SAMPLE], start=True, stop=True).then_inc(at_score, 1)

            def turned(n):
                c, hd = AT_UNITS[n]
                pe.wait_ge(at_prob, n + 1)
                if n >= 1:
                    pe.wait_ge(at_pt_ready, n)
                for j in range(keys_of(c)):
                    ins = pe.transpose(pair(2)[2][:, j * P:(j + 1) * P], at_e[:, n % 2, j * P:(j + 1) * P], C("ident"))
                ins.then_inc(at_pt, 1)

            def values(n):
                c, hd = AT_UNITS[n]
                lo, g = HS * (hd % 2), hd // 4
                pe.wait_ge(at_pt_ready, n + 1)
                if n >= 2:
                    pe.wait_ge(at_out, n - 1)
                nk = keys_of(c)
                for j in range(nk):
                    v = at_cv[:, g * HS:(g + 1) * HS] if c and j == 0 else at_v[:, j, g * HS:(g + 1) * HS]
                    ins = pe.matmul(bank(6 + n % 2, 0, P)[lo:lo + HS], v, at_t[:, n % 2, j * P:(j + 1) * P],
                                    start=(j == 0), stop=(j == nk - 1))
                ins.then_inc(at_o, 1)

            for n in range(NU + 2):
                if n < NU:
                    scores(n)
                if 1 <= n <= NU:
                    turned(n - 1)
                if n >= 2:
                    values(n - 2)

        def scalar_attention(act, turn):
            for b in range(6):
                act.activation(at_tmp[:, b, :], at_p[:, b, :], ACT.Square).then_inc(at_sq, 1)
            act.wait_ge(at_vt, 1)
            act.activation(at_v[:, 0:4, :].rearrange("p a b -> p (a b)"), bank(6), ACT.Copy)
            act.activation(at_v[:, 4, :], bank(7, 0, P), ACT.Copy).then_inc(at_v_ready, 1)
            for b in range(6):
                act.wait_ge(at_ms, b + 1)
                act.activation(at_tmp[:, b, :], at_tmp[:, b, :], ACT.Sqrt).then_inc(at_root, 1)
            for n in range(NU + 2):
                if n < NU:
                    c, hd = AT_UNITS[n]
                    w = keys_of(c) * P
                    act.wait_ge(at_max, n + 1)
                    if n >= 2:
                        act.wait_ge(at_pt, n - 1)
                    act.activation(at_e[:, n % 2, 0:w], pair(n % 2)[2][:, 0:w], ACT.Exp, scale=HS ** -0.5,
                                   bias=at_stat[:, n % 2, 1:2], accum_out=at_stat[:, n % 2, 2:3]).then_inc(at_exp, 1)
                if 1 <= n <= NU:
                    c, hd = AT_UNITS[n - 1]
                    w = keys_of(c) * P
                    act.wait_ge(at_pt, n)
                    if n >= 3:
                        act.wait_ge(at_o, n - 2)
                    act.activation(at_t[:, (n - 1) % 2, 0:w], pair(2)[2][:, 0:w], ACT.Copy).then_inc(at_pt_ready, 1)
                if n >= 2:
                    c, hd = AT_UNITS[n - 2]
                    lo = HS * (hd % 2)
                    act.wait_ge(at_o, n - 1)
                    act.activation(mix[lo:lo + HS, 4 + hd // 2, chunk(c)], bank(6 + n % 2, 0, P)[lo:lo + HS],
                                   ACT.Copy).then_inc(at_out, 1)

        def vector_attention(dve, turn):
            for b in range(6):
                dve.wait_ge(at_ss, b + 1)
                dve.tensor_scalar(at_tmp[:, b, :], pair(b % 3)[2], 1.0 / HS, EPS, ALU.mult, ALU.add)\
                   .then_inc(at_ms, 1)
            for b in range(6):
                dve.wait_ge(at_root, b + 1)
                turn(dve.reciprocal(at_tmp[:, b, :], at_tmp[:, b, :]))
                dve.scalar_tensor_tensor(out=at_p[:, b, :], in0=at_p[:, b, :],
                                         scalar=prm("q_gain" if b < 4 else "k_gain"), in1=at_tmp[:, b, :],
                                         op0=ALU.mult, op1=ALU.mult).then_inc(at_normed, 1)
            dve.wait_ge(at_normed, 6)
            for b in range(6):
                rope(dve, turn, at_p[:, b, SAMPLE], bank(b), at_rope[:, b % 2, :], at_turned, b + 1, at_roped)
            for n in range(NU + 1):
                if n < NU:
                    c, hd = AT_UNITS[n]
                    dve.wait_ge(at_score, n + 1)
                    turn(dve.tensor_reduce(at_stat[:, n % 2, 0:1], pair(n % 2)[2][:, 0:keys_of(c) * P], AX.X, ALU.max))
                    dve.tensor_scalar(at_stat[:, n % 2, 1:2], at_stat[:, n % 2, 0:1], -HS ** -0.5, None, ALU.mult)\
                       .then_inc(at_max, 1)
                if n >= 1:
                    m = n - 1
                    c, hd = AT_UNITS[m]
                    w = keys_of(c) * P
                    dve.wait_ge(at_exp, m + 1)
                    turn(dve.reciprocal(at_stat[:, m % 2, 3:4], at_stat[:, m % 2, 2:3]))
                    dve.tensor_scalar(at_e[:, m % 2, 0:w], at_e[:, m % 2, 0:w], at_stat[:, m % 2, 3:4], None,
                                      ALU.mult).then_inc(at_prob, 1)
            dve.wait_ge(at_out, NU)
            dve.wait_ge(saved, 16 * 11)
            dve.sem_inc(mix_ready, 4)

        sync_layer0 = sync_layer1 = lambda sp: None


        block = ctx.enter_context(nc.Block())

        @block.sync
        def _(sp):
            sp.dma_start(cst[:, :], consts_in).then_inc(loaded, 16)
            sp.dma_start(par[:, :], params_in).then_inc(loaded, 16)
            sp.dma_start(lora[:, :, :], lora_in).then_inc(loaded, 16)
            sp.dma_start(x[:, :, :], x_in).then_inc(loaded, 16)

            def stream(src, n0, n, cols):
                def one(i, u):
                    at = src[i * RING + u]
                    sp.wait_ge(tiles_done, i * RING + n0 + u + 1)
                    r = (n0 + u) % RING
                    sp.dma_start(ring[:, r, 0:cols], at).then_inc(land[r], 16)
                looped(sp, n, one)

            for layer in range(DEPTH):
                for name, blocks, per in stages_of_layer(layer):
                    if name in w[layer]:
                        stream(w[layer][name], tile0[layer, name], blocks * per, w[layer][name].shape[-1])
                if layer == 0:
                    sync_layer0(sp)
                else:
                    sync_layer1(sp)
            sp.wait_ge(y_ready, DB)
            sp.dma_start(outs["y"], h[:, :, :]).then_inc(stored, 16)
            sp.wait_ge(stored, 16)


        @block.tensor
        def _(pe):
            pe.wait_ge(loaded, 64)
            pe.sem_inc(tiles_done, RING)

            def linear(layer, name, n, per, rhs, k_per_tile):
                b0, n0 = blk0[layer, name], tile0[layer, name]
                pairs_read(layer, name)
                reader, f0 = (free_act, free0[layer, name]["act"]) if name in PROJECTIONS else \
                             (free_dve, free0[layer, name]["dve"])

                def one(i, u):
                    pr, sa, _ = pair((b0 + u) % SETS)
                    pe.wait_ge(reader, i * 4 + f0 + u + 1 - SETS)
                    for t in range(per):
                        n_u = n0 + per * u + t
                        r = n_u % RING
                        pe.wait_ge(land[r], i * 16 * per + 16 * (n_u // RING + 1))
                        for k in range(k_per_tile):
                            first, last = t == 0 and k == 0, t == per - 1 and k == k_per_tile - 1
                            lhs = ring[:, r, k * P:(k + 1) * P]
                            src = rhs(t * k_per_tile + k)
                            pe.matmul(pr, lhs, src[:, PROMPT], start=first, stop=last)
                            mm = pe.matmul(sa, lhs, src[:, SAMPLE], start=first, stop=last)
                        mm.then_inc(tiles_done, 1)
                looped(pe, n, one)

            def pairs_read(layer, name):
                pe.wait_ge(free_dve, free0[layer, name]["dve"])
                pe.wait_ge(free_act, free0[layer, name]["act"])

            def ada(layer):
                b0, n0 = blk0[layer, "ada"], tile0[layer, "ada"]
                pe.wait_ge(cond_ready, 1)
                pairs_read(layer, "ada")
                _, sa, _ = pair(b0 % SETS)
                at = grid(sa, DEC_SEQ // 2, 2)

                def one(i, u):
                    r = (n0 + u) % RING
                    pe.wait_ge(land[r], i * 16 + 16 * ((n0 + u) // RING + 1))
                    for k in range(DB):
                        mm = pe.matmul(at[:, i * 4 + u, :], ring[:, r, k * P:(k + 1) * P], scond[:, k, :],
                                       start=(k == 0), stop=(k == DB - 1))
                    mm.then_inc(tiles_done, 1)
                looped(pe, N_MOD * DB, one)

            norms = [0]

            def norm(layer, name):
                pr, sa, _ = pair(blk0[layer, name] % SETS)
                pairs_read(layer, name)
                for k in range(DB):
                    pe.wait_ge(sq_ready, norms[0] * DB + k + 1)
                    pe.matmul(pr, C("ones"), h[:, k, PROMPT], start=(k == 0), stop=(k == DB - 1))
                    mm = pe.matmul(sa, C("ones"), h[:, k, SAMPLE], start=(k == 0), stop=(k == DB - 1))
                mm.then_inc(norm_ready, 1)
                norms[0] += 1

            for layer in range(DEPTH):
                ada(layer)
                for j in range(3):
                    norm(layer, f"norm{j}")
                    pe.wait_ge(h_ready, DB * norms[0])
                    if j != 1:
                        half = j // 2
                        linear(layer, f"up{half}", 2 * FB, 1, lambda k: h[:, k, :], DB)
                        pe.wait_ge(gated_ready, FB * (2 * layer + half + 1) + 2)
                        linear(layer, f"down{half}", DB, 2, lambda k: gated[:, k, :], HALF_K)
                    elif layer == 0:
                        linear(layer, "ret", RET_BLOCKS, 1, lambda k: h[:, k, :], DB)
                        tensor_retention(pe)
                        linear(layer, "rwkv", RWKV_BLOCKS, 1, lambda k: h[:, k, :], DB)
                        tensor_rwkv(pe)
                        pe.wait_ge(mix_ready, 8)
                        linear(layer, "out", DB, 1, lambda k: mix[:, k, :], DB)
                    else:
                        linear(layer, "mlstm", MLSTM_BLOCKS, 1, lambda k: h[:, k, :], DB)
                        tensor_mlstm(pe)
                        linear(layer, "att", ATT_BLOCKS, 1, lambda k: h[:, k, :], DB)
                        tensor_attention(pe)
                        pe.wait_ge(mix_ready, 16)
                        linear(layer, "out", DB, 1, lambda k: mix[:, k, :], DB)
            norm(DEPTH, "norm")


        @block.scalar
        def _(act):
            turn = Order(act, act_chain)
            act.wait_ge(loaded, 64)
            act.activation(scond[:, :, :], grid(prm("cond", 0, 2 * DB), DB, 2), ACT.Silu).then_inc(cond_ready, 1)
            act.sem_inc(free_act, SETS)

            norms, ups, projected = [0], [0], [0]

            def norm(shift):
                q = norms[0]
                for k in range(DB):
                    if q:
                        act.wait_ge(x_ready, DB * (q - 1) + k + 1)
                    act.activation(h[:, k, :], x[:, k, :], ACT.Square).then_inc(sq_ready, 1)
                act.wait_ge(ms_ready, q + 1)
                act.activation(rs[:, :], rs[:, :], ACT.Sqrt).then_inc(root_ready, 1)
                if shift is not None:
                    for k in range(DB):
                        act.wait_ge(scaled, DB * q + k + 1)
                        act.activation(h[:, k, PROMPT], h[:, k, PROMPT], ACT.Identity,
                                       bias=mod[:, shift * DB + k, 0:1])
                        act.activation(h[:, k, SAMPLE], h[:, k, SAMPLE], ACT.Identity,
                                       bias=mod[:, shift * DB + k, 1:2]).then_inc(h_ready, 1)
                norms[0] += 1

            def up(layer, name):
                b0, n0, g0 = blk0[layer, name], tile0[layer, name], FB * ups[0]

                def one(i, u):
                    act.wait_ge(tiles_done, i * 4 + RING + n0 + 2 * u + 1)
                    act.wait_ge(gated_ready, i * 2 + g0 + u + 1)
                    act.activation(silu[:, u, :], pair((b0 + 2 * u) % SETS)[2], ACT.Silu).then_inc(silu_ready, 1)
                with act.Fori(0, FB // 2) as i:
                    for u in range(2):
                        one(i, u)
                ups[0] += 1

            def project(layer, name, n, dst):
                b0, n0, p0 = blk0[layer, name], tile0[layer, name], projected[0]

                def one(i, u):
                    act.wait_ge(tiles_done, i * 4 + RING + n0 + u + 1)
                    act.activation(dst[:, i * 4 + u, :], pair((b0 + u) % SETS)[2], ACT.Copy)\
                       .then_inc(proj_ready, 1)
                    act.wait_ge(proj_ready, i * 4 + p0 + u + 1)
                    act.sem_inc(free_act, 1)
                looped(act, n, one)
                projected[0] += n

            for layer in range(DEPTH):
                act.wait_ge(mod_ready, layer + 1)
                norm(0)
                up(layer, "up0")
                norm(3)
                if layer == 0:
                    project(layer, "ret", RET_BLOCKS, rt_p)
                    scalar_retention(act, turn)
                    act.wait_ge(mix_ready, 4)
                    act.wait_ge(saved, 32)
                    project(layer, "rwkv", RWKV_BLOCKS, rw_p)
                    scalar_rwkv(act, turn)
                else:
                    project(layer, "mlstm", MLSTM_BLOCKS, ml_p)
                    scalar_mlstm(act, turn)
                    act.wait_ge(mix_ready, 12)
                    act.wait_ge(saved, 16 * 8)
                    project(layer, "att", ATT_BLOCKS, at_p)
                    scalar_attention(act, turn)
                norm(6)
                up(layer, "up1")
            norm(None)


        @block.vector
        def _(dve):
            turn = Order(dve, dve_chain)
            dve.wait_ge(loaded, 64)
            dve.sem_inc(free_dve, SETS)
            dve.sem_inc(gated_ready, 2)

            norms, ups = [0], [0]

            def modulation(layer):
                dve.wait_ge(tiles_done, RING + tile0[layer, "ada"] + N_MOD * DB)
                _, sa, _ = pair(blk0[layer, "ada"] % SETS)
                turn(dve.tensor_tensor(mod[:, :, :], grid(sa[:, 0:2 * N_MOD * DB], N_MOD * DB, 2),
                                       over(prm("ada_b", layer * N_MOD * DB, N_MOD * DB), 2), ALU.add))
                dve.sem_inc(free_dve, 1)
                for g in (2, 8):
                    m = mod[:, g * DB:(g + 1) * DB, :]
                    turn(dve.tensor_scalar(m, m, 0.5, None, ALU.mult))
                for j in range(3):
                    last = dve.scalar_tensor_tensor(out=gs[:, j, :, :], in0=mod[:, (3 * j + 1) * DB:(3 * j + 2) * DB, :],
                                             scalar=1.0, in1=over(prm("norm_g", (3 * layer + j) * DB, DB), 2),
                                             op0=ALU.add, op1=ALU.mult)
                turn(last)
                dve.sem_inc(mod_ready, 1)

            def norm(j, b0):
                q = norms[0]
                dve.wait_ge(norm_ready, q + 1)
                dve.tensor_scalar(rs[:, :], pair(b0 % SETS)[2], 1.0 / D_MODEL, EPS, ALU.mult, ALU.add)\
                   .then_inc(ms_ready, 1)
                dve.wait_ge(root_ready, q + 1)
                dve.sem_inc(free_dve, 1)
                turn(dve.reciprocal(rs[:, :], rs[:, :]))
                for k in range(DB):
                    if j is None:
                        dve.scalar_tensor_tensor(out=h[:, k, :], in0=x[:, k, :], scalar=prm("final", k),
                                                 in1=rs[:, :], op0=ALU.mult, op1=ALU.mult).then_inc(y_ready, 1)
                        continue
                    for part, cond in ((PROMPT, 0), (SAMPLE, 1)):
                        ins = dve.scalar_tensor_tensor(out=h[:, k, part], in0=x[:, k, part],
                                                       scalar=gs[:, j, k, cond:cond + 1], in1=rs[:, part],
                                                       op0=ALU.mult, op1=ALU.mult)
                    ins.then_inc(scaled, 1)
                norms[0] += 1

            def up(layer, name):
                b0, n0, g0 = blk0[layer, name], tile0[layer, name], FB * ups[0]
                with dve.Fori(0, FB // 2) as i:
                    for u in range(2):
                        dve.wait_ge(tiles_done, i * 4 + RING + n0 + 2 * u + 2)
                        dve.wait_ge(silu_ready, i * 2 + g0 + u + 1)
                        dve.tensor_tensor(gated[:, i * 2 + u, :], silu[:, u, :],
                                          pair((b0 + 2 * u + 1) % SETS)[2], ALU.mult).then_inc(gated_ready, 1)
                        dve.wait_ge(gated_ready, i * 2 + g0 + u + 3)
                        dve.sem_inc(free_dve, 2)
                ups[0] += 1

            def residual(layer, name, per, gate):
                b0, n0, x0 = blk0[layer, name], tile0[layer, name], DB * (norms[0] - 1)

                def one(i, u):
                    pr, sa, _ = pair((b0 + u) % SETS)
                    dve.wait_ge(tiles_done, i * 4 * per + RING + n0 + per * (u + 1))
                    for src, part, cond in ((pr, PROMPT, 0), (sa, SAMPLE, 1)):
                        xb = x[:, i * 4 + u, part]
                        ins = dve.scalar_tensor_tensor(out=xb, in0=src,
                                                       scalar=mod[:, i * 4 + (gate * DB + u), cond:cond + 1],
                                                       in1=xb, op0=ALU.mult, op1=ALU.add)
                    ins.then_inc(x_ready, 1)
                    dve.wait_ge(x_ready, i * 4 + x0 + u + 1)
                    dve.sem_inc(free_dve, 1)
                looped(dve, DB, one)

            for layer in range(DEPTH):
                modulation(layer)
                norm(0, blk0[layer, "norm0"])
                up(layer, "up0")
                residual(layer, "down0", 2, 2)
                norm(1, blk0[layer, "norm1"])
                if layer == 0:
                    vector_retention(dve, turn)
                    vector_rwkv(dve, turn)
                else:
                    vector_mlstm(dve, turn)
                    vector_attention(dve, turn)
                residual(layer, "out", 1, 5)
                norm(2, blk0[layer, "norm2"])
                up(layer, "up1")
                residual(layer, "down1", 2, 8)
            norm(None, blk0[DEPTH, "norm"])


        @block.gpsimd
        def _(pool):
            pool_retention(pool)
            pool_rwkv(pool)
            pool_mlstm(pool)
            pool_attention(pool)
            pool.wait_ge(saved, 16 * 11)



def _tiles(a, k):
    r, c = a.shape
    t = a.reshape(r // (k * P), k, P, c // P, P).transpose(3, 0, 2, 1, 4)
    return np.ascontiguousarray(t.reshape(-1, P, k * P))


def _cols(v):
    return np.ascontiguousarray(v).reshape(-1, P).T


def kernel(**inputs):
    import concourse.bacc as _bacc
    from concourse.bass_utils import run_bass_kernel_spmd as _run

    v = {k: np.asarray(a) for k, a in inputs.items()}
    f = np.float32
    arrays = {}
    tok = np.concatenate([v["x_prompt"][0], v["x_sample"][0]], 0)
    arrays["x_in"] = np.ascontiguousarray(tok.T.reshape(DB, P, NT).transpose(1, 0, 2))
    at, table = const_layout()
    arrays["consts"] = table

    for layer in range(DEPTH):
        arrays[f"w{layer}_ada"] = _tiles(v["ada_w"][layer], DB)
        for j in range(2):
            w1 = v["ffn_w1"][layer, j].reshape(D_MODEL, 2, FB, P).transpose(0, 2, 1, 3).reshape(D_MODEL, -1)
            arrays[f"w{layer}_up{j}"] = _tiles(w1, DB)
            arrays[f"w{layer}_down{j}"] = _tiles(v["ffn_w2"][layer, j], HALF_K)
    even, odd = v["w_in_even"][0], v["w_in_odd"][0]
    arrays["w0_ret"] = _tiles(even[:, :RET_BLOCKS * P], DB)
    arrays["w0_rwkv"] = _tiles(even[:, RET_BLOCKS * P:], DB)
    arrays["w0_out"] = _tiles(v["w_out_even"][0], DB)
    gates = np.zeros((2, D_MODEL, P), f)
    for g in range(2):
        for d in range(2):
            gates[g, :, 32 * d:32 * d + 4] = odd[:, 1536 + 8 * g + 4 * d:1536 + 8 * g + 4 * d + 4]
    arrays["w1_mlstm"] = _tiles(np.concatenate([odd[:, :1536], gates[0], gates[1], odd[:, 1552:2064]], 1), DB)
    q, k0, k1, vv = odd[:, 2064:2576], odd[:, 2576:2640], odd[:, 2640:2704], odd[:, 2704:2832]
    arrays["w1_att"] = _tiles(np.concatenate([q, k0, k0, k1, k1, vv], 1), DB)
    arrays["w1_out"] = _tiles(v["w_out_odd"][0], DB)

    pat, npar = param_layout()
    par = np.zeros((P, npar), f)

    def put(name, a):
        par[:a.shape[0], pat[name][0]:pat[name][0] + a.shape[1]] = a

    def rows(a):
        r = np.zeros((P, 1), f)
        r[0:4, 0], r[32:36, 0] = a[0], a[1]
        return r

    for name, key in (("norm_g", "norm_g"), ("final", "final_norm"), ("ada_b", "ada_b"), ("gn_w", "ret_gn_w"),
                      ("mu", "rwkv_mu"), ("w0", "rwkv_w0"), ("a0", "rwkv_a0"), ("k_k", "rwkv_k_k"),
                      ("k_a", "rwkv_k_a"), ("r_k", "rwkv_r_k"), ("ln_w", "rwkv_ln_w"), ("ln_b", "rwkv_ln_b"),
                      ("mn_w", "mlstm_norm_w")):
        put(name, _cols(v[key]))
    put("q_gain", np.tile(v["attn_qk_norm"][0, 0], 2)[:, None])
    put("k_gain", np.tile(v["attn_qk_norm"][0, 1], 2)[:, None])
    lg = v["ret_log_decay"][0]
    put("lg_head", np.tile(lg.reshape(1, 8), (P, 1)))
    put("lg_part", np.repeat(lg.reshape(2, 2, 2), HS, axis=2).reshape(4, P).T)
    put("m_init", rows(v["state_mlstm_m"][0, 0]))
    put("i_bias", rows(v["mlstm_i_bias"][0]))
    put("f_bias", rows(v["mlstm_f_bias"][0]))
    cond = np.stack([v["c_ctx"], v["c"][0]], 1)
    put("cond", cond.reshape(DB, P, 2).transpose(1, 0, 2).reshape(P, 2 * DB))
    arrays["params"] = par
    lora = np.zeros((P, 3, 512), f)
    for d in range(2):
        lora[:HS, d], lora[HS:, d] = v["rwkv_w2"][0, d], v["rwkv_a2"][0, d]
    lora[:, 2] = v["rwkv_g2"][0]
    arrays["lora_in"] = lora

    arrays["s_ret"] = v["state_ret"][0, 0].reshape(2, 2, P, P).transpose(0, 2, 1, 3)
    arrays["s_rwkv"] = v["state_rwkv"][0, 0].transpose(0, 1, 3, 2).reshape(2, 4, P, HS).transpose(0, 2, 1, 3)
    arrays["s_mc"] = np.concatenate([v["state_mlstm_c"][0, 0], v["state_mlstm_n"][0, 0][..., None]], -1)\
        .transpose(0, 2, 1, 3)
    ck = v["cache_k"][0, 0].transpose(2, 0, 1)
    arrays["s_ck"] = np.concatenate([ck, ck], 0)
    arrays["s_cv"] = v["cache_v"][0, 0].transpose(1, 0, 2)

    nc = _bacc.Bacc("TRN2", target_bir_lowering=False, num_devices=1)
    arrays = {k: np.ascontiguousarray(a) for k, a in arrays.items()}
    ap = {k: nc.dram_tensor(k, a.shape, F32, kind="ExternalInput").ap() for k, a in arrays.items()}
    shapes = {"y": (P, DB, NT), "ret": (2, P, 2, P), "rwkv": (2, P, 4, HS), "mc": (2, P, 4, P + 1),
              "m": (2, 4, 1), "ck": (2, HS, P), "cv": (P, P)}
    outs = {k: nc.dram_tensor(f"out_{k}", s, F32, kind="ExternalOutput").ap() for k, s in shapes.items()}
    w = [{n: ap[f"w{layer}_{n}"] for n, _, per in stages_of_layer(layer) if per} for layer in range(DEPTH)]
    st = {k: ap[k] for k in ("s_ret", "s_rwkv", "s_mc", "s_ck", "s_cv")}
    build(nc, w, ap["x_in"], ap["consts"], ap["params"], ap["lora_in"], st, outs)
    r = _run(nc, [arrays], core_ids=[0]).results[0]
    y = r["out_y"].transpose(2, 1, 0).reshape(NT, D_MODEL)
    ret = r["out_ret"].transpose(0, 2, 1, 3).reshape(1, 1, 2, 4, HS, P)
    rwkv = r["out_rwkv"].transpose(0, 2, 1, 3).reshape(2, 8, HS, HS).transpose(0, 1, 3, 2)[None, None]
    mc = r["out_mc"].transpose(0, 2, 1, 3)
    out = (y[None, :SEQ], y[None, SEQ:], ret, rwkv, mc[None, None, ..., :P], mc[None, None, ..., P],
           r["out_m"].reshape(1, 1, 2, 4), r["out_ck"].transpose(0, 2, 1)[None, None],
           r["out_cv"].reshape(P, 2, HS).transpose(1, 0, 2)[None, None])
    return tuple(np.ascontiguousarray(a) for a in out)
```

```python
from contextlib import ExitStack

import numpy as np
import concourse.bass as bass
from concourse import mybir

F32 = mybir.dt.float32
F32R = mybir.dt.float32r
ALU = mybir.AluOpType
ACT = mybir.ActivationFunctionType
AX = mybir.AxisListType

P = 128
D_MODEL, D_FF, N_MOD, DEPTH = 1024, 2816, 9, 2
SEQ, DEC_SEQ, PAST = 128, 512, 128
NT = SEQ + DEC_SEQ
NCH = NT // P
DB = D_MODEL // P
FB = D_FF // P
HALF_F = FB // 2
RING = 4
REST = 18560
SPLITS = 2
SETS = 4
EPS = 1e-6
GRID_W, ROPE_BASE = 64, 10000.0
HS = 64
LEVELS = 7
DECAY_MAX = float(np.exp(-0.5))

PROMPT = slice(0, SEQ)
SAMPLE = slice(SEQ, NT)
LEFT = slice(0, NT // 2)
RIGHT = slice(NT // 2, NT)

PROJECTIONS = ("ret", "rwkv", "mlstm", "att")
RET_BLOCKS, RWKV_BLOCKS = 12, 14
MLSTM_BLOCKS, ATT_BLOCKS = 18, 7


def const_layout():
    r = np.arange(P)
    row, col = r[:, None], r[None, :]
    parts = {
        "ident": (row == col),
        "ones": np.ones((P, P)),
        "ones64": (row // HS == col // HS),
        "mask_f": np.concatenate([row < col, row <= col], 1),
        "mask_b": np.concatenate([row > col, row >= col], 1),
    }
    lv = []
    for b in (1 << n for n in range(LEVELS)):
        same = row // (2 * b) == col // (2 * b)
        lv.append(same & (row % (2 * b) < b) & (col % (2 * b) >= b))
    parts["merge_f"] = np.concatenate(lv, 1)
    parts["merge_b"] = np.concatenate([m.T for m in lv], 1)
    perm = np.zeros((P, P))
    for m in range(P):
        if m % 32 < 16:
            perm[m + 16, m] = -1.0
        else:
            perm[m - 16, m] = 1.0
    parts["turn"] = perm
    nf = HS // 4
    inv = (np.float32(ROPE_BASE) ** (-np.arange(nf, dtype=np.float32) / np.float32(nf))).astype(np.float32)
    t = np.arange(DEC_SEQ)
    pos = np.where((r % HS < HS // 2)[:, None], (t // GRID_W)[None, :], (t % GRID_W)[None, :]).astype(np.float32)
    ang = pos * inv[r % nf][:, None]
    parts["cos"] = np.cos(ang)
    parts["sin"] = np.sin(ang)
    parts["ahead"] = np.maximum(col - row, 0)
    parts["behind"] = np.maximum(row - col, 0)
    parts["from1"] = np.broadcast_to(col + 1, (P, P))
    parts["to1"] = np.broadcast_to(P - col, (P, P))
    parts["left_f"] = (P - 1) - row
    parts["left_b"] = row
    parts["neg_f"] = np.where(row <= col, 0.0, -1e30)
    parts["neg_b"] = np.where(row >= col, 0.0, -1e30)
    at, cols = {}, 0
    for k, v in parts.items():
        at[k] = (cols, cols + v.shape[1])
        cols += v.shape[1]
    return at, np.concatenate([np.asarray(v, np.float32) for v in parts.values()], 1)


PARAM_COLS = [("norm_g", DEPTH * 3 * DB), ("final", DB), ("ada_b", DEPTH * N_MOD * DB), ("gn_w", 4), ("mu", 14),
              ("w0", 8), ("a0", 8), ("k_k", 4), ("k_a", 4), ("r_k", 4), ("ln_w", 4), ("ln_b", 4), ("mn_w", 4),
              ("q_gain", 1), ("k_gain", 1), ("lg_head", 8), ("lg_part", 4), ("m_init", 1), ("i_bias", 1),
              ("f_bias", 1), ("cond", 2 * DB)]


def param_layout():
    at, cols = {}, 0
    for k, n in PARAM_COLS:
        at[k] = (cols, cols + n)
        cols += n
    return at, cols


def stages_of_layer(layer):
    mixers = [("ret", RET_BLOCKS, DB), ("rwkv", RWKV_BLOCKS, DB)] if layer == 0 else \
             [("mlstm", MLSTM_BLOCKS, DB), ("att", ATT_BLOCKS, DB)]

    def ffn(j):
        return [(f"{what}{j}{half}", n, k) for half in "ab" for what, n, k in (("up", 2 * HALF_F, DB), ("down", DB, HALF_F))]

    return [("ada", N_MOD * DB, DB), ("norm0", 1, 0)] + ffn(0) + [("norm1", 1, 0)] + mixers + \
           [("out", DB, DB), ("norm2", 1, 0)] + ffn(1)


AFTER_MIXER = {"rwkv": 4, "out": 8, "att": 4}


def build(nc, w, x_in, consts_in, params_in, lora_in, st, outs, stop=None):
    cat, _ = const_layout()
    pat, npar = param_layout()

    tile0, blk0, free0, x0, tile_cols = {}, {}, {}, {}, []
    tiles = blks = xs = 0
    freed = {"dve": SETS, "act": SETS}
    for layer in range(DEPTH):
        for name, blocks, k in stages_of_layer(layer):
            tile0[layer, name], blk0[layer, name], x0[layer, name] = tiles, blks, xs
            free0[layer, name] = dict(freed)
            freed["act" if name in PROJECTIONS else "dve"] += 1 if name == "ada" else blocks
            if k:
                tiles += blocks
                tile_cols += [k * P] * blocks
            blks += 1 if name == "ada" else blocks
            xs += blocks if name == "out" or name.startswith("down") else 0
    blk0[DEPTH, "norm"], free0[DEPTH, "norm"], x0[DEPTH, "norm"] = blks, dict(freed), xs
    held = {tile0[0, "rwkv"], tile0[0, "out"], tile0[1, "att"], tile0[1, "out"]}
    held |= {tile0[layer, name] for layer in range(DEPTH) for name in ("ada", "up0a")}

    with ExitStack() as ctx:
        def sb(name, shape):
            return ctx.enter_context(nc.sbuf_tensor(name, shape, F32))

        def rounded(name, shape):
            return ctx.enter_context(nc.sbuf_tensor(name, shape, F32R))

        def shared(name, floats):
            with nc.sbuf_tensor(name, [P, floats], F32) as t:
                return t

        def sem(name):
            return ctx.enter_context(nc.semaphore(name))

        cst = sb("cst", [P, max(b for _, b in cat.values())])
        par = sb("par", [P, npar])
        x = sb("x", [P, DB, NT])
        lora = sb("lora", [P, 3, 512])
        mod = sb("mod", [P, N_MOD * DB, 2])
        gs = sb("gs", [P, 3, DB, 2])
        scond = sb("scond", [P, DB, 2])
        rs = sb("rs", [P, NT])

        h_mem = shared("h_mem", 2 * DB * NT)
        h_hi = rounded("h_hi", [P, DB, NT])
        h_lo = rounded("h_lo", [P, DB, NT])
        y = h_mem[:, 0:DB * NT].rearrange("p (a b) -> p a b", a=DB)
        ada_row = h_mem[0:2, 0:N_MOD * D_MODEL]
        TILE = HALF_F * P
        w_mem = shared("w_mem", (RING + 2 * SPLITS) * TILE)
        ring = sb("ring", [P, RING, TILE])
        w_hi = rounded("w_hi", [P, SPLITS, TILE])
        w_lo = rounded("w_lo", [P, SPLITS, TILE])
        rest = shared("rest", REST)
        g_hi = rounded("g_hi", [P, HALF_F, NT])
        g_lo = rounded("g_lo", [P, HALF_F, NT])
        silu = sb("silu", [P, 2, NT])
        prod = sb("prod", [P, 2, NT])
        normed = sb("normed", [P, 2, NT])
        sb("spare", [P, REST - (2 * HALF_F + 6) * NT])
        ps = ctx.enter_context(nc.psum_tensor("ps", [P, 8 * 512], F32))

        def C(name, rows=P):
            a, b = cat[name]
            return cst[0:rows, a:b]

        def prm(name, i=0, n=1, rows=P):
            a, _ = pat[name]
            return par[0:rows, a + i:a + i + n]

        def over(ap, n):
            return ap.unsqueeze(2).to_broadcast([ap.shape[0], ap.shape[1], n])

        def each(ap, n):
            return ap.unsqueeze(1).to_broadcast([ap.shape[0], n, ap.shape[1]])

        def pair(s):
            at = 1024 * s + 512
            return ps[:, at - NT // 2:at], ps[:, at:at + NT // 2], ps[:, at - NT // 2:at + NT // 2]

        def bank(b, lo=0, hi=512):
            return ps[:, 512 * b + lo:512 * b + hi]

        def grid(ap, *dims):
            names = "abcde"[:len(dims)]
            return ap.rearrange(f"p ({' '.join(names)}) -> p {' '.join(names)}",
                                **{k: d for k, d in zip(names[1:], dims[1:])})

        class Area:

            def __init__(self, mem, at=0, end=None):
                self.mem, self.at, self.end = mem, at, mem.shape[1] if end is None else end

            def take(self, *dims):
                n = int(np.prod(dims))
                v = self.mem[:, self.at:self.at + n]
                self.at += n
                assert self.at <= self.end, self.at
                return grid(v, *dims) if len(dims) > 1 else v

        def chunk(c):
            return slice(c * P, (c + 1) * P)

        ORDER = ([0, 1, 2, 3, 4], [0, 4, 3, 2, 1])

        par_loaded = sem("par_loaded")
        loaded = sem("loaded")
        land = [sem(f"land{r}") for r in range(RING)]
        high_ready = sem("high_ready")
        split_ready = sem("split_ready")
        tiles_done = sem("tiles_done")
        norm_ready = sem("norm_ready")
        free_dve = sem("free_dve")
        free_act = sem("free_act")
        silu_ready = sem("silu_ready")
        prod_ready = sem("prod_ready")
        g_high = sem("g_high")
        gated_ready = sem("gated_ready")
        mix_high = sem("mix_high")
        mix_split = sem("mix_split")
        cond_ready = sem("cond_ready")
        ada_row_ready = sem("ada_row_ready")
        ada_turned = sem("ada_turned")
        mod_ready = sem("mod_ready")
        x_ready = sem("x_ready")
        sq_ready = sem("sq_ready")
        ms_ready = sem("ms_ready")
        root_ready = sem("root_ready")
        scaled = sem("scaled")
        h_high = sem("h_high")
        h_ready = sem("h_ready")
        proj_ready = sem("proj_ready")
        mix_ready = sem("mix_ready")
        y_ready = sem("y_ready")
        stored = sem("stored")
        dve_chain = sem("dve_chain")
        act_chain = sem("act_chain")
        pool_chain = sem("pool_chain")

        class Order:

            def __init__(self, eng, s):
                self.eng, self.s, self.n = eng, s, 0

            def __call__(self, ins):
                self.n += 1
                ins.then_inc(self.s, 1)
                self.eng.wait_ge(self.s, self.n)

        def parts_first(eng, n):
            return range(n, n + SPLITS) if n in held else ()

        def high_part(act, n, i=0):
            r, cols = n % RING, tile_cols[n]
            act.wait_ge(land[r], i * 16 + 16 * (n // RING + 1))
            act.wait_ge(tiles_done, i * 4 + n + 1)
            act.activation(w_hi[:, n % SPLITS, 0:cols], ring[:, r, 0:cols], ACT.Copy).then_inc(high_ready, 1)

        def low_part(dve, n, i=0):
            r, cols = n % RING, tile_cols[n]
            dve.wait_ge(high_ready, i * 4 + n + 1)
            dve.tensor_tensor(w_lo[:, n % SPLITS, 0:cols], ring[:, r, 0:cols],
                              w_hi[:, n % SPLITS, 0:cols].bitcast(F32), ALU.subtract).then_inc(split_ready, 1)

        def stepped(eng, n0, n, part, body):
            def ahead(i, u):
                if n0 + u + SPLITS < tiles and not held & {n0 + u + 1, n0 + u + SPLITS}:
                    part(eng, n0 + u + SPLITS, i)
            m = (n - SPLITS) // 4
            if m > 1:
                with eng.Fori(0, m) as i:
                    for u in range(4):
                        body(i, u, lambda: part(eng, n0 + u + SPLITS, i))
            else:
                m = 0
            for t in range(4 * m, n):
                body(t // 4, t % 4, lambda: ahead(0, t))

        def looped(eng, n, body):
            if n // 4 > 1:
                with eng.Fori(0, n // 4) as i:
                    for u in range(4):
                        body(i, u)
            elif n // 4:
                for u in range(4):
                    body(0, u)
            for u in range(n % 4):
                body(n // 4, u)

        mx = Area(rest)
        mix = mx.take(DB, NT)

        def squares(name):
            return mix if name == "norm2" else y

        saved = sem("saved")
        first = sem("first")

        hn_mean = sem("hn_mean")
        hn_cent = sem("hn_cent")
        hn_sq = sem("hn_sq")
        hn_var = sem("hn_var")
        hn_ms = sem("hn_ms")
        hn_root = sem("hn_root")

        def tensor_head_norm(pe, q, src, table, tmp):
            for stage, go, done in ((src, None, hn_mean), (tmp, hn_sq, hn_var)):
                for b in range(4):
                    if go is not None:
                        pe.wait_ge(go, 4 * q + b + 1)
                    pr, sa, _ = pair(b)
                    pe.matmul(pr, table, stage[:, b, LEFT], start=True, stop=True)
                    pe.matmul(sa, table, stage[:, b, RIGHT], start=True, stop=True).then_inc(done, 1)

        def scalar_head_norm(act, q, src, tmp):
            for b in range(4):
                act.wait_ge(hn_cent, 4 * q + b + 1)
                act.activation(tmp[:, b, :], src[:, b, :], ACT.Square).then_inc(hn_sq, 1)
            for b in range(4):
                act.wait_ge(hn_ms, 4 * q + b + 1)
                act.activation(tmp[:, b, :], tmp[:, b, :], ACT.Sqrt).then_inc(hn_root, 1)

        def vector_head_norm(dve, turn, q, src, tmp, n, eps, weight):
            for b in range(4):
                dve.wait_ge(hn_mean, 4 * q + b + 1)
                dve.scalar_tensor_tensor(out=src[:, b, :], in0=pair(b)[2], scalar=-1.0 / n, in1=src[:, b, :],
                                         op0=ALU.mult, op1=ALU.add).then_inc(hn_cent, 1)
            for b in range(4):
                dve.wait_ge(hn_var, 4 * q + b + 1)
                dve.tensor_scalar(tmp[:, b, :], pair(b)[2], 1.0 / n, eps, ALU.mult, ALU.add).then_inc(hn_ms, 1)
            for b in range(4):
                dve.wait_ge(hn_root, 4 * q + b + 1)
                turn(dve.reciprocal(tmp[:, b, :], tmp[:, b, :]))
                turn(dve.scalar_tensor_tensor(out=src[:, b, :], in0=src[:, b, :], scalar=prm(weight, b),
                                              in1=tmp[:, b, :], op0=ALU.mult, op1=ALU.mult))

        ra = Area(rest, mx.at)
        rt_p = ra.take(RET_BLOCKS, NT)
        rl, ra = ra, Area(w_mem)
        rt_v = ra.take(NCH, 512)
        rt_k = ra.take(2, NCH, 256)
        rt_decay = ra.take(4, P)
        rt_back = rl.take(4, P)
        rt_qdec = rl.take(4, P)
        rt_q = rl.take(2, 4, P)
        rt_att = rl.take(2, 4, P)
        rt_s = ra.take(2, NCH, 2, P)
        rt_end = ra.take(2, 2, P)
        rt_kdec = rl.take(8)
        rt_cdec = rl.take(4)
        rt_rope = rl.take(2, DEC_SEQ)

        rt_tab = sem("rt_tab")
        rt_turned = sem("rt_turned")
        rt_roped = sem("rt_roped")
        rt_vt = sem("rt_vt")
        rt_v_ready = sem("rt_v_ready")
        rt_kt = sem("rt_kt")
        rt_k_ready = sem("rt_k_ready")
        rt_zero = sem("rt_zero")
        rt_upd = sem("rt_upd")
        rt_state = sem("rt_state")
        rt_qs = sem("rt_qs")
        rt_score = sem("rt_score")
        rt_weighed = sem("rt_weighed")
        rt_o = sem("rt_o")
        rt_out = sem("rt_out")
        rt_silu = sem("rt_silu")
        RT_UPD = [(d, i) for d in range(2) for i in range(NCH - 1)]

        def pool_retention(pool):
            pool.wait_ge(proj_ready, RET_BLOCKS)
            for d in range(2):
                pool.memset(rt_s[:, d, 0, :, :], 0.0).then_inc(rt_zero, 1)
                pool.dma_start(rt_s[:, d, ORDER[d][1], :, :], st["s_ret"][d]).then_inc(first, 16)
            for d in range(2):
                pool.wait_ge(rt_state, (NCH - 1) * d + 1)
                pool.dma_start(outs["ret"][d], rt_end[:, d, :, :]).then_inc(saved, 16)

        def tensor_retention(pe):
            pe.wait_ge(proj_ready, RET_BLOCKS)
            for b in range(4):
                pe.matmul(bank(b), C("turn"), rt_p[:, b, SAMPLE], start=True, stop=True).then_inc(rt_turned, 1)
            for c in range(NCH):
                if c >= 2:
                    pe.wait_ge(rt_v_ready, c - 1)
                for b in range(4):
                    ins = pe.transpose(bank(4 + c % 2, b * P, b * P + P), rt_p[:, 4 + b, chunk(c)], C("ident"))
                ins.then_inc(rt_vt, 1)
            pe.wait_ge(rt_roped, 4)
            for c in range(NCH):
                if c >= 2:
                    pe.wait_ge(rt_k_ready, c - 1)
                for b in range(2):
                    ins = pe.transpose(bank(6 + c % 2, b * P, b * P + P), rt_p[:, 2 + b, chunk(c)], C("ident"))
                ins.then_inc(rt_kt, 1)
            pe.wait_ge(rt_v_ready, NCH)
            pe.wait_ge(rt_k_ready, NCH)
            for n, (d, i) in enumerate(RT_UPD):
                c = ORDER[d][i]
                for hd in range(4):
                    lo, b = HS * (hd % 2), hd // 2
                    ins = pe.matmul(bank(n, b * P, b * P + P)[lo:lo + HS], rt_k[:, d, c, hd * HS:hd * HS + HS],
                                    rt_v[:, c, hd * P:hd * P + P], start=True, stop=True)
                ins.then_inc(rt_upd, 1)
            pe.wait_ge(rt_state, 2 * (NCH - 1))
            pe.wait_ge(first, 32)
            pe.wait_ge(rt_zero, 2)

            def scores(c):
                if c >= 2:
                    pe.wait_ge(rt_weighed, c - 1)
                for hd in range(4):
                    lo, b = HS * (hd % 2), hd // 2
                    ins = pe.matmul(bank(4 * (c % 2) + hd % 2, b * P, b * P + P), rt_p[lo:lo + HS, 2 + b, chunk(c)],
                                    rt_p[lo:lo + HS, b, chunk(c)], start=True, stop=True)
                ins.then_inc(rt_score, 1)

            def output(c):
                if c >= 2:
                    pe.wait_ge(rt_out, c - 1)
                pe.wait_ge(rt_weighed, c + 1)
                pe.wait_ge(rt_qs, c + 1)
                for hd in (0, 2, 1, 3):
                    lo, b = HS * (hd % 2), hd // 2
                    out = bank(4 * (c % 2) + 2 + hd % 2, b * P, b * P + P)
                    pe.matmul(out, rt_v[:, c, hd * P:hd * P + P], rt_att[:, c % 2, 2 * (hd % 2) + b, :],
                              start=True, stop=False)
                    for d in range(2):
                        ins = pe.matmul(out, rt_s[lo:lo + HS, d, c, b, :], rt_q[lo:lo + HS, c % 2, 2 * d + b, :],
                                        start=False, stop=(d == 1))
                ins.then_inc(rt_o, 1)

            scores(0)
            for c in range(NCH):
                if c + 1 < NCH:
                    scores(c + 1)
                output(c)
            pe.wait_ge(rt_out, NCH)
            tensor_head_norm(pe, 0, mix[:, 0:4, :], C("ones"), rt_v.rearrange("p a b -> p (a b)")
                             .rearrange("p (a b) -> p a b", a=4))
            pe.wait_ge(hn_ms, 4)

        def scalar_retention(act, turn):
            for d, table in ((0, rt_decay), (1, rt_back)):
                for hd in range(4):
                    act.activation(table[:, 2 * (hd % 2) + hd // 2, :], C(("ahead", "behind")[d]), ACT.Exp,
                                   scale=prm("lg_head", 4 * d + hd))
                for b in range(2):
                    act.activation(rt_qdec[:, 2 * d + b, :], C(("from1", "to1")[d]), ACT.Exp,
                                   scale=prm("lg_part", 2 * d + b))
                act.activation(rt_kdec[:, 4 * d:4 * d + 4], prm("lg_head", 4 * d, 4), ACT.Exp,
                               scale=C(("left_f", "left_b")[d]))
            act.activation(rt_cdec[:, :], prm("lg_part", 0, 4), ACT.Exp, scale=float(P)).then_inc(rt_tab, 1)
            for c in range(NCH):
                act.wait_ge(rt_vt, c + 1)
                act.activation(rt_v[:, c, :], bank(4 + c % 2), ACT.Copy).then_inc(rt_v_ready, 1)
            act.activation(rt_p[:, 8:12, :], rt_p[:, 8:12, :], ACT.Silu).then_inc(rt_silu, 1)
            for c in range(NCH):
                act.wait_ge(rt_o, c + 1)
                for q in range(2):
                    ins = act.activation(mix[:, q:4:2, chunk(c)], grid(bank(4 * (c % 2) + 2 + q, 0, 256), 2, P), ACT.Copy)
                ins.then_inc(rt_out, 1)
            scalar_head_norm(act, 0, mix[:, 0:4, :], rt_v.rearrange("p a b -> p (a b)")
                             .rearrange("p (a b) -> p a b", a=4))

        def vector_retention(dve, turn):
            dve.wait_ge(rt_tab, 1)
            turn(dve.tensor_scalar(rt_kdec[:, :], rt_kdec[:, :], HS ** -0.5, None, ALU.mult))
            dve.tensor_tensor(rt_decay[:, :, :], rt_decay[:, :, :], each(C("mask_f")[:, P:2 * P], 4), ALU.mult)
            turn(dve.tensor_tensor(rt_back[:, :, :], rt_back[:, :, :], each(C("mask_b")[:, P:2 * P], 4), ALU.mult))
            turn(dve.tensor_tensor(rt_decay[:, :, :], rt_decay[:, :, :], rt_back[:, :, :], ALU.add))
            turn(dve.tensor_scalar(rt_decay[:, :, :], rt_decay[:, :, :], HS ** -0.5, None, ALU.mult))
            for b in range(4):
                rope(dve, turn, rt_p[:, b, SAMPLE], bank(b), rt_rope[:, b % 2, :], rt_turned, b + 1, rt_roped)
            for c in range(NCH):
                dve.wait_ge(rt_kt, c + 1)
                for d in range(2):
                    ins = dve.tensor_tensor(grid(rt_k[:, d, c, :], 4, HS), grid(bank(6 + c % 2, 0, 256), 4, HS),
                                            over(rt_kdec[:, 4 * d:4 * d + 4], HS), ALU.mult)
                ins.then_inc(rt_k_ready, 1)
            dve.wait_ge(rt_zero, 2)
            dve.wait_ge(first, 32)
            for n, (d, i) in enumerate(RT_UPD):
                dve.wait_ge(rt_upd, n + 1)
                old = rt_s[:, d, ORDER[d][i], :, :]
                new = rt_end[:, d, :, :] if i == 0 else rt_s[:, d, ORDER[d][i + 1], :, :]
                for b in range(2):
                    ins = dve.scalar_tensor_tensor(out=new[:, b, :], in0=old[:, b, :],
                                                   scalar=rt_cdec[:, 2 * d + b:2 * d + b + 1],
                                                   in1=bank(n, b * P, b * P + P), op0=ALU.mult, op1=ALU.add)
                ins.then_inc(rt_state, 1)
                dve.wait_ge(rt_state, n + 1)
            for c in range(NCH):
                dve.wait_ge(rt_score, c + 1)
                if c >= 2:
                    dve.wait_ge(rt_o, c - 1)
                two = grid(ps[:, 2048 * (c % 2):2048 * (c % 2) + 1024], 2, 512)[:, :, 0:256]
                dve.tensor_tensor(grid(rt_att[:, c % 2, :, :].rearrange("p a b -> p (a b)"), 2, 256), two,
                                  grid(rt_decay[:, :, :].rearrange("p a b -> p (a b)"), 2, 256), ALU.mult)\
                   .then_inc(rt_weighed, 1)
                for d in range(2):
                    ins = dve.tensor_tensor(rt_q[:, c % 2, 2 * d:2 * d + 2, :], rt_p[:, 0:2, chunk(c)],
                                            rt_qdec[:, 2 * d:2 * d + 2, :], ALU.mult)
                ins.then_inc(rt_qs, 1)
            tmp = rt_v.rearrange("p a b -> p (a b)").rearrange("p (a b) -> p a b", a=4)
            vector_head_norm(dve, turn, 0, mix[:, 0:4, :], tmp, P, 1e-5, "gn_w")
            dve.wait_ge(rt_silu, 1)
            turn(dve.tensor_tensor(mix[:, 0:4, :], mix[:, 0:4, :], rt_p[:, 8:12, :], ALU.mult))
            dve.sem_inc(mix_ready, 4)

        def rope(dve, turn, v, turned, tmp, go, count, done):
            dve.wait_ge(go, count)
            dve.tensor_tensor(tmp, turned, C("sin"), ALU.mult)
            turn(dve.tensor_tensor(v, v, C("cos"), ALU.mult))
            dve.tensor_tensor(v, v, tmp, ALU.add).then_inc(done, 1)
            dve.wait_ge(done, count)

        wa = Area(rest, mx.at)
        rw_p = wa.take(RWKV_BLOCKS, NT)
        shifted = wa.take(2, NT)
        wl = wa
        wa, wh = Area(w_mem), Area(h_mem)
        rw_kk = wh.take(4, NT)
        rw_v = wh.take(NCH, 512)
        rw_w = wa.take(4, P)
        rw_f = wa.take(4, P + 1)
        rw_up = wa.take(4, P + 1)
        rw_dn = wa.take(4, P + 1)
        rw_a = wa.take(4, P)
        rw_k = wa.take(4, P)
        rw_b = wa.take(4, P)
        rw_ar = wa.take(4, 2, P)
        rw_bn = wa.take(4, P)
        rw_kn = wa.take(4, P)
        rw_mb = wh.take(2, 4, 2, P)
        rw_mk = wh.take(2, 4, 2, P)
        rw_abt = wh.take(2, 4, P)
        rw_t = wa.take(2, 4, P)
        rw_tt = wa.take(2, 4, P)
        rw_q = wa.take(2, 4, P)
        rw_r = wl.take(8, HS)
        rw_u = wl.take(8, HS)
        rw_s = wl.take(2, 4, HS)
        rw_tmp = Area(w_mem).take(4, NT)
        rw_one_ka = rs[:, 0:4]

        rw_shift = sem("rw_shift")
        rw_near = sem("rw_near")
        rw_tanh = sem("rw_tanh")
        rw_kraw = sem("rw_kraw")
        rw_ksq = sem("rw_ksq")
        rw_ksum = sem("rw_ksum")
        rw_kroot = sem("rw_kroot")
        rw_kk_ready = sem("rw_kk_ready")
        rw_vt = sem("rw_vt")
        rw_v_ready = sem("rw_v_ready")
        rw_lora = sem("rw_lora")
        rw_z = sem("rw_z")
        rw_th = sem("rw_th")
        rw_sum = sem("rw_sum")
        rw_exp = sem("rw_exp")
        rw_prep = sem("rw_prep")
        rw_mm = [sem(f"rw_mm{g}") for g in range(2)]
        rw_masked = [sem(f"rw_masked{g}") for g in range(2)]
        rw_tr = [sem(f"rw_tr{g}") for g in range(2)]
        rw_qm = [sem(f"rw_qm{g}") for g in range(2)]
        rw_qs = [sem(f"rw_qs{g}") for g in range(2)]
        rw_zm = [sem(f"rw_zm{g}") for g in range(2)]
        rw_tp = [sem(f"rw_tp{g}") for g in range(2)]
        rw_tt_ready = [sem(f"rw_tt_ready{g}") for g in range(2)]
        rw_natp = sem("rw_natp")
        rw_nat = sem("rw_nat")
        rw_s0 = sem("rw_s0")
        rw_rm = sem("rw_rm")
        rw_r_ready = sem("rw_r_ready")
        rw_um = sem("rw_um")
        rw_u_ready = sem("rw_u_ready")
        rw_y = sem("rw_y")
        rw_y_added = sem("rw_y_added")
        rw_sm = sem("rw_sm")
        rw_s_ready = sem("rw_s_ready")
        rw_zero = sem("rw_zero")
        rw_first = sem("rw_first")
        rw_bonus = sem("rw_bonus")
        rw_bsum = sem("rw_bsum")
        rw_badd = sem("rw_badd")
        rw_g = sem("rw_g")

        RW_BATCHES = [(d, i) for i in range(NCH) for d in range(2)]
        NB = len(RW_BATCHES)

        def where(hd):
            b, odd = hd // 2, hd % 2
            return b, HS * odd, b // 2, 2 * odd + b % 2

        def pool_rwkv(pool):
            pool.wait_ge(proj_ready, RET_BLOCKS + RWKV_BLOCKS)
            for d in range(2):
                pool.memset(rw_s[:, d, :, :], 0.0).then_inc(rw_zero, 1)
            for d in range(2):
                pool.wait_ge(rw_s_ready, d + 1)
                pool.dma_start(outs["rwkv"][d], rw_s[:, d, :, :]).then_inc(saved, 16)
                pool.wait_ge(saved, 16 * (d + 3))
                pool.dma_start(rw_s[:, d, :, :], st["s_rwkv"][d]).then_inc(rw_first, 16)

        def tensor_rwkv(pe):
            pe.wait_ge(proj_ready, RET_BLOCKS + RWKV_BLOCKS)
            pe.wait_ge(rw_shift, RWKV_BLOCKS)
            for b in range(4):
                pe.wait_ge(rw_ksq, b + 1)
                left, right, _ = pair(b)
                pe.matmul(left, C("ones64"), rw_tmp[:, b, LEFT], start=True, stop=True)
                pe.matmul(right, C("ones64"), rw_tmp[:, b, RIGHT], start=True, stop=True).then_inc(rw_ksum, 1)
            pe.wait_ge(rw_kroot, 4)
            for c in range(NCH):
                if c >= 2:
                    pe.wait_ge(rw_v_ready, c - 1)
                for b in range(4):
                    ins = pe.transpose(bank(c % 2, b * P, b * P + P), rw_p[:, 8 + b, chunk(c)], C("ident"))
                ins.then_inc(rw_vt, 1)
            pe.wait_ge(rw_v_ready, NCH)
            pe.wait_ge(rw_tanh, 1)
            for n, (d, i) in enumerate(RW_BATCHES):
                c = ORDER[d][i]
                if n:
                    pe.wait_ge(rw_u_ready, n)
                    pe.wait_ge(rw_r_ready, n)
                    pe.wait_ge(rw_y_added, n)
                    pe.wait_ge(rw_s_ready, n)
                    pe.wait_ge(rw_nat, 2 * n)
                for b in range(4):
                    pe.matmul(bank(0, b * P, b * P + P), lora[0:HS, d, b * P:(b + 1) * P],
                              rw_p[0:HS, 12, chunk(c)], start=True, stop=True)
                for b in range(4):
                    ins = pe.matmul(bank(1, b * P, b * P + P), lora[HS:P, d, b * P:(b + 1) * P],
                                    rw_p[HS:P, 12, chunk(c)], start=True, stop=True)
                ins.then_inc(rw_lora, 1)
                pe.wait_ge(rw_prep, n + 1)
                for g in range(2):
                    heads = [hd for hd in range(8) if where(hd)[2] == g]
                    for k, lhs in ((0, rw_b), (1, rw_k)):
                        for hd in heads:
                            b, lo, _, q = where(hd)
                            ins = pe.matmul(bank(4 * g + 2 * k + q // 2, 256 * (q % 2), 256 * (q % 2) + 256),
                                            lhs[lo:lo + HS, b, :], rw_ar[lo:lo + HS, b, :, :]
                                            .rearrange("p a b -> p (a b)"), start=True, stop=True)
                        ins.then_inc(rw_mm[g], 1)
                for g in range(2):
                    pe.wait_ge(rw_masked[g], 3 * n + 1)
                    for hd in [hd for hd in range(8) if where(hd)[2] == g]:
                        b, lo, _, q = where(hd)
                        ins = pe.matmul(bank(4 * g + q // 2, P * (q % 2), P * (q % 2) + P),
                                        rw_ar[lo:lo + HS, b, 0, :], rw_b[lo:lo + HS, b, :], start=True, stop=True)
                    ins.then_inc(rw_mm[g], 1)
                for lv in range(1, LEVELS):
                    for g in range(2):
                        pe.wait_ge(rw_tr[g], LEVELS * n + lv)
                        if lv == 1:
                            pe.wait_ge(rw_masked[g], 3 * n + 3)
                        for q in range(4):
                            ins = pe.matmul(bank(4 * g, q * P, q * P + P), rw_abt[:, g, q, :], rw_t[:, g, q, :],
                                            start=True, stop=True)
                        ins.then_inc(rw_qm[g], 1)
                    for g in range(2):
                        pe.wait_ge(rw_qs[g], (LEVELS - 1) * n + lv)
                        if lv > 1:
                            pe.wait_ge(rw_tt_ready[g], (LEVELS - 2) * n + lv - 1)
                        for q in range(4):
                            ins = pe.matmul(bank(4 * g + 1, q * P, q * P + P), rw_tt[:, g, q, :], rw_q[:, g, q, :],
                                            start=True, stop=True)
                        ins.then_inc(rw_zm[g], 1)
                    if lv < LEVELS - 1:
                        for g in range(2):
                            pe.wait_ge(rw_tr[g], LEVELS * n + lv + 1)
                            for q in range(4):
                                ins = pe.transpose(bank(4 * g + 2, q * P, q * P + P), rw_t[:, g, q, :], C("ident"))
                            ins.then_inc(rw_tp[g], 1)
                for g in range(2):
                    pe.wait_ge(rw_tr[g], LEVELS * (n + 1))
                for j, src in ((0, rw_b), (1, rw_k)):
                    for b in range(4):
                        ins = pe.transpose(bank(5 + j, b * P, b * P + P), src[:, b, :], C("ident"))
                    ins.then_inc(rw_natp, 1)
                pe.wait_ge(rw_s0, n + 1)
                for hd in (0, 2, 4, 6, 1, 3, 5, 7):
                    b, lo, g, q = where(hd)
                    out = bank(3 + 4 * (hd % 2), b * HS, b * HS + HS)
                    pe.matmul(out, rw_ar[lo:lo + HS, b, 0, :], rw_s[lo:lo + HS, d, b, :], start=True, stop=False)
                    ins = pe.matmul(out, rw_mk[:, g, q, 0, :], rw_v[:, c, hd * HS:hd * HS + HS],
                                    start=False, stop=True)
                ins.then_inc(rw_rm, 1)
                pe.wait_ge(rw_r_ready, n + 1)
                for hd in range(8):
                    b, lo, g, q = where(hd)
                    ins = pe.matmul(bank(0, hd * HS, hd * HS + HS), rw_t[:, g, q, :], rw_r[:, hd, :],
                                    start=True, stop=True)
                ins.then_inc(rw_um, 1)
                pe.wait_ge(rw_u_ready, n + 1)
                for hd in (0, 2, 4, 6, 1, 3, 5, 7):
                    b, lo, g, q = where(hd)
                    out = bank(1 + hd % 2, b * P, b * P + P)[lo:lo + HS]
                    pe.matmul(out, rw_s[lo:lo + HS, d, b, :], rw_ar[lo:lo + HS, b, 1, :], start=True, stop=False)
                    pe.matmul(out, rw_u[:, hd, :], rw_mb[:, g, q, 1, :], start=False, stop=False)
                    ins = pe.matmul(out, rw_v[:, c, hd * HS:hd * HS + HS], rw_mk[:, g, q, 1, :],
                                    start=False, stop=True)
                ins.then_inc(rw_y, 1)
                pe.wait_ge(rw_nat, 2 * (n + 1))
                for hd in range(8):
                    b, lo, g, q = where(hd)
                    out = bank(4, b * HS, b * HS + HS)[lo:lo + HS]
                    pe.matmul(out, rw_bn[:, b, lo:lo + HS], rw_u[:, hd, :], start=True, stop=False)
                    ins = pe.matmul(out, rw_kn[:, b, lo:lo + HS], rw_v[:, c, hd * HS:hd * HS + HS],
                                    start=False, stop=True)
                ins.then_inc(rw_sm, 1)
            pe.wait_ge(rw_y_added, NB)
            pe.wait_ge(rw_s_ready, NB)
            tensor_head_norm(pe, 1, mix[:, 4:8, :], C("ones64"), rw_tmp)
            for b in range(4):
                pe.wait_ge(rw_bonus, b + 1)
                left, right, _ = pair(b)
                pe.matmul(left, C("ones64"), rw_p[:, b, LEFT], start=True, stop=True)
                pe.matmul(right, C("ones64"), rw_p[:, b, RIGHT], start=True, stop=True).then_inc(rw_bsum, 1)
            for b in range(4):
                pe.wait_ge(rw_badd, b + 1)
                left, right, _ = pair(b)
                pe.matmul(left, lora[:, 2, b * P:(b + 1) * P], rw_p[:, 13, LEFT], start=True, stop=True)
                pe.matmul(right, lora[:, 2, b * P:(b + 1) * P], rw_p[:, 13, RIGHT], start=True, stop=True)\
                  .then_inc(rw_g, 1)

        def scalar_rwkv(act, turn):
            act.wait_ge(rw_shift, RWKV_BLOCKS)
            act.activation(rw_p[0:HS, 12, :], rw_p[0:HS, 12, :], ACT.Tanh)
            act.activation(rw_p[:, 13, :], rw_p[:, 13, :], ACT.Sigmoid).then_inc(rw_tanh, 1)
            for b in range(4):
                act.wait_ge(rw_kraw, b + 1)
                act.activation(rw_tmp[:, b, :], rw_kk[:, b, :], ACT.Square).then_inc(rw_ksq, 1)
            for b in range(4):
                act.wait_ge(rw_ksum, b + 1)
                act.activation(rw_tmp[:, b, :], pair(b)[2], ACT.Sqrt).then_inc(rw_kroot, 1)
            for c in range(NCH):
                act.wait_ge(rw_vt, c + 1)
                act.activation(rw_v[:, c, :], bank(c % 2), ACT.Copy).then_inc(rw_v_ready, 1)
            for n in range(NB):
                act.wait_ge(rw_z, 2 * n + 1)
                act.activation(rw_w[:, :, :], rw_w[:, :, :], ACT.Tanh, scale=0.5).then_inc(rw_th, 1)
                act.wait_ge(rw_z, 2 * n + 2)
                act.activation(rw_a[:, :, :], rw_a[:, :, :], ACT.Tanh, scale=0.5).then_inc(rw_th, 1)
                act.wait_ge(rw_sum, n + 1)
                act.activation(rw_dn[:, :, :], rw_up[:, :, :], ACT.Exp, scale=-1.0)
                act.activation(rw_up[:, :, :], rw_up[:, :, :], ACT.Exp).then_inc(rw_exp, 1)
                for lv in range(1, LEVELS - 1):
                    for g in range(2):
                        act.wait_ge(rw_tp[g], (LEVELS - 2) * n + lv)
                        act.activation(rw_tt[:, g, :, :].rearrange("p a b -> p (a b)"), bank(4 * g + 2), ACT.Copy)\
                           .then_inc(rw_tt_ready[g], 1)
                for j, dst in ((0, rw_bn), (1, rw_kn)):
                    act.wait_ge(rw_natp, 2 * n + j + 1)
                    act.activation(dst[:, :, :].rearrange("p a b -> p (a b)"), bank(5 + j), ACT.Copy)\
                       .then_inc(rw_nat, 1)
                act.wait_ge(rw_rm, n + 1)
                for odd in range(2):
                    ins = act.activation(rw_r[:, odd:8:2, :], grid(bank(3 + 4 * odd, 0, 256), 4, HS), ACT.Copy)
                ins.then_inc(rw_r_ready, 1)
                act.wait_ge(rw_um, n + 1)
                act.activation(rw_u[:, :, :].rearrange("p a b -> p (a b)"), bank(0), ACT.Copy).then_inc(rw_u_ready, 1)
            scalar_head_norm(act, 1, mix[:, 4:8, :], rw_tmp)

        def vector_shift(dve, i, u):
            dve.wait_ge(proj_ready, i * 4 + RET_BLOCKS + u + 1)
            s, v = shifted[:, u % 2, :], rw_p[:, i * 4 + u, :]
            mu = par[:, bass.ds(i * 4 + (pat["mu"][0] + u), 1)]
            for lo, hi in ((0, SEQ), (SEQ, NT)):
                dve.tensor_tensor(s[:, lo + 1:hi - 1], v[:, lo:hi - 2], v[:, lo + 2:hi], ALU.add)
                dve.tensor_copy(s[:, lo:lo + 1], v[:, lo + 1:lo + 2])
                last = dve.tensor_copy(s[:, hi - 1:hi], v[:, hi - 2:hi - 1])
            last.then_inc(rw_near, 1)
            dve.wait_ge(rw_near, i * 8 + 2 * u + 1)
            dve.scalar_tensor_tensor(out=s, in0=s, scalar=0.5, in1=v, op0=ALU.mult, op1=ALU.subtract)\
               .then_inc(rw_near, 1)
            dve.wait_ge(rw_near, i * 8 + 2 * u + 2)
            dve.scalar_tensor_tensor(out=v, in0=s, scalar=mu, in1=v, op0=ALU.mult, op1=ALU.add)\
               .then_inc(rw_shift, 1)

        def vector_rwkv(dve, turn):
            turn(dve.tensor_scalar(rw_one_ka, prm("k_a", 0, 4), -1.0, 1.0, ALU.mult, ALU.add))
            dve.wait_ge(rw_shift, RWKV_BLOCKS)
            for b in range(4):
                dve.tensor_scalar(rw_kk[:, b, :], rw_p[:, 4 + b, :], prm("k_k", b), None, ALU.mult)\
                   .then_inc(rw_kraw, 1)
            for b in range(4):
                dve.wait_ge(rw_kroot, b + 1)
                turn(dve.tensor_scalar(rw_tmp[:, b, :], rw_tmp[:, b, :], 1e-12, None, ALU.max))
                turn(dve.reciprocal(rw_tmp[:, b, :], rw_tmp[:, b, :]))
                dve.tensor_tensor(rw_kk[:, b, :], rw_kk[:, b, :], rw_tmp[:, b, :], ALU.mult).then_inc(rw_kk_ready, 1)
            dve.wait_ge(rw_kk_ready, 4)
            turn(dve.memset(rw_f[:, :, 0:1], 0.0))
            dve.wait_ge(rw_zero, 2)
            for n, (d, i) in enumerate(RW_BATCHES):
                c = ORDER[d][i]
                grow, shrink = (rw_dn, rw_up) if d == 0 else (rw_up, rw_dn)
                with_own = slice(1, P + 1) if d == 0 else slice(0, P)
                before = slice(0, P) if d == 0 else slice(1, P + 1)
                start, end = (0, P) if d == 0 else (P, 0)
                dve.wait_ge(rw_lora, n + 1)
                dve.tensor_tensor(rw_w[:, :, :], grid(bank(0), 4, P), over(prm("w0", 4 * d, 4), P), ALU.add)\
                   .then_inc(rw_z, 1)
                dve.tensor_tensor(rw_a[:, :, :], grid(bank(1), 4, P), over(prm("a0", 4 * d, 4), P), ALU.add)\
                   .then_inc(rw_z, 1)
                dve.wait_ge(rw_th, 2 * n + 1)
                turn(dve.tensor_scalar(rw_w[:, :, :], rw_w[:, :, :], -DECAY_MAX / 2, -DECAY_MAX / 2,
                                       ALU.mult, ALU.add))
                for b in range(4):
                    last = dve.tensor_tensor_scan(rw_f[:, b, 1:P + 1], C("ones"), rw_w[:, b, :], 0.0,
                                                  ALU.mult, ALU.add)
                turn(last)
                dve.tensor_tensor(rw_up[:, :, :], rw_f[:, :, :],
                                  rw_f[:, :, P // 2:P // 2 + 1].to_broadcast([P, 4, P + 1]), ALU.subtract)\
                   .then_inc(rw_sum, 1)
                dve.wait_ge(rw_th, 2 * n + 2)
                turn(dve.tensor_scalar(rw_a[:, :, :], rw_a[:, :, :], 0.5, 0.5, ALU.mult, ALU.add))
                dve.tensor_tensor(rw_b[:, :, :], rw_kk[:, :, chunk(c)], rw_a[:, :, :], ALU.mult)
                turn(dve.tensor_tensor(rw_k[:, :, :], rw_a[:, :, :], over(prm("k_a", 0, 4), P), ALU.mult))
                turn(dve.tensor_tensor(rw_k[:, :, :], rw_k[:, :, :], over(rw_one_ka, P), ALU.add))
                turn(dve.tensor_tensor(rw_k[:, :, :], rw_k[:, :, :], rw_p[:, 4:8, chunk(c)], ALU.mult))
                dve.wait_ge(rw_exp, n + 1)
                dve.tensor_tensor(rw_k[:, :, :], rw_k[:, :, :], grow[:, :, with_own], ALU.mult)
                dve.tensor_tensor(rw_b[:, :, :], rw_b[:, :, :], grow[:, :, with_own], ALU.mult)
                dve.scalar_tensor_tensor(out=rw_ar[:, :, 0, :], in0=rw_kk[:, :, chunk(c)], scalar=-1.0,
                                         in1=shrink[:, :, before], op0=ALU.mult, op1=ALU.mult)
                dve.tensor_tensor(rw_ar[:, :, 1, :], rw_p[:, 0:4, chunk(c)], shrink[:, :, with_own], ALU.mult)\
                   .then_inc(rw_prep, 1)
                mask, other = (C("mask_f"), C("mask_b")) if d == 0 else (C("mask_b"), C("mask_f"))
                merge, merge_t = (C("merge_f"), C("merge_b")) if d == 0 else (C("merge_b"), C("merge_f"))
                for k, dst in ((0, rw_mb), (1, rw_mk)):
                    for g in range(2):
                        dve.wait_ge(rw_mm[g], 3 * n + k + 1)
                        at = 2048 * g + 1024 * k
                        dve.tensor_tensor(dst[:, g, :, :, :].rearrange("p a b c -> p a (b c)"),
                                          grid(ps[:, at:at + 1024], 4, 256), each(mask, 4), ALU.mult)\
                           .then_inc(rw_masked[g], 1)
                for g in range(2):
                    dve.wait_ge(rw_mm[g], 3 * n + 3)
                    dve.tensor_tensor(rw_abt[:, g, :, :].rearrange("p (a b) c -> p a b c", a=2),
                                      grid(ps[:, 2048 * g:2048 * g + 1024], 2, 4, P)[:, :, 0:2, :],
                                      each(other[:, 0:P], 4).rearrange("p (a b) c -> p a b c", a=2), ALU.mult)\
                       .then_inc(rw_masked[g], 1)
                for g in range(2):
                    dve.wait_ge(rw_masked[g], 3 * n + 3)
                    dve.tensor_tensor(rw_t[:, g, :, :], rw_mb[:, g, :, 0, :], each(merge[:, 0:P], 4), ALU.mult)
                    turn(dve.tensor_tensor(rw_tt[:, g, :, :], rw_abt[:, g, :, :], each(merge_t[:, 0:P], 4), ALU.mult))
                    dve.tensor_tensor(rw_t[:, g, :, :], rw_t[:, g, :, :], each(C("ident"), 4), ALU.add)
                    dve.tensor_tensor(rw_tt[:, g, :, :], rw_tt[:, g, :, :], each(C("ident"), 4), ALU.add)\
                       .then_inc(rw_tr[g], 1)
                for lv in range(1, LEVELS):
                    for g in range(2):
                        dve.wait_ge(rw_qm[g], (LEVELS - 1) * n + lv)
                        dve.tensor_tensor(rw_q[:, g, :, :], grid(bank(4 * g), 4, P),
                                          each(merge[:, lv * P:(lv + 1) * P], 4), ALU.mult).then_inc(rw_qs[g], 1)
                    for g in range(2):
                        dve.wait_ge(rw_zm[g], (LEVELS - 1) * n + lv)
                        dve.wait_ge(rw_tr[g], LEVELS * n + lv)
                        dve.tensor_tensor(rw_t[:, g, :, :], rw_t[:, g, :, :], grid(bank(4 * g + 1), 4, P), ALU.add)\
                           .then_inc(rw_tr[g], 1)
                if n >= 2:
                    dve.wait_ge(rw_s_ready, n - 1)
                if i == 1:
                    dve.wait_ge(rw_first, 16 * (d + 1))
                S = rw_s[:, d, :, :]
                dve.tensor_tensor(S, S, grow[:, :, start:start + 1].to_broadcast([P, 4, HS]), ALU.mult)\
                   .then_inc(rw_s0, 1)
                dve.wait_ge(rw_y, n + 1)
                for odd in range(2):
                    lo = HS * odd
                    dst = mix[lo:lo + HS, 4:8, chunk(c)]
                    src = grid(bank(1 + odd), 4, P)[lo:lo + HS]
                    seen = [ORDER[e][j] for e, j in RW_BATCHES[:n]]
                    if c in seen:
                        last = dve.tensor_tensor(dst, dst, src, ALU.add)
                    else:
                        last = dve.tensor_copy(dst, src)
                last.then_inc(rw_y_added, 1)
                dve.wait_ge(rw_y_added, n + 1)
                dve.wait_ge(rw_sm, n + 1)
                turn(dve.tensor_tensor(S, S, grid(bank(4, 0, 256), 4, HS), ALU.add))
                dve.tensor_tensor(S, S, shrink[:, :, end:end + 1].to_broadcast([P, 4, HS]), ALU.mult)\
                   .then_inc(rw_s_ready, 1)
            vector_head_norm(dve, turn, 1, mix[:, 4:8, :], rw_tmp, HS, 64e-5, "ln_w")
            for b in range(4):
                dve.scalar_tensor_tensor(out=rw_p[:, b, :], in0=rw_p[:, b, :], scalar=prm("r_k", b),
                                         in1=rw_p[:, 4 + b, :], op0=ALU.mult, op1=ALU.mult).then_inc(rw_bonus, 1)
            for b in range(4):
                dve.wait_ge(rw_bsum, b + 1)
                turn(dve.tensor_tensor(rw_p[:, 8 + b, :], rw_p[:, 8 + b, :], pair(b)[2], ALU.mult))
                dve.scalar_tensor_tensor(out=mix[:, 4 + b, :], in0=mix[:, 4 + b, :], scalar=prm("ln_b", b),
                                         in1=rw_p[:, 8 + b, :], op0=ALU.add, op1=ALU.add).then_inc(rw_badd, 1)
            for b in range(4):
                dve.wait_ge(rw_g, b + 1)
                last = dve.tensor_tensor(mix[:, 4 + b, :], mix[:, 4 + b, :], pair(b)[2], ALU.mult)
            turn(last)
            dve.sem_inc(mix_ready, 4)

        la = Area(rest, mx.at)
        ml_p = la.take(MLSTM_BLOCKS, NT)
        ll, la = la, Area(w_mem)
        ml_v = la.take(NCH, 4, P + 1)
        ml_kn = la.take(NCH, 4, P)
        ml_b = la.take(NT)
        ml_top = la.take(NT)
        ml_share = la.take(NT)
        ml_floor = la.take(NT)
        ml_left = la.take(NT)
        ml_m = ll.take(NCH)
        ml_last = ll.take(NCH)
        ml_dec = ll.take(NCH)
        ml_mend = ll.take(1)
        ml_g = ll.take(2, NCH, HS)
        lv_ = Area(rest, mx.at + 8 * NT, mx.at + 12 * NT)
        ml_w = lv_.take(4, P)
        ml_sw = lv_.take(4, P)
        ml_q = lv_.take(4, P)
        ml_wk = lv_.take(4, P)
        ml_c = la.take(2, 4, P + 1)
        ml_decb = ll.take(4)
        ml_bd = rs[:, 0:4 * P].rearrange("p (a b) -> p a b", a=4)
        R = HS

        ml_fg = sem("ml_fg")
        ml_soft = sem("ml_soft")
        ml_rows = sem("ml_rows")
        ml_exps = sem("ml_exps")
        ml_kscaled = sem("ml_kscaled")
        ml_vt = sem("ml_vt")
        ml_kt = sem("ml_kt")
        ml_nat = sem("ml_nat")
        ml_gt = sem("ml_gt")
        ml_g_ready = sem("ml_g_ready")
        ml_mm = sem("ml_mm")
        ml_arg = sem("ml_arg")
        ml_w_ready = sem("ml_w_ready")
        ml_bd_ready = sem("ml_bd_ready")
        ml_fed = sem("ml_fed")
        ml_nd = sem("ml_nd")
        ml_abs = sem("ml_abs")
        ml_done = sem("ml_done")
        ml_zero = sem("ml_zero")
        ml_first = sem("ml_first")
        ml_sig = sem("ml_sig")

        def run(d, c):
            lo, hi = c * P, (c + 1) * P
            return slice(lo, hi) if d == 0 else slice(hi - 1, lo - 1 if lo else None, -1)

        def pool_mlstm(pool):
            pool.wait_ge(proj_ready, RET_BLOCKS + RWKV_BLOCKS + MLSTM_BLOCKS)
            for d in range(2):
                pool.memset(ml_c[:, d, :, :], 0.0).then_inc(ml_zero, 1)
            pool.memset(ml_v[:, :, :, P:P + 1], 1.0).then_inc(ml_zero, 1)
            for d in range(2):
                pool.wait_ge(ml_done, d + 1)
                pool.dma_start(outs["mc"][d], ml_c[:, d, :, :]).then_inc(saved, 16)
                pool.wait_ge(saved, 16 * (5 + d))
                pool.dma_start(ml_c[:, d, :, :], st["s_mc"][d]).then_inc(ml_first, 16)
            for d in range(2):
                pool.dma_start(outs["m"][d], ml_mend[32 * d:32 * d + 4, :]).then_inc(saved, 16)

        def tensor_mlstm(pe):
            pe.wait_ge(proj_ready, RET_BLOCKS + RWKV_BLOCKS + MLSTM_BLOCKS)
            pe.wait_ge(ml_kscaled, 1)
            for c in range(NCH):
                if c >= 2:
                    pe.wait_ge(ml_nat, 2 * (c - 1))
                for j, go in ((8, ml_vt), (4, ml_kt)):
                    for b in range(4):
                        ins = pe.transpose(bank((j == 4) * 2 + c % 2, b * P, b * P + P), ml_p[:, j + b, chunk(c)],
                                           C("ident"))
                    ins.then_inc(go, 1)
            pe.wait_ge(ml_exps, 1)
            for j, row in ((0, ml_p[:, 12, :]), (1, ml_left)):
                for c in range(NCH):
                    ins = pe.transpose(bank(4 + j, c * HS, c * HS + HS), row[0:R, chunk(c)], C("ident", R)[:, 0:R])
            ins.then_inc(ml_gt, 1)
            pe.wait_ge(ml_nat, 2 * NCH)
            pe.wait_ge(ml_g_ready, 1)
            for n, (d, i) in enumerate(RW_BATCHES):
                c = ORDER[d][i]
                if n:
                    pe.wait_ge(ml_done, n)
                for hd in range(4):
                    pe.matmul(bank(0, hd * P, hd * P + P), ml_p[:, 4 + hd, chunk(c)], ml_p[:, hd, chunk(c)],
                              start=True, stop=True)
                for hd in range(4):
                    r = 32 * d + hd
                    unit = C("ident", R)[:, r:r + 1].to_broadcast([R, P])
                    for b, row in ((1, ml_top), (2, ml_share), (3, ml_floor)):
                        pe.matmul(bank(b, hd * P, hd * P + P), unit, row[0:R, chunk(c)], start=True, stop=True)
                    ins = pe.matmul(bank(7, hd, hd + 1), unit, ml_dec[0:R, c:c + 1], start=True, stop=True)
                ins.then_inc(ml_mm, 1)
                pe.wait_ge(ml_fed, n + 1)
                for hd in range(4):
                    pe.matmul(bank(4, hd * P, hd * P + P), ml_v[:, c, hd, 0:P], ml_sw[:, hd, :],
                              start=True, stop=False)
                    pe.matmul(bank(4, hd * P, hd * P + P), ml_c[:, d, hd, 0:P], ml_q[:, hd, :],
                              start=False, stop=True)
                for hd in range(4):
                    pe.matmul(bank(5, hd * P, hd * P + P), C("ones"), ml_sw[:, hd, :], start=True, stop=False)
                    pe.matmul(bank(5, hd * P, hd * P + P), ml_c[:, d, hd, P:P + 1].to_broadcast([P, P]),
                              ml_q[:, hd, :], start=False, stop=True)
                for hd in range(4):
                    at = (P + 1) * (hd % 2)
                    ins = pe.matmul(bank(6 + hd // 2, at, at + P + 1), ml_wk[:, hd, :], ml_v[:, c, hd, :],
                                    start=True, stop=True)
                ins.then_inc(ml_nd, 1)
            pe.wait_ge(ml_done, NB)
            tensor_head_norm(pe, 2, mix[:, 0:4, :], C("ones"), ml_kn.rearrange("p a b c -> p (a b c)")
                             .rearrange("p (a b) -> p a b", a=4))
            pe.wait_ge(hn_ms, 12)

        def scalar_mlstm(act, turn):
            act.activation(ml_p[:, 4:8, :], ml_p[:, 4:8, :], ACT.Copy, scale=float(P) ** -0.5).then_inc(ml_kscaled, 1)
            act.wait_ge(ml_fg, 1)
            t = ml_left[0:R, :]
            turn(act.activation(t, ml_p[0:R, 13, :], ACT.Abs))
            turn(act.activation(t, t, ACT.Exp, scale=-1.0))
            act.activation(t, t, ACT.Ln, bias=1.0).then_inc(ml_soft, 1)
            for c in range(NCH):
                for j, (go, src) in enumerate(((ml_vt, ml_v[:, c, :, 0:P]), (ml_kt, ml_kn[:, c, :, :]))):
                    act.wait_ge(go, c + 1)
                    act.activation(src, grid(bank(2 * j + c % 2), 4, P), ACT.Copy).then_inc(ml_nat, 1)
            act.wait_ge(ml_rows, 1)
            for c in range(NCH):
                act.activation(ml_share[0:R, chunk(c)], ml_top[0:R, chunk(c)], ACT.Exp, scale=-1.0,
                               bias=ml_m[0:R, c:c + 1])
            act.activation(ml_floor[0:R, :], ml_floor[0:R, :], ACT.Exp, scale=-1.0)
            act.activation(ml_dec[0:R, :], ml_dec[0:R, :], ACT.Exp)
            act.activation(ml_left[0:R, :], ml_left[0:R, :], ACT.Exp).then_inc(ml_exps, 1)
            act.wait_ge(ml_gt, 1)
            for j in range(2):
                ins = act.activation(ml_g[:, j, :, :].rearrange("p a b -> p (a b)"), bank(4 + j, 0, NCH * HS), ACT.Copy)
            ins.then_inc(ml_g_ready, 1)
            for n in range(NB):
                act.wait_ge(ml_mm, n + 1)
                act.activation(ml_bd, grid(bank(3), 4, P), ACT.Copy).then_inc(ml_bd_ready, 1)
                act.wait_ge(ml_arg, n + 1)
                act.activation(ml_w[:, :, :], ml_w[:, :, :], ACT.Exp).then_inc(ml_w_ready, 1)
                act.wait_ge(ml_nd, n + 1)
                act.activation(ml_w[:, :, :], grid(bank(5), 4, P), ACT.Abs).then_inc(ml_abs, 1)
            act.activation(ml_p[:, 14:18, :], ml_p[:, 14:18, :], ACT.Sigmoid).then_inc(ml_sig, 1)
            scalar_head_norm(act, 2, mix[:, 0:4, :], ml_kn.rearrange("p a b c -> p (a b c)")
                             .rearrange("p (a b) -> p a b", a=4))

        def vector_mlstm(dve, turn):
            dve.wait_ge(proj_ready, RET_BLOCKS + RWKV_BLOCKS + MLSTM_BLOCKS)
            ig, fg = ml_p[0:R, 12, :], ml_p[0:R, 13, :]
            dve.tensor_scalar(fg, fg, prm("f_bias", rows=R), None, ALU.add).then_inc(ml_fg, 1)
            dve.tensor_scalar(ig, ig, prm("i_bias", rows=R), None, ALU.add)
            dve.memset(ml_b[0:R, :], 0.0)
            dve.memset(ml_top[0:R, :], 0.0)
            dve.memset(ml_last[0:R, :], 0.0)
            turn(dve.memset(ml_m[0:R, :], 0.0))
            for d in range(2):
                rows = slice(32 * d, 32 * d + 4)
                c = ORDER[d][1]
                dve.tensor_copy(ml_m[rows, c:c + 1], par[rows, pat["m_init"][0]:pat["m_init"][1]])
            dve.wait_ge(ml_soft, 1)
            turn(dve.scalar_tensor_tensor(out=fg, in0=fg, scalar=0.0, in1=ml_left[0:R, :], op0=ALU.min,
                                          op1=ALU.subtract))
            for d in range(2):
                rows = slice(32 * d, 32 * d + 4)
                for c in range(NCH):
                    last = dve.tensor_tensor_scan(ml_b[rows, run(d, c)], C("ones")[rows, :],
                                                  ml_p[rows, 13, run(d, c)], 0.0, ALU.mult, ALU.add)
            turn(last)
            turn(dve.tensor_tensor(ig, ig, ml_b[0:R, :], ALU.subtract))
            for i in range(NCH):
                for d in range(2):
                    rows, c = slice(32 * d, 32 * d + 4), ORDER[d][i]
                    g = ml_p[rows, 12, run(d, c)]
                    last = dve.tensor_tensor_scan(ml_top[rows, run(d, c)], g, g, ml_m[rows, c:c + 1],
                                                  ALU.max, ALU.max)
                turn(last)
                for d in range(2):
                    rows, c = slice(32 * d, 32 * d + 4), ORDER[d][i]
                    e = c * P + (P - 1 if d == 0 else 0)
                    last = dve.tensor_copy(ml_last[rows, c:c + 1], ml_top[rows, e:e + 1])
                    if i + 1 < NCH:
                        m = ml_mend[rows, :] if i == 0 else ml_m[rows, ORDER[d][i + 1]:ORDER[d][i + 1] + 1]
                        last = dve.tensor_tensor(m, ml_top[rows, e:e + 1], ml_b[rows, e:e + 1], ALU.add)
                turn(last)
            dve.tensor_tensor(ml_floor[0:R, :], ml_b[0:R, :], ml_top[0:R, :], ALU.add)
            dve.tensor_tensor(ml_dec[0:R, :], ml_m[0:R, :], ml_last[0:R, :], ALU.subtract)
            dve.tensor_tensor(grid(ml_left[0:R, :], NCH, P), grid(ig, NCH, P), over(ml_last[0:R, :], P),
                              ALU.subtract).then_inc(ml_rows, 1)
            dve.wait_ge(ml_g_ready, 1)
            dve.wait_ge(ml_zero, 3)
            for n, (d, i) in enumerate(RW_BATCHES):
                c = ORDER[d][i]
                col = slice(32 * d, 32 * d + 4)
                dve.wait_ge(ml_mm, n + 1)
                turn(dve.scalar_tensor_tensor(out=ml_w[:, :, :], in0=grid(bank(1), 4, P), scalar=-1.0,
                                              in1=over(ml_g[:, 0, c, col], P), op0=ALU.mult, op1=ALU.add))
                dve.scalar_tensor_tensor(out=ml_w[:, :, :], in0=ml_w[:, :, :], scalar=0.0,
                                         in1=each(C(("neg_f", "neg_b")[d]), 4), op0=ALU.min, op1=ALU.add)\
                   .then_inc(ml_arg, 1)
                dve.tensor_tensor(ml_q[:, :, :], ml_p[:, 0:4, chunk(c)], grid(bank(2), 4, P), ALU.mult)
                dve.tensor_tensor(ml_wk[:, :, :], ml_kn[:, c, :, :], over(ml_g[:, 1, c, col], P), ALU.mult)
                dve.tensor_copy(ml_decb[:, :], bank(7, 0, 4))
                if i == 1:
                    dve.wait_ge(ml_first, 16 * (d + 1))
                dve.wait_ge(ml_w_ready, n + 1)
                dve.tensor_tensor(ml_sw[:, :, :], ml_w[:, :, :], grid(bank(0), 4, P), ALU.mult).then_inc(ml_fed, 1)
                dve.wait_ge(ml_fed, n + 1)
                dve.wait_ge(ml_nd, n + 1)
                dve.wait_ge(ml_bd_ready, n + 1)
                dve.wait_ge(ml_abs, n + 1)
                turn(dve.tensor_tensor(ml_w[:, :, :], ml_w[:, :, :], ml_bd, ALU.max))
                turn(dve.reciprocal(ml_w[:, :, :], ml_w[:, :, :]))
                dst = mix[:, 0:4, chunk(c)]
                if c in [ORDER[e][j] for e, j in RW_BATCHES[:n]]:
                    turn(dve.tensor_tensor(ml_w[:, :, :], ml_w[:, :, :], grid(bank(4), 4, P), ALU.mult))
                    dve.tensor_tensor(dst, dst, ml_w[:, :, :], ALU.add)
                else:
                    dve.tensor_tensor(dst, ml_w[:, :, :], grid(bank(4), 4, P), ALU.mult)
                s = ml_c[:, d, :, :]
                turn(dve.tensor_tensor(s, s, over(ml_decb[:, :], P + 1), ALU.mult))
                s = s.rearrange("p (a b) c -> p a (b c)", a=2)
                dve.tensor_tensor(s, s, grid(ps[:, 3072:4096], 2, 512)[:, :, 0:2 * (P + 1)], ALU.add)\
                   .then_inc(ml_done, 1)
                dve.wait_ge(ml_done, n + 1)
            tmp = ml_kn.rearrange("p a b c -> p (a b c)").rearrange("p (a b) -> p a b", a=4)
            vector_head_norm(dve, turn, 2, mix[:, 0:4, :], tmp, P, 1e-5, "mn_w")
            dve.wait_ge(ml_sig, 1)
            turn(dve.tensor_tensor(mix[:, 0:4, :], mix[:, 0:4, :], ml_p[:, 14:18, :], ALU.mult))
            dve.sem_inc(mix_ready, 4)

        aa = Area(rest, mx.at)
        at_p = aa.take(ATT_BLOCKS, NT)
        aa = Area(w_mem)
        at_ck = aa.take(2, PAST)
        at_cv = aa.take(2 * HS)
        at_v = aa.take(NCH, 2 * HS)
        at_tmp = aa.take(6, NT)
        at_rope = aa.take(2, DEC_SEQ)
        at_e = aa.take(2, NT)
        at_t = aa.take(2, NT)
        at_stat = aa.take(2, 4)

        at_sq = sem("at_sq")
        at_ss = sem("at_ss")
        at_ms = sem("at_ms")
        at_root = sem("at_root")
        at_normed = sem("at_normed")
        at_turned = sem("at_turned")
        at_roped = sem("at_roped")
        at_vt = sem("at_vt")
        at_v_ready = sem("at_v_ready")
        at_cached = sem("at_cached")
        at_score = sem("at_score")
        at_max = sem("at_max")
        at_exp = sem("at_exp")
        at_prob = sem("at_prob")
        at_pt = sem("at_pt")
        at_pt_ready = sem("at_pt_ready")
        at_o = sem("at_o")
        at_out = sem("at_out")
        AT_UNITS = [(c, hd) for c in range(NCH) for hd in range(8)]
        NU = len(AT_UNITS)

        def key_pair(s):
            at = 1024 * s + 384
            return ps[:, at:at + P], ps[:, at + P:at + NT], ps[:, at:at + NT]

        def keys_of(c):
            return 1 if c == 0 else NCH

        def pool_attention(pool):
            pool.wait_ge(proj_ready, RET_BLOCKS + RWKV_BLOCKS + MLSTM_BLOCKS + ATT_BLOCKS)
            pool.dma_start(at_ck[:, :, :], st["s_ck"]).then_inc(at_cached, 16)
            pool.dma_start(grid(at_cv, 2, HS), st["s_cv"]).then_inc(at_cached, 16)
            pool.wait_ge(at_normed, 6)
            for g in range(2):
                pool.dma_start(outs["ck"][g], at_p[0:HS, 4 + g, PROMPT]).then_inc(saved, 16)
            pool.wait_ge(at_v_ready, 1)
            pool.dma_start(outs["cv"], at_v[:, 0, :]).then_inc(saved, 16)

        def tensor_attention(pe):
            pe.wait_ge(proj_ready, RET_BLOCKS + RWKV_BLOCKS + MLSTM_BLOCKS + ATT_BLOCKS)
            for b in range(6):
                pe.wait_ge(at_sq, b + 1)
                if b >= 3:
                    pe.wait_ge(at_ms, b - 2)
                left, right, _ = pair(b % 3)
                pe.matmul(left, C("ones64"), at_tmp[:, b, LEFT], start=True, stop=True)
                pe.matmul(right, C("ones64"), at_tmp[:, b, RIGHT], start=True, stop=True).then_inc(at_ss, 1)
            for c in range(NCH):
                ins = pe.transpose(bank(6 + c // 4, c % 4 * P, c % 4 * P + P), at_p[:, 6, chunk(c)], C("ident"))
            ins.then_inc(at_vt, 1)
            pe.wait_ge(at_ms, 6)
            for b in range(6):
                pe.wait_ge(at_normed, b + 1)
                pe.matmul(bank(b), C("turn"), at_p[:, b, SAMPLE], start=True, stop=True).then_inc(at_turned, 1)
            pe.wait_ge(at_roped, 6)
            pe.wait_ge(at_v_ready, 1)
            pe.wait_ge(at_cached, 32)

            def scores(n):
                c, hd = AT_UNITS[n]
                lo, g = HS * (hd % 2), hd // 4
                pr, sa, _ = key_pair(n % 2)
                q = at_p[lo:lo + HS, hd // 2, chunk(c)]
                if n >= 2:
                    pe.wait_ge(at_exp, n - 1)
                if c == 0:
                    pe.matmul(pr, q, at_p[lo:lo + HS, 4 + g, PROMPT], start=True, stop=True).then_inc(at_score, 1)
                else:
                    pe.matmul(pr, q, at_ck[lo:lo + HS, g, :], start=True, stop=True)
                    pe.matmul(sa, q, at_p[lo:lo + HS, 4 + g, SAMPLE], start=True, stop=True).then_inc(at_score, 1)

            def turned(n):
                c, hd = AT_UNITS[n]
                pe.wait_ge(at_prob, n + 1)
                if n >= 1:
                    pe.wait_ge(at_pt_ready, n)
                for j in range(keys_of(c)):
                    ins = pe.transpose(key_pair(2)[2][:, j * P:(j + 1) * P], at_e[:, n % 2, j * P:(j + 1) * P], C("ident"))
                ins.then_inc(at_pt, 1)

            def values(n):
                c, hd = AT_UNITS[n]
                lo, g = HS * (hd % 2), hd // 4
                pe.wait_ge(at_pt_ready, n + 1)
                if n >= 2:
                    pe.wait_ge(at_out, n - 1)
                nk = keys_of(c)
                for j in range(nk):
                    v = at_cv[:, g * HS:(g + 1) * HS] if c and j == 0 else at_v[:, j, g * HS:(g + 1) * HS]
                    ins = pe.matmul(bank(6 + n % 2, 0, P)[lo:lo + HS], v, at_t[:, n % 2, j * P:(j + 1) * P],
                                    start=(j == 0), stop=(j == nk - 1))
                ins.then_inc(at_o, 1)

            for n in range(NU + 2):
                if n < NU:
                    scores(n)
                if 1 <= n <= NU:
                    turned(n - 1)
                if n >= 2:
                    values(n - 2)

        def scalar_attention(act, turn):
            for b in range(6):
                act.activation(at_tmp[:, b, :], at_p[:, b, :], ACT.Square).then_inc(at_sq, 1)
            act.wait_ge(at_vt, 1)
            act.activation(at_v[:, 0:4, :].rearrange("p a b -> p (a b)"), bank(6), ACT.Copy)
            act.activation(at_v[:, 4, :], bank(7, 0, P), ACT.Copy).then_inc(at_v_ready, 1)
            for b in range(6):
                act.wait_ge(at_ms, b + 1)
                act.activation(at_tmp[:, b, :], at_tmp[:, b, :], ACT.Sqrt).then_inc(at_root, 1)
            for n in range(NU + 2):
                if n < NU:
                    c, hd = AT_UNITS[n]
                    w = keys_of(c) * P
                    act.wait_ge(at_max, n + 1)
                    if n >= 2:
                        act.wait_ge(at_pt, n - 1)
                    act.activation(at_e[:, n % 2, 0:w], key_pair(n % 2)[2][:, 0:w], ACT.Exp, scale=HS ** -0.5,
                                   bias=at_stat[:, n % 2, 1:2], accum_out=at_stat[:, n % 2, 2:3]).then_inc(at_exp, 1)
                if 1 <= n <= NU:
                    c, hd = AT_UNITS[n - 1]
                    w = keys_of(c) * P
                    act.wait_ge(at_pt, n)
                    if n >= 3:
                        act.wait_ge(at_o, n - 2)
                    act.activation(at_t[:, (n - 1) % 2, 0:w], key_pair(2)[2][:, 0:w], ACT.Copy).then_inc(at_pt_ready, 1)
                if n >= 2:
                    c, hd = AT_UNITS[n - 2]
                    lo = HS * (hd % 2)
                    act.wait_ge(at_o, n - 1)
                    act.activation(mix[lo:lo + HS, 4 + hd // 2, chunk(c)], bank(6 + n % 2, 0, P)[lo:lo + HS],
                                   ACT.Copy).then_inc(at_out, 1)

        def vector_attention(dve, turn):
            for b in range(6):
                dve.wait_ge(at_ss, b + 1)
                dve.tensor_scalar(at_tmp[:, b, :], pair(b % 3)[2], 1.0 / HS, EPS, ALU.mult, ALU.add)\
                   .then_inc(at_ms, 1)
            for b in range(6):
                dve.wait_ge(at_root, b + 1)
                turn(dve.reciprocal(at_tmp[:, b, :], at_tmp[:, b, :]))
                dve.scalar_tensor_tensor(out=at_p[:, b, :], in0=at_p[:, b, :],
                                         scalar=prm("q_gain" if b < 4 else "k_gain"), in1=at_tmp[:, b, :],
                                         op0=ALU.mult, op1=ALU.mult).then_inc(at_normed, 1)
            dve.wait_ge(at_normed, 6)
            for b in range(6):
                rope(dve, turn, at_p[:, b, SAMPLE], bank(b), at_rope[:, b % 2, :], at_turned, b + 1, at_roped)
            for n in range(NU + 1):
                if n < NU:
                    c, hd = AT_UNITS[n]
                    dve.wait_ge(at_score, n + 1)
                    turn(dve.tensor_reduce(at_stat[:, n % 2, 0:1], key_pair(n % 2)[2][:, 0:keys_of(c) * P], AX.X, ALU.max))
                    dve.tensor_scalar(at_stat[:, n % 2, 1:2], at_stat[:, n % 2, 0:1], -HS ** -0.5, None, ALU.mult)\
                       .then_inc(at_max, 1)
                if n >= 1:
                    m = n - 1
                    c, hd = AT_UNITS[m]
                    w = keys_of(c) * P
                    dve.wait_ge(at_exp, m + 1)
                    turn(dve.reciprocal(at_stat[:, m % 2, 3:4], at_stat[:, m % 2, 2:3]))
                    dve.tensor_scalar(at_e[:, m % 2, 0:w], at_e[:, m % 2, 0:w], at_stat[:, m % 2, 3:4], None,
                                      ALU.mult).then_inc(at_prob, 1)
            dve.wait_ge(at_out, NU)
            dve.wait_ge(saved, 16 * 11)
            dve.sem_inc(mix_ready, 4)


        block = ctx.enter_context(nc.Block())

        @block.sync
        def _(sp):
            sp.dma_start(par[:, :], params_in).then_inc(par_loaded, 16)

            def stream(src, n0, n, cols):
                def one(i, u):
                    at = src[i * RING + u]
                    sp.wait_ge(split_ready, i * RING + n0 + u + 1)
                    r = (n0 + u) % RING
                    sp.dma_start(ring[:, r, 0:cols], at).then_inc(land[r], 16)
                looped(sp, n, one)

            for layer in range(DEPTH):
                for name, blocks, k in stages_of_layer(layer):
                    if name in ("rwkv", "att", "out"):
                        sp.wait_ge(mix_ready, 4 * (1 + (name == "out")) + 8 * layer)
                        if name != "out":
                            sp.wait_ge(saved, 16 * (2 if layer == 0 else 8))
                    if k:
                        stream(w[layer][name], tile0[layer, name], blocks, k * P)
            sp.wait_ge(y_ready, DB)
            sp.dma_start(outs["y"], y).then_inc(stored, 16)
            sp.wait_ge(stored, 16)


        @block.tensor
        def _(pe):
            pe.sem_inc(tiles_done, SPLITS)

            def pairs_read(layer, name):
                pe.wait_ge(free_dve, free0[layer, name]["dve"])
                pe.wait_ge(free_act, free0[layer, name]["act"])

            def linear(layer, name, n, k_blocks, hi, lo, last_k=None):
                b0, n0 = blk0[layer, name], tile0[layer, name]
                pairs_read(layer, name)
                reader, f0 = (free_act, free0[layer, name]["act"]) if name in PROJECTIONS else \
                             (free_dve, free0[layer, name]["dve"])

                def one(i, u):
                    left, right, _ = pair((b0 + u) % SETS)
                    s = (n0 + u) % SPLITS
                    pe.wait_ge(reader, i * 4 + f0 + u + 1 - SETS)
                    pe.wait_ge(split_ready, i * 4 + RING + n0 + u + 1)
                    for k in range(k_blocks):
                        if last_k is not None and k == k_blocks - 1:
                            pe.wait_ge(gated_ready, last_k)
                        w_h, w_l = w_hi[:, s, k * P:(k + 1) * P], w_lo[:, s, k * P:(k + 1) * P]
                        first, last = k == 0, k == k_blocks - 1
                        for weights, acts in ((w_h, hi), (w_h, lo), (w_l, hi)):
                            start, stop = first and weights is w_h and acts is hi, last and weights is w_l
                            pe.matmul(left, weights, acts[:, k, LEFT], start=start, stop=stop)
                            mm = pe.matmul(right, weights, acts[:, k, RIGHT], start=start, stop=stop)
                    mm.then_inc(tiles_done, 1)
                looped(pe, n, one)

            def ada(layer):
                n0 = tile0[layer, "ada"]
                pairs_read(layer, "ada")
                pe.wait_ge(cond_ready, 1)

                def group(i, u):
                    pe.wait_ge(ada_row_ready, i * 4 + N_MOD * layer + u + 1)
                    for k in range(DB):
                        n = n0 + u * DB + k
                        r = n % RING
                        pe.wait_ge(land[r], i * (4 * DB // RING * 16) + 16 * (n // RING + 1))
                        for half in range(2):
                            at = u % 2 * D_MODEL + half * 512
                            mm = pe.matmul(ps[0:2, at:at + 512], scond[:, k, :],
                                           ring[:, r, half * 512:(half + 1) * 512],
                                           start=(k == 0), stop=(k == DB - 1))
                        mm.then_inc(tiles_done, 1)
                looped(pe, N_MOD, group)
                pe.wait_ge(ada_row_ready, N_MOD * (layer + 1) + 2)
                pe.wait_ge(loaded, 48)

                for b in range(N_MOD * DB):
                    ins = pe.transpose(bank(4, 2 * b, 2 * b + 2), ada_row[:, b * P:(b + 1) * P], C("ident", 2)[:, 0:2])
                ins.then_inc(ada_turned, 1)

            norms = [0]

            def norm(layer, name):
                left, right, _ = pair(blk0[layer, name] % SETS)
                pairs_read(layer, name)
                for k in range(DB):
                    pe.wait_ge(sq_ready, norms[0] * DB + k + 1)
                    pe.matmul(left, C("ones"), squares(name)[:, k, LEFT], start=(k == 0), stop=(k == DB - 1))
                    mm = pe.matmul(right, C("ones"), squares(name)[:, k, RIGHT], start=(k == 0), stop=(k == DB - 1))
                mm.then_inc(norm_ready, 1)
                norms[0] += 1

            halves = 0
            for layer in range(DEPTH):
                ada(layer)
                for j in range(3):
                    norm(layer, f"norm{j}")
                    pe.wait_ge(h_ready, DB * norms[0])
                    if j != 1:
                        for half in "ab":
                            linear(layer, f"up{j // 2}{half}", 2 * HALF_F, DB, h_hi, h_lo)
                            halves += 1
                            pe.wait_ge(gated_ready, HALF_F * halves + 1)
                            linear(layer, f"down{j // 2}{half}", DB, HALF_F, g_hi, g_lo, HALF_F * halves + 2)
                    elif layer == 0:
                        linear(layer, "ret", RET_BLOCKS, DB, h_hi, h_lo)
                        tensor_retention(pe)
                        linear(layer, "rwkv", RWKV_BLOCKS, DB, h_hi, h_lo)
                        tensor_rwkv(pe)
                    else:
                        linear(layer, "mlstm", MLSTM_BLOCKS, DB, h_hi, h_lo)
                        tensor_mlstm(pe)
                        linear(layer, "att", ATT_BLOCKS, DB, h_hi, h_lo)
                        tensor_attention(pe)
                    if j == 1:
                        pe.wait_ge(mix_split, DB * (layer + 1))
                        linear(layer, "out", DB, DB, h_hi, h_lo)
            norm(DEPTH, "norm")


        @block.scalar
        def _(act):
            turn = Order(act, act_chain)
            act.wait_ge(par_loaded, 16)
            act.activation(scond[:, :, :], grid(prm("cond", 0, 2 * DB), DB, 2), ACT.Silu).then_inc(cond_ready, 1)
            act.sem_inc(ada_row_ready, 2)
            act.sem_inc(free_act, SETS)

            norms, fblocks, projected = [0], [0], [0]

            def parts(layer, name):
                for n in parts_first(act, tile0[layer, name]):
                    high_part(act, n)

            def only_parts(layer, name, n):
                n0 = tile0[layer, name]
                parts(layer, name)

                def one(i, u, split_ahead):
                    act.wait_ge(tiles_done, i * 4 + SPLITS + n0 + u + 1)
                    split_ahead()
                stepped(act, n0, n, high_part, one)

            def ada(layer):
                n0 = tile0[layer, "ada"]

                def row(i, u):
                    act.wait_ge(tiles_done, i * 4 * DB + SPLITS + n0 + (u + 1) * DB)
                    act.activation(ada_row[:, bass.ds(i * 4 * D_MODEL + u * D_MODEL, D_MODEL)],
                                   ps[0:2, u % 2 * D_MODEL:(u % 2 + 1) * D_MODEL], ACT.Copy)\
                       .then_inc(ada_row_ready, 1)
                looped(act, N_MOD, row)
                act.sem_inc(high_ready, N_MOD * DB)
                parts(layer, "up0a")

            def norm(layer, name, shift):
                q = norms[0]
                for k in range(DB):
                    if q:
                        act.wait_ge(x_ready, x0[layer, name] - DB + k + 1)
                    act.activation(squares(name)[:, k, :], x[:, k, :], ACT.Square).then_inc(sq_ready, 1)
                act.wait_ge(ms_ready, q + 1)
                act.activation(rs[:, :], rs[:, :], ACT.Sqrt).then_inc(root_ready, 1)
                if shift is not None:
                    for k in range(DB):
                        act.wait_ge(scaled, DB * q + k + 1)
                        act.activation(h_hi[:, k, PROMPT], normed[:, k % 2, PROMPT], ACT.Identity,
                                       bias=mod[:, shift * DB + k, 0:1])
                        act.activation(h_hi[:, k, SAMPLE], normed[:, k % 2, SAMPLE], ACT.Identity,
                                       bias=mod[:, shift * DB + k, 1:2]).then_inc(h_high, 1)
                norms[0] += 1

            def up(layer, name):
                b0, n0, g0 = blk0[layer, name], tile0[layer, name], fblocks[0]

                def one(i, u, split_ahead):
                    act.wait_ge(tiles_done, i * 4 + SPLITS + n0 + u + 1)
                    split_ahead()
                    f = u // 2
                    if u % 2 == 0:
                        act.activation(silu[:, f % 2, :], pair((b0 + u) % SETS)[2], ACT.Silu).then_inc(silu_ready, 1)
                    else:
                        act.wait_ge(prod_ready, i * 2 + g0 + f + 1)
                        act.activation(g_hi[:, i * 2 + f, :], prod[:, f % 2, :], ACT.Copy).then_inc(g_high, 1)
                stepped(act, n0, 2 * HALF_F, high_part, one)
                fblocks[0] += HALF_F

            def project(layer, name, n, dst):
                b0, n0, p0 = blk0[layer, name], tile0[layer, name], projected[0]
                parts(layer, name)

                def one(i, u, split_ahead):
                    act.wait_ge(tiles_done, i * 4 + SPLITS + n0 + u + 1)
                    split_ahead()
                    act.activation(dst[:, i * 4 + u, :], pair((b0 + u) % SETS)[2], ACT.Copy)\
                       .then_inc(proj_ready, 1)
                    act.wait_ge(proj_ready, i * 4 + p0 + u + 1)
                    act.sem_inc(free_act, 1)
                stepped(act, n0, n, high_part, one)
                projected[0] += n

            for layer in range(DEPTH):
                ada(layer)
                act.wait_ge(loaded, 48)
                act.wait_ge(mod_ready, layer + 1)
                for j in range(3):
                    norm(layer, f"norm{j}", 3 * j)
                    if j != 1:
                        for half in "ab":
                            up(layer, f"up{j // 2}{half}")
                            only_parts(layer, f"down{j // 2}{half}", DB)
                        continue
                    if layer == 0:
                        project(layer, "ret", RET_BLOCKS, rt_p)
                        scalar_retention(act, turn)
                        act.wait_ge(mix_ready, 4)
                        act.wait_ge(saved, 32)
                        project(layer, "rwkv", RWKV_BLOCKS, rw_p)
                        scalar_rwkv(act, turn)
                    else:
                        project(layer, "mlstm", MLSTM_BLOCKS, ml_p)
                        scalar_mlstm(act, turn)
                        act.wait_ge(mix_ready, 12)
                        act.wait_ge(saved, 16 * 8)
                        project(layer, "att", ATT_BLOCKS, at_p)
                        scalar_attention(act, turn)
                    act.wait_ge(mix_ready, 8 * (layer + 1))
                    for k in range(DB):
                        act.activation(h_hi[:, k, :], mix[:, k, :], ACT.Copy).then_inc(mix_high, 1)
                    only_parts(layer, "out", DB)
            norm(DEPTH, "norm", None)


        @block.vector
        def _(dve):
            turn = Order(dve, dve_chain)
            dve.sem_inc(free_dve, SETS)
            dve.sem_inc(gated_ready, 2)
            dve.sem_inc(split_ready, RING)

            norms, fblocks = [0], [0]

            def parts(layer, name):
                for n in parts_first(dve, tile0[layer, name]):
                    low_part(dve, n)

            def only_parts(layer, name, n, then=None):
                parts(layer, name)

                def one(i, u, split_ahead):
                    split_ahead()
                    if then is not None:
                        then(i, u)
                stepped(dve, tile0[layer, name], n, low_part, one)

            def modulation(layer):
                def free(i, u):
                    dve.wait_ge(tiles_done, i * 4 + SPLITS + tile0[layer, "ada"] + u + 1)
                    dve.sem_inc(split_ready, 1)
                looped(dve, N_MOD * DB, free)
                parts(layer, "up0a")
                dve.wait_ge(ada_turned, layer + 1)
                dve.wait_ge(par_loaded, 16)
                dve.wait_ge(loaded, 48)
                src = grid(bank(4, 0, 2 * N_MOD * DB), N_MOD * DB, 2)
                turn(dve.tensor_tensor(mod[:, :, :], src, over(prm("ada_b", layer * N_MOD * DB, N_MOD * DB), 2),
                                       ALU.add))
                dve.sem_inc(free_dve, 1)
                for g in (2, 8):
                    m = mod[:, g * DB:(g + 1) * DB, :]
                    turn(dve.tensor_scalar(m, m, 0.5, None, ALU.mult))
                for j in range(3):
                    last = dve.scalar_tensor_tensor(out=gs[:, j, :, :], in0=mod[:, (3 * j + 1) * DB:(3 * j + 2) * DB, :],
                                                    scalar=1.0, in1=over(prm("norm_g", (3 * layer + j) * DB, DB), 2),
                                                    op0=ALU.add, op1=ALU.mult)
                turn(last)
                dve.sem_inc(mod_ready, 1)

            def norm(layer, name, j):
                q = norms[0]
                dve.wait_ge(norm_ready, q + 1)
                dve.tensor_scalar(rs[:, :], pair(blk0[layer, name] % SETS)[2], 1.0 / D_MODEL, EPS, ALU.mult, ALU.add)\
                   .then_inc(ms_ready, 1)
                dve.wait_ge(root_ready, q + 1)
                dve.sem_inc(free_dve, 1)
                turn(dve.reciprocal(rs[:, :], rs[:, :]))

                def low(k):
                    dve.wait_ge(h_high, DB * q + k + 1)
                    for part, cond in ((PROMPT, 0), (SAMPLE, 1)):
                        shift = mod[:, 3 * j * DB + k, cond:cond + 1]
                        ins = dve.scalar_tensor_tensor(out=h_lo[:, k, part], in0=normed[:, k % 2, part], scalar=shift,
                                                       in1=h_hi[:, k, part].bitcast(F32),
                                                       op0=ALU.add, op1=ALU.subtract)
                    ins.then_inc(h_ready, 1)

                for k in range(DB):
                    if j is None:
                        dve.scalar_tensor_tensor(out=y[:, k, :], in0=x[:, k, :], scalar=prm("final", k),
                                                 in1=rs[:, :], op0=ALU.mult, op1=ALU.mult).then_inc(y_ready, 1)
                        continue
                    if k >= 2:
                        dve.wait_ge(h_ready, DB * q + k - 1)
                    for part, cond in ((PROMPT, 0), (SAMPLE, 1)):
                        ins = dve.scalar_tensor_tensor(out=normed[:, k % 2, part], in0=x[:, k, part],
                                                       scalar=gs[:, j, k, cond:cond + 1], in1=rs[:, part],
                                                       op0=ALU.mult, op1=ALU.mult)
                    ins.then_inc(scaled, 1)
                    if k:
                        low(k - 1)
                if j is not None:
                    low(DB - 1)
                norms[0] += 1

            def up(layer, name):
                b0, n0, g0 = blk0[layer, name], tile0[layer, name], fblocks[0]

                def one(i, u, split_ahead):
                    dve.wait_ge(tiles_done, i * 4 + SPLITS + n0 + u + 1)
                    split_ahead()
                    f = u // 2
                    if u % 2:
                        dve.wait_ge(silu_ready, i * 2 + g0 + f + 1)
                        dve.wait_ge(gated_ready, i * 2 + g0 + f + 1)
                        dve.tensor_tensor(prod[:, f % 2, :], silu[:, f % 2, :], pair((b0 + u) % SETS)[2], ALU.mult)\
                           .then_inc(prod_ready, 1)
                        dve.wait_ge(g_high, i * 2 + g0 + f + 1)
                        dve.sem_inc(free_dve, 2)
                        dve.tensor_tensor(g_lo[:, i * 2 + f, :], prod[:, f % 2, :],
                                          g_hi[:, i * 2 + f, :].bitcast(F32), ALU.subtract).then_inc(gated_ready, 1)
                stepped(dve, n0, 2 * HALF_F, low_part, one)
                fblocks[0] += HALF_F

            def residual(layer, name, gate):
                b0, n0, xn = blk0[layer, name], tile0[layer, name], x0[layer, name]
                parts(layer, name)

                def one(i, u, split_ahead):
                    dve.wait_ge(tiles_done, i * 4 + SPLITS + n0 + u + 1)
                    split_ahead()
                    src = pair((b0 + u) % SETS)[2]
                    for part, cond in ((PROMPT, 0), (SAMPLE, 1)):
                        xb = x[:, i * 4 + u, part]
                        ins = dve.scalar_tensor_tensor(out=xb, in0=src[:, part],
                                                       scalar=mod[:, i * 4 + (gate * DB + u), cond:cond + 1],
                                                       in1=xb, op0=ALU.mult, op1=ALU.add)
                    ins.then_inc(x_ready, 1)
                    dve.wait_ge(x_ready, i * 4 + xn + u + 1)
                    dve.sem_inc(free_dve, 1)
                stepped(dve, n0, DB, low_part, one)

            for layer in range(DEPTH):
                modulation(layer)
                for j in range(3):
                    norm(layer, f"norm{j}", j)
                    if j != 1:
                        for half in "ab":
                            up(layer, f"up{j // 2}{half}")
                            residual(layer, f"down{j // 2}{half}", 2 + 3 * j)
                        continue
                    if layer == 0:
                        only_parts(layer, "ret", RET_BLOCKS)
                        vector_retention(dve, turn)
                        only_parts(layer, "rwkv", RWKV_BLOCKS, lambda i, u: vector_shift(dve, i, u))
                        vector_rwkv(dve, turn)
                    else:
                        only_parts(layer, "mlstm", MLSTM_BLOCKS)
                        vector_mlstm(dve, turn)
                        only_parts(layer, "att", ATT_BLOCKS)
                        vector_attention(dve, turn)
                    for k in range(DB):
                        dve.wait_ge(mix_high, DB * layer + k + 1)
                        dve.tensor_tensor(h_lo[:, k, :], mix[:, k, :], h_hi[:, k, :].bitcast(F32), ALU.subtract)\
                           .then_inc(mix_split, 1)
                    residual(layer, "out", 5)
            norm(DEPTH, "norm", None)


        @block.gpsimd
        def _(pool):
            pool.dma_start(cst[:, :], consts_in).then_inc(loaded, 16)
            pool.dma_start(x[:, :, :], x_in).then_inc(loaded, 16)
            pool.dma_start(lora[:, :, :], lora_in).then_inc(loaded, 16)
            pool_retention(pool)
            pool_rwkv(pool)
            pool_mlstm(pool)
            pool_attention(pool)
            pool.wait_ge(saved, 16 * 11)



def _tiles(a, k):
    r, c = a.shape
    t = a.reshape(r // (k * P), k, P, c // P, P).transpose(3, 0, 2, 1, 4)
    return np.ascontiguousarray(t.reshape(-1, P, k * P))


def _cols(v):
    return np.ascontiguousarray(v).reshape(-1, P).T


def kernel(**inputs):
    import concourse.bacc as _bacc
    from concourse.bass_utils import run_bass_kernel_spmd as _run

    v = {k: np.asarray(a) for k, a in inputs.items()}
    f = np.float32
    arrays = {}
    tok = np.concatenate([v["x_prompt"][0], v["x_sample"][0]], 0)
    arrays["x_in"] = np.ascontiguousarray(tok.T.reshape(DB, P, NT).transpose(1, 0, 2))
    at, table = const_layout()
    arrays["consts"] = table

    for layer in range(DEPTH):
        arrays[f"w{layer}_ada"] = np.ascontiguousarray(
            v["ada_w"][layer].reshape(DB, P, N_MOD, D_MODEL).transpose(2, 0, 1, 3).reshape(-1, P, D_MODEL))
        for j in range(2):
            w1 = v["ffn_w1"][layer, j].reshape(D_MODEL, 2, FB, P).transpose(0, 2, 1, 3).reshape(D_MODEL, -1)
            for half in range(2):
                cols = slice(half * 2 * HALF_F * P, (half + 1) * 2 * HALF_F * P)
                arrays[f"w{layer}_up{j}{'ab'[half]}"] = _tiles(w1[:, cols], DB)
            for half in range(2):
                rows_ = slice(half * HALF_F * P, (half + 1) * HALF_F * P)
                arrays[f"w{layer}_down{j}{'ab'[half]}"] = _tiles(v["ffn_w2"][layer, j][rows_], HALF_F)
    even, odd = v["w_in_even"][0], v["w_in_odd"][0]
    arrays["w0_ret"] = _tiles(even[:, :RET_BLOCKS * P], DB)
    arrays["w0_rwkv"] = _tiles(even[:, RET_BLOCKS * P:], DB)
    arrays["w0_out"] = _tiles(v["w_out_even"][0], DB)
    gates = np.zeros((2, D_MODEL, P), f)
    for g in range(2):
        for d in range(2):
            gates[g, :, 32 * d:32 * d + 4] = odd[:, 1536 + 8 * g + 4 * d:1536 + 8 * g + 4 * d + 4]
    arrays["w1_mlstm"] = _tiles(np.concatenate([odd[:, :1536], gates[0], gates[1], odd[:, 1552:2064]], 1), DB)
    q, k0, k1, vv = odd[:, 2064:2576], odd[:, 2576:2640], odd[:, 2640:2704], odd[:, 2704:2832]
    arrays["w1_att"] = _tiles(np.concatenate([q, k0, k0, k1, k1, vv], 1), DB)
    arrays["w1_out"] = _tiles(v["w_out_odd"][0], DB)

    pat, npar = param_layout()
    par = np.zeros((P, npar), f)

    def put(name, a):
        par[:a.shape[0], pat[name][0]:pat[name][0] + a.shape[1]] = a

    def rows(a):
        r = np.zeros((P, 1), f)
        r[0:4, 0], r[32:36, 0] = a[0], a[1]
        return r

    for name, key in (("norm_g", "norm_g"), ("final", "final_norm"), ("ada_b", "ada_b"), ("gn_w", "ret_gn_w"),
                      ("mu", "rwkv_mu"), ("w0", "rwkv_w0"), ("a0", "rwkv_a0"), ("k_k", "rwkv_k_k"),
                      ("k_a", "rwkv_k_a"), ("r_k", "rwkv_r_k"), ("ln_w", "rwkv_ln_w"), ("ln_b", "rwkv_ln_b"),
                      ("mn_w", "mlstm_norm_w")):
        put(name, _cols(v[key]))
    put("q_gain", np.tile(v["attn_qk_norm"][0, 0], 2)[:, None])
    put("k_gain", np.tile(v["attn_qk_norm"][0, 1], 2)[:, None])
    lg = v["ret_log_decay"][0]
    put("lg_head", np.tile(lg.reshape(1, 8), (P, 1)))
    put("lg_part", np.repeat(lg.reshape(2, 2, 2), HS, axis=2).reshape(4, P).T)
    put("m_init", rows(v["state_mlstm_m"][0, 0]))
    put("i_bias", rows(v["mlstm_i_bias"][0]))
    put("f_bias", rows(v["mlstm_f_bias"][0]))
    cond = np.stack([v["c_ctx"], v["c"][0]], 1)
    put("cond", cond.reshape(DB, P, 2).transpose(1, 0, 2).reshape(P, 2 * DB))
    arrays["params"] = par
    lora = np.zeros((P, 3, 512), f)
    for d in range(2):
        lora[:HS, d], lora[HS:, d] = v["rwkv_w2"][0, d], v["rwkv_a2"][0, d]
    lora[:, 2] = v["rwkv_g2"][0]
    arrays["lora_in"] = lora

    arrays["s_ret"] = v["state_ret"][0, 0].reshape(2, 2, P, P).transpose(0, 2, 1, 3)
    arrays["s_rwkv"] = v["state_rwkv"][0, 0].transpose(0, 1, 3, 2).reshape(2, 4, P, HS).transpose(0, 2, 1, 3)
    arrays["s_mc"] = np.concatenate([v["state_mlstm_c"][0, 0], v["state_mlstm_n"][0, 0][..., None]], -1)\
        .transpose(0, 2, 1, 3)
    ck = v["cache_k"][0, 0].transpose(2, 0, 1)
    arrays["s_ck"] = np.concatenate([ck, ck], 0)
    arrays["s_cv"] = v["cache_v"][0, 0].transpose(1, 0, 2)

    nc = _bacc.Bacc("TRN2", target_bir_lowering=False, num_devices=1)
    arrays = {k: np.ascontiguousarray(a) for k, a in arrays.items()}
    ap = {k: nc.dram_tensor(k, a.shape, F32, kind="ExternalInput").ap() for k, a in arrays.items()}
    shapes = {"y": (P, DB, NT), "ret": (2, P, 2, P), "rwkv": (2, P, 4, HS), "mc": (2, P, 4, P + 1),
              "m": (2, 4, 1), "ck": (2, HS, P), "cv": (P, P)}
    outs = {k: nc.dram_tensor(f"out_{k}", s, F32, kind="ExternalOutput").ap() for k, s in shapes.items()}
    w = [{n: ap[f"w{layer}_{n}"] for n, _, k in stages_of_layer(layer) if k} for layer in range(DEPTH)]
    st = {k: ap[k] for k in ("s_ret", "s_rwkv", "s_mc", "s_ck", "s_cv")}
    build(nc, w, ap["x_in"], ap["consts"], ap["params"], ap["lora_in"], st, outs)
    r = _run(nc, [arrays], core_ids=[0]).results[0]
    y = r["out_y"].transpose(2, 1, 0).reshape(NT, D_MODEL)
    ret = r["out_ret"].transpose(0, 2, 1, 3).reshape(1, 1, 2, 4, HS, P)
    rwkv = r["out_rwkv"].transpose(0, 2, 1, 3).reshape(2, 8, HS, HS).transpose(0, 1, 3, 2)[None, None]
    mc = r["out_mc"].transpose(0, 2, 1, 3)
    out = (y[None, :SEQ], y[None, SEQ:], ret, rwkv, mc[None, None, ..., :P], mc[None, None, ..., P],
           r["out_m"].reshape(1, 1, 2, 4), r["out_ck"].transpose(0, 2, 1)[None, None],
           r["out_cv"].reshape(P, 2, HS).transpose(1, 0, 2)[None, None])
    return tuple(np.ascontiguousarray(a) for a in out)
```

```python
from contextlib import ExitStack

import numpy as np
import concourse.bass as bass
from concourse import mybir

F32 = mybir.dt.float32
F32R = mybir.dt.float32r
ALU = mybir.AluOpType
ACT = mybir.ActivationFunctionType
AX = mybir.AxisListType

P = 128
D_MODEL, D_FF, N_MOD, DEPTH = 1024, 2816, 9, 2
SEQ, DEC_SEQ, PAST = 128, 512, 128
NT = SEQ + DEC_SEQ
NCH = NT // P
DB = D_MODEL // P
FB = D_FF // P
HALF_F = FB // 2
RING = 4
REST = 18560
SPLITS = 2
SETS = 4
EPS = 1e-6
GRID_W, ROPE_BASE = 64, 10000.0
HS = 64
LEVELS = 7
DECAY_MAX = float(np.exp(-0.5))

PROMPT = slice(0, SEQ)
SAMPLE = slice(SEQ, NT)
LEFT = slice(0, NT // 2)
RIGHT = slice(NT // 2, NT)

PROJECTIONS = ("ret", "rwkv", "mlstm", "att")
RET_BLOCKS, RWKV_BLOCKS = 12, 14
MLSTM_BLOCKS, ATT_BLOCKS = 18, 7


def const_layout():
    r = np.arange(P)
    row, col = r[:, None], r[None, :]
    parts = {
        "ident": (row == col),
        "ones": np.ones((P, P)),
        "ones64": (row // HS == col // HS),
        "mask_f": np.concatenate([row < col, row <= col], 1),
        "mask_b": np.concatenate([row > col, row >= col], 1),
    }
    lv = []
    for b in (1 << n for n in range(LEVELS)):
        same = row // (2 * b) == col // (2 * b)
        lv.append(same & (row % (2 * b) < b) & (col % (2 * b) >= b))
    parts["merge_f"] = np.concatenate(lv, 1)
    parts["merge_b"] = np.concatenate([m.T for m in lv], 1)
    perm = np.zeros((P, P))
    for m in range(P):
        if m % 32 < 16:
            perm[m + 16, m] = -1.0
        else:
            perm[m - 16, m] = 1.0
    parts["turn"] = perm
    nf = HS // 4
    inv = (np.float32(ROPE_BASE) ** (-np.arange(nf, dtype=np.float32) / np.float32(nf))).astype(np.float32)
    t = np.arange(DEC_SEQ)
    pos = np.where((r % HS < HS // 2)[:, None], (t // GRID_W)[None, :], (t % GRID_W)[None, :]).astype(np.float32)
    ang = pos * inv[r % nf][:, None]
    parts["cos"] = np.cos(ang)
    parts["sin"] = np.sin(ang)
    parts["ahead"] = np.maximum(col - row, 0)
    parts["behind"] = np.maximum(row - col, 0)
    parts["from1"] = np.broadcast_to(col + 1, (P, P))
    parts["to1"] = np.broadcast_to(P - col, (P, P))
    parts["left_f"] = (P - 1) - row
    parts["left_b"] = row
    parts["neg_f"] = np.where(row <= col, 0.0, -1e30)
    parts["neg_b"] = np.where(row >= col, 0.0, -1e30)
    at, cols = {}, 0
    for k, v in parts.items():
        at[k] = (cols, cols + v.shape[1])
        cols += v.shape[1]
    return at, np.concatenate([np.asarray(v, np.float32) for v in parts.values()], 1)


PARAM_COLS = [("norm_g", DEPTH * 3 * DB), ("final", DB), ("ada_b", DEPTH * N_MOD * DB), ("gn_w", 4), ("mu", 14),
              ("w0", 8), ("a0", 8), ("k_k", 4), ("k_a", 4), ("r_k", 4), ("ln_w", 4), ("ln_b", 4), ("mn_w", 4),
              ("q_gain", 1), ("k_gain", 1), ("lg_head", 8), ("lg_part", 4), ("m_init", 1), ("i_bias", 1),
              ("f_bias", 1), ("cond", 2 * DB)]


def param_layout():
    at, cols = {}, 0
    for k, n in PARAM_COLS:
        at[k] = (cols, cols + n)
        cols += n
    return at, cols


def stages_of_layer(layer):
    mixers = [("ret", RET_BLOCKS, DB), ("rwkv", RWKV_BLOCKS, DB)] if layer == 0 else \
             [("mlstm", MLSTM_BLOCKS, DB), ("att", ATT_BLOCKS, DB)]

    def ffn(j):
        return [(f"{what}{j}{half}", n, k) for half in "ab" for what, n, k in (("up", 2 * HALF_F, DB), ("down", DB, HALF_F))]

    return [("ada", N_MOD * DB, DB), ("norm0", 1, 0)] + ffn(0) + [("norm1", 1, 0)] + mixers + \
           [("out", DB, DB), ("norm2", 1, 0)] + ffn(1)


def build(nc, w, x_in, consts_in, params_in, lora_in, st, outs):
    cat, _ = const_layout()
    pat, npar = param_layout()

    tile0, blk0, free0, x0, tile_cols = {}, {}, {}, {}, []
    tiles = blks = xs = 0
    freed = {"dve": SETS, "act": SETS}
    for layer in range(DEPTH):
        for name, blocks, k in stages_of_layer(layer):
            tile0[layer, name], blk0[layer, name], x0[layer, name] = tiles, blks, xs
            free0[layer, name] = dict(freed)
            freed["act" if name in PROJECTIONS else "dve"] += 1 if name == "ada" else blocks
            if k:
                tiles += blocks
                tile_cols += [k * P] * blocks
            blks += 1 if name == "ada" else blocks
            xs += blocks if name == "out" or name.startswith("down") else 0
    blk0[DEPTH, "norm"], free0[DEPTH, "norm"], x0[DEPTH, "norm"] = blks, dict(freed), xs
    held = {tile0[0, "rwkv"], tile0[0, "out"], tile0[1, "att"], tile0[1, "out"]}
    held |= {tile0[layer, name] for layer in range(DEPTH) for name in ("ada", "up0a")}

    with ExitStack() as ctx:
        def sb(name, shape):
            return ctx.enter_context(nc.sbuf_tensor(name, shape, F32))

        def rounded(name, shape):
            return ctx.enter_context(nc.sbuf_tensor(name, shape, F32R))

        def shared(name, floats):
            with nc.sbuf_tensor(name, [P, floats], F32) as t:
                return t

        def sem(name):
            return ctx.enter_context(nc.semaphore(name))

        cst = sb("cst", [P, max(b for _, b in cat.values())])
        par = sb("par", [P, npar])
        x = sb("x", [P, DB, NT])
        lora = sb("lora", [P, 3, 512])
        mod = sb("mod", [P, N_MOD * DB, 2])
        gs = sb("gs", [P, 3, DB, 2])
        scond = sb("scond", [P, DB, 2])
        rs = sb("rs", [P, NT])

        h_mem = shared("h_mem", 2 * DB * NT)
        h_hi = rounded("h_hi", [P, DB, NT])
        h_lo = rounded("h_lo", [P, DB, NT])
        y = h_mem[:, 0:DB * NT].rearrange("p (a b) -> p a b", a=DB)
        ada_row = h_mem[0:2, 0:N_MOD * D_MODEL]
        TILE = HALF_F * P
        w_mem = shared("w_mem", (RING + 2 * SPLITS) * TILE)
        ring = sb("ring", [P, RING, TILE])
        w_hi = rounded("w_hi", [P, SPLITS, TILE])
        w_lo = rounded("w_lo", [P, SPLITS, TILE])
        rest = shared("rest", REST)
        g_hi = rounded("g_hi", [P, HALF_F, NT])
        g_lo = rounded("g_lo", [P, HALF_F, NT])
        silu = sb("silu", [P, 2, NT])
        prod = sb("prod", [P, 2, NT])
        normed = sb("normed", [P, 2, NT])
        sb("spare", [P, REST - (2 * HALF_F + 6) * NT])
        ps = ctx.enter_context(nc.psum_tensor("ps", [P, 8 * 512], F32))

        def C(name, rows=P):
            a, b = cat[name]
            return cst[0:rows, a:b]

        def prm(name, i=0, n=1, rows=P):
            a, _ = pat[name]
            return par[0:rows, a + i:a + i + n]

        def over(ap, n):
            return ap.unsqueeze(2).to_broadcast([ap.shape[0], ap.shape[1], n])

        def each(ap, n):
            return ap.unsqueeze(1).to_broadcast([ap.shape[0], n, ap.shape[1]])

        def pair(s):
            at = 1024 * s + 512
            return ps[:, at - NT // 2:at], ps[:, at:at + NT // 2], ps[:, at - NT // 2:at + NT // 2]

        def bank(b, lo=0, hi=512):
            return ps[:, 512 * b + lo:512 * b + hi]

        def grid(ap, *dims):
            names = "abcde"[:len(dims)]
            return ap.rearrange(f"p ({' '.join(names)}) -> p {' '.join(names)}",
                                **{k: d for k, d in zip(names[1:], dims[1:])})

        class Area:

            def __init__(self, mem, at=0, end=None):
                self.mem, self.at, self.end = mem, at, mem.shape[1] if end is None else end

            def take(self, *dims):
                n = int(np.prod(dims))
                v = self.mem[:, self.at:self.at + n]
                self.at += n
                assert self.at <= self.end, self.at
                return grid(v, *dims) if len(dims) > 1 else v

        def chunk(c):
            return slice(c * P, (c + 1) * P)

        ORDER = ([0, 1, 2, 3, 4], [0, 4, 3, 2, 1])

        par_loaded = sem("par_loaded")
        loaded = sem("loaded")
        land = [sem(f"land{r}") for r in range(RING)]
        high_ready = sem("high_ready")
        split_ready = sem("split_ready")
        tiles_done = sem("tiles_done")
        norm_ready = sem("norm_ready")
        free_dve = sem("free_dve")
        free_act = sem("free_act")
        silu_ready = sem("silu_ready")
        prod_ready = sem("prod_ready")
        g_high = sem("g_high")
        gated_ready = sem("gated_ready")
        mix_high = sem("mix_high")
        mix_split = sem("mix_split")
        cond_ready = sem("cond_ready")
        ada_row_ready = sem("ada_row_ready")
        ada_turned = sem("ada_turned")
        mod_ready = sem("mod_ready")
        x_ready = sem("x_ready")
        sq_ready = sem("sq_ready")
        ms_ready = sem("ms_ready")
        root_ready = sem("root_ready")
        scaled = sem("scaled")
        h_high = sem("h_high")
        h_ready = sem("h_ready")
        proj_ready = sem("proj_ready")
        mix_ready = sem("mix_ready")
        y_ready = sem("y_ready")
        stored = sem("stored")
        dve_chain = sem("dve_chain")
        act_chain = sem("act_chain")
        pool_chain = sem("pool_chain")

        class Order:

            def __init__(self, eng, s):
                self.eng, self.s, self.n = eng, s, 0

            def __call__(self, ins):
                self.n += 1
                ins.then_inc(self.s, 1)
                self.eng.wait_ge(self.s, self.n)

        def parts_first(eng, n):
            return range(n, n + SPLITS) if n in held else ()

        def high_part(act, n, i=0):
            r, cols = n % RING, tile_cols[n]
            act.wait_ge(land[r], i * 16 + 16 * (n // RING + 1))
            act.wait_ge(tiles_done, i * 4 + n + 1)
            act.activation(w_hi[:, n % SPLITS, 0:cols], ring[:, r, 0:cols], ACT.Copy).then_inc(high_ready, 1)

        def low_part(dve, n, i=0):
            r, cols = n % RING, tile_cols[n]
            dve.wait_ge(high_ready, i * 4 + n + 1)
            dve.tensor_tensor(w_lo[:, n % SPLITS, 0:cols], ring[:, r, 0:cols],
                              w_hi[:, n % SPLITS, 0:cols].bitcast(F32), ALU.subtract).then_inc(split_ready, 1)

        def stepped(eng, n0, n, part, body):
            def ahead(i, u):
                if n0 + u + SPLITS < tiles and not held & {n0 + u + 1, n0 + u + SPLITS}:
                    part(eng, n0 + u + SPLITS, i)
            m = (n - SPLITS) // 4
            if m > 1:
                with eng.Fori(0, m) as i:
                    for u in range(4):
                        body(i, u, lambda: part(eng, n0 + u + SPLITS, i))
            else:
                m = 0
            for t in range(4 * m, n):
                body(t // 4, t % 4, lambda: ahead(0, t))

        def looped(eng, n, body):
            if n // 4 > 1:
                with eng.Fori(0, n // 4) as i:
                    for u in range(4):
                        body(i, u)
            elif n // 4:
                for u in range(4):
                    body(0, u)
            for u in range(n % 4):
                body(n // 4, u)

        mx = Area(rest)
        mix = mx.take(DB, NT)

        def squares(name):
            return mix if name == "norm2" else y

        saved = sem("saved")
        first = sem("first")

        hn_mean = sem("hn_mean")
        hn_cent = sem("hn_cent")
        hn_sq = sem("hn_sq")
        hn_var = sem("hn_var")
        hn_ms = sem("hn_ms")
        hn_root = sem("hn_root")

        def tensor_head_norm(pe, q, src, table, tmp):
            for stage, go, done in ((src, None, hn_mean), (tmp, hn_sq, hn_var)):
                for b in range(4):
                    if go is not None:
                        pe.wait_ge(go, 4 * q + b + 1)
                    pr, sa, _ = pair(b)
                    pe.matmul(pr, table, stage[:, b, LEFT], start=True, stop=True)
                    pe.matmul(sa, table, stage[:, b, RIGHT], start=True, stop=True).then_inc(done, 1)

        def scalar_head_norm(act, turn, q, src, tmp):
            for b in range(4):
                act.wait_ge(hn_cent, 4 * q + b + 1)
                act.activation(tmp[:, b, :], src[:, b, :], ACT.Square).then_inc(hn_sq, 1)
            for b in range(4):
                act.wait_ge(hn_ms, 4 * q + b + 1)
                last = act.activation(tmp[:, b, :], tmp[:, b, :], ACT.Ln)
            turn(last)
            for b in range(4):
                act.activation(tmp[:, b, :], tmp[:, b, :], ACT.Exp, scale=-0.5).then_inc(hn_root, 1)

        def vector_head_norm(dve, turn, q, src, tmp, n, eps, weight):
            for b in range(4):
                dve.wait_ge(hn_mean, 4 * q + b + 1)
                dve.scalar_tensor_tensor(out=src[:, b, :], in0=pair(b)[2], scalar=-1.0 / n, in1=src[:, b, :],
                                         op0=ALU.mult, op1=ALU.add).then_inc(hn_cent, 1)
            for b in range(4):
                dve.wait_ge(hn_var, 4 * q + b + 1)
                dve.tensor_scalar(tmp[:, b, :], pair(b)[2], 1.0 / n, eps, ALU.mult, ALU.add).then_inc(hn_ms, 1)
            for b in range(4):
                dve.wait_ge(hn_root, 4 * q + b + 1)
                last = dve.scalar_tensor_tensor(out=src[:, b, :], in0=src[:, b, :], scalar=prm(weight, b),
                                                in1=tmp[:, b, :], op0=ALU.mult, op1=ALU.mult)
            turn(last)

        ra = Area(rest, mx.at)
        rt_p = ra.take(RET_BLOCKS, NT)
        rl, ra = ra, Area(w_mem)
        rt_v = ra.take(NCH, 512)
        rt_k = ra.take(2, NCH, 256)
        rt_decay = ra.take(4, P)
        rt_back = rl.take(4, P)
        rt_qdec = rl.take(4, P)
        rt_q = rl.take(2, 4, P)
        rt_att = rl.take(2, 4, P)
        rt_s = ra.take(2, NCH, 2, P)
        rt_end = ra.take(2, 2, P)
        rt_kdec = rl.take(8)
        rt_cdec = rl.take(4)
        rt_rope = rl.take(2, DEC_SEQ)

        rt_tab = sem("rt_tab")
        rt_turned = sem("rt_turned")
        rt_roped = sem("rt_roped")
        rt_vt = sem("rt_vt")
        rt_v_ready = sem("rt_v_ready")
        rt_kt = sem("rt_kt")
        rt_k_ready = sem("rt_k_ready")
        rt_zero = sem("rt_zero")
        rt_upd = sem("rt_upd")
        rt_state = sem("rt_state")
        rt_qs = sem("rt_qs")
        rt_score = sem("rt_score")
        rt_weighed = sem("rt_weighed")
        rt_o = sem("rt_o")
        rt_out = sem("rt_out")
        rt_silu = sem("rt_silu")
        RT_UPD = [(d, i) for d in range(2) for i in range(NCH - 1)]

        def pool_retention(pool):
            pool.wait_ge(proj_ready, RET_BLOCKS)
            for d in range(2):
                pool.memset(rt_s[:, d, 0, :, :], 0.0).then_inc(rt_zero, 1)
                pool.dma_start(rt_s[:, d, ORDER[d][1], :, :], st["s_ret"][d]).then_inc(first, 16)
            for d in range(2):
                pool.wait_ge(rt_state, (NCH - 1) * d + 1)
                pool.dma_start(outs["ret"][d], rt_end[:, d, :, :]).then_inc(saved, 16)

        def tensor_retention(pe):
            pe.wait_ge(proj_ready, RET_BLOCKS)
            for b in range(4):
                pe.matmul(bank(b), C("turn"), rt_p[:, b, SAMPLE], start=True, stop=True).then_inc(rt_turned, 1)
            for c in range(NCH):
                if c >= 2:
                    pe.wait_ge(rt_v_ready, c - 1)
                for b in range(4):
                    ins = pe.transpose(bank(4 + c % 2, b * P, b * P + P), rt_p[:, 4 + b, chunk(c)], C("ident"))
                ins.then_inc(rt_vt, 1)
            pe.wait_ge(rt_roped, 4)
            for c in range(NCH):
                if c >= 2:
                    pe.wait_ge(rt_k_ready, c - 1)
                for b in range(2):
                    ins = pe.transpose(bank(6 + c % 2, b * P, b * P + P), rt_p[:, 2 + b, chunk(c)], C("ident"))
                ins.then_inc(rt_kt, 1)
            pe.wait_ge(rt_v_ready, NCH)
            pe.wait_ge(rt_k_ready, NCH)
            for n, (d, i) in enumerate(RT_UPD):
                c = ORDER[d][i]
                for hd in range(4):
                    lo, b = HS * (hd % 2), hd // 2
                    ins = pe.matmul(bank(n, b * P, b * P + P)[lo:lo + HS], rt_k[:, d, c, hd * HS:hd * HS + HS],
                                    rt_v[:, c, hd * P:hd * P + P], start=True, stop=True)
                ins.then_inc(rt_upd, 1)
            pe.wait_ge(rt_state, 2 * (NCH - 1))
            pe.wait_ge(first, 32)
            pe.wait_ge(rt_zero, 2)

            def scores(c):
                if c >= 2:
                    pe.wait_ge(rt_weighed, c - 1)
                for hd in range(4):
                    lo, b = HS * (hd % 2), hd // 2
                    ins = pe.matmul(bank(4 * (c % 2) + hd % 2, b * P, b * P + P), rt_p[lo:lo + HS, 2 + b, chunk(c)],
                                    rt_p[lo:lo + HS, b, chunk(c)], start=True, stop=True)
                ins.then_inc(rt_score, 1)

            def output(c):
                if c >= 2:
                    pe.wait_ge(rt_out, c - 1)
                pe.wait_ge(rt_weighed, c + 1)
                pe.wait_ge(rt_qs, c + 1)
                for hd in (0, 2, 1, 3):
                    lo, b = HS * (hd % 2), hd // 2
                    out = bank(4 * (c % 2) + 2 + hd % 2, b * P, b * P + P)
                    pe.matmul(out, rt_v[:, c, hd * P:hd * P + P], rt_att[:, c % 2, 2 * (hd % 2) + b, :],
                              start=True, stop=False)
                    for d in range(2):
                        ins = pe.matmul(out, rt_s[lo:lo + HS, d, c, b, :], rt_q[lo:lo + HS, c % 2, 2 * d + b, :],
                                        start=False, stop=(d == 1))
                ins.then_inc(rt_o, 1)

            scores(0)
            for c in range(NCH):
                if c + 1 < NCH:
                    scores(c + 1)
                output(c)
            pe.wait_ge(rt_out, NCH)
            tensor_head_norm(pe, 0, mix[:, 0:4, :], C("ones"), rt_v.rearrange("p a b -> p (a b)")
                             .rearrange("p (a b) -> p a b", a=4))
            pe.wait_ge(hn_ms, 4)

        def scalar_retention(act, turn):
            for d, table in ((0, rt_decay), (1, rt_back)):
                for hd in range(4):
                    act.activation(table[:, 2 * (hd % 2) + hd // 2, :], C(("ahead", "behind")[d]), ACT.Exp,
                                   scale=prm("lg_head", 4 * d + hd))
                for b in range(2):
                    act.activation(rt_qdec[:, 2 * d + b, :], C(("from1", "to1")[d]), ACT.Exp,
                                   scale=prm("lg_part", 2 * d + b))
                act.activation(rt_kdec[:, 4 * d:4 * d + 4], prm("lg_head", 4 * d, 4), ACT.Exp,
                               scale=C(("left_f", "left_b")[d]))
            act.activation(rt_cdec[:, :], prm("lg_part", 0, 4), ACT.Exp, scale=float(P)).then_inc(rt_tab, 1)
            for c in range(NCH):
                act.wait_ge(rt_vt, c + 1)
                act.activation(rt_v[:, c, :], bank(4 + c % 2), ACT.Copy).then_inc(rt_v_ready, 1)
            act.activation(rt_p[:, 8:12, :], rt_p[:, 8:12, :], ACT.Silu).then_inc(rt_silu, 1)
            for c in range(NCH):
                act.wait_ge(rt_o, c + 1)
                for q in range(2):
                    ins = act.activation(mix[:, q:4:2, chunk(c)], grid(bank(4 * (c % 2) + 2 + q, 0, 256), 2, P), ACT.Copy)
                ins.then_inc(rt_out, 1)
            scalar_head_norm(act, turn, 0, mix[:, 0:4, :], rt_v.rearrange("p a b -> p (a b)")
                             .rearrange("p (a b) -> p a b", a=4))

        def vector_retention(dve, turn):
            dve.wait_ge(rt_tab, 1)
            turn(dve.tensor_scalar(rt_kdec[:, :], rt_kdec[:, :], HS ** -0.5, None, ALU.mult))
            dve.tensor_tensor(rt_decay[:, :, :], rt_decay[:, :, :], each(C("mask_f")[:, P:2 * P], 4), ALU.mult)
            turn(dve.tensor_tensor(rt_back[:, :, :], rt_back[:, :, :], each(C("mask_b")[:, P:2 * P], 4), ALU.mult))
            turn(dve.tensor_tensor(rt_decay[:, :, :], rt_decay[:, :, :], rt_back[:, :, :], ALU.add))
            turn(dve.tensor_scalar(rt_decay[:, :, :], rt_decay[:, :, :], HS ** -0.5, None, ALU.mult))
            for b in range(4):
                rope(dve, turn, rt_p[:, b, SAMPLE], bank(b), rt_rope[:, b % 2, :], rt_turned, b + 1, rt_roped)
            for c in range(NCH):
                dve.wait_ge(rt_kt, c + 1)
                for d in range(2):
                    ins = dve.tensor_tensor(grid(rt_k[:, d, c, :], 4, HS), grid(bank(6 + c % 2, 0, 256), 4, HS),
                                            over(rt_kdec[:, 4 * d:4 * d + 4], HS), ALU.mult)
                ins.then_inc(rt_k_ready, 1)
            dve.wait_ge(rt_zero, 2)
            dve.wait_ge(first, 32)
            for n, (d, i) in enumerate(RT_UPD):
                dve.wait_ge(rt_upd, n + 1)
                old = rt_s[:, d, ORDER[d][i], :, :]
                new = rt_end[:, d, :, :] if i == 0 else rt_s[:, d, ORDER[d][i + 1], :, :]
                for b in range(2):
                    ins = dve.scalar_tensor_tensor(out=new[:, b, :], in0=old[:, b, :],
                                                   scalar=rt_cdec[:, 2 * d + b:2 * d + b + 1],
                                                   in1=bank(n, b * P, b * P + P), op0=ALU.mult, op1=ALU.add)
                ins.then_inc(rt_state, 1)
                dve.wait_ge(rt_state, n + 1)
            for c in range(NCH):
                dve.wait_ge(rt_score, c + 1)
                if c >= 2:
                    dve.wait_ge(rt_o, c - 1)
                two = grid(ps[:, 2048 * (c % 2):2048 * (c % 2) + 1024], 2, 512)[:, :, 0:256]
                dve.tensor_tensor(grid(rt_att[:, c % 2, :, :].rearrange("p a b -> p (a b)"), 2, 256), two,
                                  grid(rt_decay[:, :, :].rearrange("p a b -> p (a b)"), 2, 256), ALU.mult)\
                   .then_inc(rt_weighed, 1)
                for d in range(2):
                    ins = dve.tensor_tensor(rt_q[:, c % 2, 2 * d:2 * d + 2, :], rt_p[:, 0:2, chunk(c)],
                                            rt_qdec[:, 2 * d:2 * d + 2, :], ALU.mult)
                ins.then_inc(rt_qs, 1)
            tmp = rt_v.rearrange("p a b -> p (a b)").rearrange("p (a b) -> p a b", a=4)
            vector_head_norm(dve, turn, 0, mix[:, 0:4, :], tmp, P, 1e-5, "gn_w")
            dve.wait_ge(rt_silu, 1)
            turn(dve.tensor_tensor(mix[:, 0:4, :], mix[:, 0:4, :], rt_p[:, 8:12, :], ALU.mult))
            dve.sem_inc(mix_ready, 4)

        def rope(dve, turn, v, turned, tmp, go, count, done):
            dve.wait_ge(go, count)
            dve.tensor_tensor(tmp, turned, C("sin"), ALU.mult)
            turn(dve.tensor_tensor(v, v, C("cos"), ALU.mult))
            dve.tensor_tensor(v, v, tmp, ALU.add).then_inc(done, 1)
            dve.wait_ge(done, count)

        wa = Area(rest, mx.at)
        rw_p = wa.take(RWKV_BLOCKS, NT)
        shifted = wa.take(2, NT)
        wl = wa
        wa, wh = Area(w_mem), Area(h_mem)
        rw_kk = wh.take(4, NT)
        rw_v = wh.take(NCH, 512)
        rw_w = wa.take(4, P)
        rw_f = wa.take(4, P + 1)
        rw_up = wa.take(4, P + 1)
        rw_dn = wa.take(4, P + 1)
        rw_a = wa.take(4, P)
        rw_k = wa.take(2, 4, P)
        rw_b = wa.take(2, 4, P)
        rw_ar = wa.take(2, 4, 2, P)
        rw_edge = wa.take(2, 2, 4)
        rw_bn = wa.take(4, P)
        rw_kn = wa.take(4, P)
        rw_mb = wh.take(2, 4, 2, P)
        rw_mk = wh.take(2, 4, 2, P)
        rw_abt = wh.take(2, 4, P)
        rw_t = wa.take(2, 4, P)
        rw_tt = wa.take(2, 4, P)
        rw_q = wa.take(2, 4, P)
        rw_r = wl.take(8, HS)
        rw_u = wl.take(8, HS)
        rw_s = wl.take(2, 4, HS)
        rw_tmp = Area(w_mem).take(4, NT)
        rw_ktmp = Area(h_mem, 4 * NT + NCH * 512).take(4, NT)
        rw_one_ka = rs[:, 0:4]
        rw_neg_ka = rs[:, 4:8]

        rw_shift = sem("rw_shift")
        rw_near = sem("rw_near")
        rw_tanh = sem("rw_tanh")
        rw_kraw = sem("rw_kraw")
        rw_ksq = sem("rw_ksq")
        rw_ksum = sem("rw_ksum")
        rw_kguard = sem("rw_kguard")
        rw_kroot = sem("rw_kroot")
        rw_kk_ready = sem("rw_kk_ready")
        rw_vt = sem("rw_vt")
        rw_v_ready = sem("rw_v_ready")
        rw_lora = sem("rw_lora")
        rw_z = sem("rw_z")
        rw_th = sem("rw_th")
        rw_sum = sem("rw_sum")
        rw_exp = sem("rw_exp")
        rw_prep = sem("rw_prep")
        rw_mm = [sem(f"rw_mm{g}") for g in range(2)]
        rw_masked = [sem(f"rw_masked{g}") for g in range(2)]
        rw_tr = [sem(f"rw_tr{g}") for g in range(2)]
        rw_qm = [sem(f"rw_qm{g}") for g in range(2)]
        rw_qs = [sem(f"rw_qs{g}") for g in range(2)]
        rw_zm = [sem(f"rw_zm{g}") for g in range(2)]
        rw_tp = [sem(f"rw_tp{g}") for g in range(2)]
        rw_tt_ready = [sem(f"rw_tt_ready{g}") for g in range(2)]
        rw_natp = sem("rw_natp")
        rw_nat = sem("rw_nat")
        rw_s0 = sem("rw_s0")
        rw_rm = sem("rw_rm")
        rw_r_ready = sem("rw_r_ready")
        rw_um = sem("rw_um")
        rw_u_ready = sem("rw_u_ready")
        rw_y = sem("rw_y")
        rw_y_added = sem("rw_y_added")
        rw_sm = sem("rw_sm")
        rw_s_ready = sem("rw_s_ready")
        rw_zero = sem("rw_zero")
        rw_first = sem("rw_first")
        rw_bonus = sem("rw_bonus")
        rw_bsum = sem("rw_bsum")
        rw_badd = sem("rw_badd")
        rw_g = sem("rw_g")

        RW_BATCHES = [(d, i) for i in range(NCH) for d in range(2)]
        NB = len(RW_BATCHES)

        def where(hd):
            b, odd = hd // 2, hd % 2
            return b, HS * odd, b // 2, 2 * odd + b % 2

        def pool_rwkv(pool):
            turn = Order(pool, pool_chain)
            pool.wait_ge(proj_ready, RET_BLOCKS + RWKV_BLOCKS)
            for d in range(2):
                pool.memset(rw_s[:, d, :, :], 0.0).then_inc(rw_zero, 1)
            for n, (d, i) in enumerate(RW_BATCHES):
                c, p = ORDER[d][i], n % 2
                grow, shrink = (rw_dn, rw_up) if d == 0 else (rw_up, rw_dn)
                with_own = slice(1, P + 1) if d == 0 else slice(0, P)
                before = slice(0, P) if d == 0 else slice(1, P + 1)
                start, end = (0, P) if d == 0 else (P, 0)
                pool.wait_ge(rw_th, 2 * n + 2)
                if n >= 2:
                    pool.wait_ge(rw_s_ready, n - 1)
                turn(pool.tensor_scalar(rw_a[:, :, :], rw_a[:, :, :], -0.5, -0.5, ALU.mult, ALU.add))
                turn(pool.tensor_tensor(rw_k[:, p, :, :], rw_a[:, :, :], over(rw_neg_ka, P), ALU.mult))
                turn(pool.tensor_tensor(rw_k[:, p, :, :], rw_k[:, p, :, :], over(rw_one_ka, P), ALU.add))
                turn(pool.tensor_tensor(rw_k[:, p, :, :], rw_k[:, p, :, :], rw_p[:, 4:8, chunk(c)], ALU.mult))
                pool.wait_ge(rw_kk_ready, 4)
                turn(pool.tensor_tensor(rw_b[:, p, :, :], rw_kk[:, :, chunk(c)], rw_a[:, :, :], ALU.mult))
                pool.wait_ge(rw_exp, n + 1)
                pool.tensor_copy(rw_edge[:, p, 0, :], grow[:, :, start])
                pool.tensor_copy(rw_edge[:, p, 1, :], shrink[:, :, end])
                pool.tensor_tensor(rw_b[:, p, :, :], rw_b[:, p, :, :], grow[:, :, with_own], ALU.mult)
                pool.tensor_tensor(rw_ar[:, p, :, 0, :], rw_kk[:, :, chunk(c)], shrink[:, :, before], ALU.mult)
                pool.tensor_tensor(rw_ar[:, p, :, 1, :], rw_p[:, 0:4, chunk(c)], shrink[:, :, with_own], ALU.mult)
                pool.tensor_tensor(rw_k[:, p, :, :], rw_k[:, p, :, :], grow[:, :, with_own], ALU.mult)\
                    .then_inc(rw_prep, 1)
                if n in (1, 2):
                    e = n - 1
                    pool.wait_ge(rw_s_ready, e + 1)
                    pool.dma_start(outs["rwkv"][e], rw_s[:, e, :, :]).then_inc(saved, 16)
                    pool.wait_ge(saved, 16 * (e + 3))
                    pool.dma_start(rw_s[:, e, :, :], st["s_rwkv"][e]).then_inc(rw_first, 16)

        def tensor_rwkv(pe):
            def low_rank(n):
                d, i = RW_BATCHES[n]
                c = ORDER[d][i]
                if n:
                    for g in range(2):
                        pe.wait_ge(rw_masked[g], 3 * (n - 1) + 2)
                for b in range(4):
                    pe.matmul(bank(3, b * P, b * P + P), lora[0:HS, d, b * P:(b + 1) * P],
                              rw_p[0:HS, 12, chunk(c)], start=True, stop=True)
                for b in range(4):
                    ins = pe.matmul(bank(7, b * P, b * P + P), lora[HS:P, d, b * P:(b + 1) * P],
                                    rw_p[HS:P, 12, chunk(c)], start=True, stop=True)
                ins.then_inc(rw_lora, 1)

            pe.wait_ge(proj_ready, RET_BLOCKS + RWKV_BLOCKS)
            pe.wait_ge(rw_shift, RWKV_BLOCKS)
            pe.wait_ge(rw_tanh, 1)
            low_rank(0)
            pe.wait_ge(rw_z, 2)
            for b in range(4):
                pe.wait_ge(rw_ksq, b + 1)
                left, right, _ = pair(b)
                pe.matmul(left, C("ones64"), rw_ktmp[:, b, LEFT], start=True, stop=True)
                pe.matmul(right, C("ones64"), rw_ktmp[:, b, RIGHT], start=True, stop=True).then_inc(rw_ksum, 1)
            pe.wait_ge(rw_kroot, 4)
            for c in range(NCH):
                if c >= 2:
                    pe.wait_ge(rw_v_ready, c - 1)
                for b in range(4):
                    ins = pe.transpose(bank(c % 2, b * P, b * P + P), rw_p[:, 8 + b, chunk(c)], C("ident"))
                ins.then_inc(rw_vt, 1)
            pe.wait_ge(rw_v_ready, NCH)

            def matrices(n, g, k):
                lhs = (rw_b, rw_k)[k]
                for hd in [hd for hd in range(8) if where(hd)[2] == g]:
                    b, lo, _, q = where(hd)
                    ins = pe.matmul(bank(4 * g + 2 * k + q // 2, 256 * (q % 2), 256 * (q % 2) + 256),
                                    lhs[lo:lo + HS, n % 2, b, :], rw_ar[lo:lo + HS, n % 2, b, :, :]
                                    .rearrange("p a b -> p (a b)"), start=True, stop=True)
                ins.then_inc(rw_mm[g], 1)

            def matrix_turned(n, g):
                pe.wait_ge(rw_masked[g], 3 * n + 1)
                for hd in [hd for hd in range(8) if where(hd)[2] == g]:
                    b, lo, _, q = where(hd)
                    ins = pe.matmul(bank(4 * g + q // 2, P * (q % 2), P * (q % 2) + P),
                                    rw_ar[lo:lo + HS, n % 2, b, 0, :], rw_b[lo:lo + HS, n % 2, b, :],
                                    start=True, stop=True)
                ins.then_inc(rw_mm[g], 1)

            def inverse_turned(n, lv):
                for g in (1, 0):
                    pe.wait_ge(rw_tr[g], LEVELS * n + lv + 1)
                    for q in range(4):
                        ins = pe.transpose(bank(4 * g + 2, q * P, q * P + P), rw_t[:, g, q, :], C("ident"))
                    ins.then_inc(rw_tp[g], 1)

            pe.wait_ge(rw_prep, 1)
            for g in (1, 0):
                for k in range(2):
                    matrices(0, g, k)
            for g in (1, 0):
                matrix_turned(0, g)
            for n, (d, i) in enumerate(RW_BATCHES):
                c = ORDER[d][i]
                if n + 1 < NB:
                    low_rank(n + 1)
                inverse_turned(n, 0)
                for lv in range(1, LEVELS):
                    for g in (1, 0):
                        if lv == 1:
                            pe.wait_ge(rw_masked[g], 3 * n + 3)
                        for q in range(4):
                            ins = pe.matmul(bank(4 * g, q * P, q * P + P), rw_abt[:, g, q, :], rw_t[:, g, q, :],
                                            start=True, stop=True)
                        ins.then_inc(rw_qm[g], 1)
                    if lv == 4:
                        if n + 1 < NB:
                            pe.wait_ge(rw_z, 2 * (n + 2))
                        for j, src in ((0, rw_b), (1, rw_k)):
                            for b in range(4):
                                ins = pe.transpose(bank(3 + 4 * j, b * P, b * P + P), src[:, n % 2, b, :], C("ident"))
                            ins.then_inc(rw_natp, 1)
                    for g in (1, 0):
                        pe.wait_ge(rw_qs[g], (LEVELS - 1) * n + lv)
                        pe.wait_ge(rw_tt_ready[g], (LEVELS - 1) * n + lv)
                        for q in range(4):
                            ins = pe.matmul(bank(4 * g + 1, q * P, q * P + P), rw_tt[:, g, q, :], rw_q[:, g, q, :],
                                            start=True, stop=True)
                        ins.then_inc(rw_zm[g], 1)
                    if lv < LEVELS - 1:
                        inverse_turned(n, lv)
                for g in range(2):
                    pe.wait_ge(rw_tr[g], LEVELS * (n + 1))
                pe.wait_ge(rw_nat, 2 * (n + 1))
                pe.wait_ge(rw_s0, n + 1)
                for hd in (0, 2, 4, 6, 1, 3, 5, 7):
                    b, lo, g, q = where(hd)
                    out = bank(2 + hd % 2, b * HS, b * HS + HS)
                    pe.matmul(out, rw_ar[lo:lo + HS, n % 2, b, 0, :], rw_s[lo:lo + HS, d, b, :], start=True, stop=False)
                    ins = pe.matmul(out, rw_mk[:, g, q, 0, :], rw_v[:, c, hd * HS:hd * HS + HS],
                                    start=False, stop=True)
                ins.then_inc(rw_rm, 1)
                if n + 1 < NB:
                    pe.wait_ge(rw_prep, n + 2)
                    matrices(n + 1, 1, 0)
                pe.wait_ge(rw_r_ready, n + 1)
                for hd in range(8):
                    b, lo, g, q = where(hd)
                    ins = pe.matmul(bank(0, hd * HS, hd * HS + HS), rw_t[:, g, q, :], rw_r[:, hd, :],
                                    start=True, stop=True)
                ins.then_inc(rw_um, 1)
                if n + 1 < NB:
                    matrices(n + 1, 1, 1)
                pe.wait_ge(rw_u_ready, n + 1)
                for hd in (0, 2, 4, 6, 1, 3, 5, 7):
                    b, lo, g, q = where(hd)
                    out = bank(1 + hd % 2, b * P, b * P + P)[lo:lo + HS]
                    pe.matmul(out, rw_s[lo:lo + HS, d, b, :], rw_ar[lo:lo + HS, n % 2, b, 1, :], start=True, stop=False)
                    pe.matmul(out, rw_u[:, hd, :], rw_mb[:, g, q, 1, :], start=False, stop=False)
                    ins = pe.matmul(out, rw_v[:, c, hd * HS:hd * HS + HS], rw_mk[:, g, q, 1, :],
                                    start=False, stop=True)
                ins.then_inc(rw_y, 1)
                for hd in range(8):
                    b, lo, g, q = where(hd)
                    out = bank(3, b * HS, b * HS + HS)[lo:lo + HS]
                    pe.matmul(out, rw_bn[:, b, lo:lo + HS], rw_u[:, hd, :], start=True, stop=False)
                    ins = pe.matmul(out, rw_kn[:, b, lo:lo + HS], rw_v[:, c, hd * HS:hd * HS + HS],
                                    start=False, stop=True)
                ins.then_inc(rw_sm, 1)
                if n + 1 < NB:
                    pe.wait_ge(rw_y_added, n + 1)
                    matrices(n + 1, 0, 0)
                    pe.wait_ge(rw_s_ready, n + 1)
                    matrices(n + 1, 0, 1)
                    for g in (1, 0):
                        matrix_turned(n + 1, g)
            pe.wait_ge(rw_y_added, NB)
            pe.wait_ge(rw_s_ready, NB)
            tensor_head_norm(pe, 1, mix[:, 4:8, :], C("ones64"), rw_tmp)
            for b in range(4):
                pe.wait_ge(rw_bonus, b + 1)
                left, right, _ = pair(b)
                pe.matmul(left, C("ones64"), rw_p[:, b, LEFT], start=True, stop=True)
                pe.matmul(right, C("ones64"), rw_p[:, b, RIGHT], start=True, stop=True).then_inc(rw_bsum, 1)
            for b in range(4):
                pe.wait_ge(rw_badd, b + 1)
                left, right, _ = pair(b)
                pe.matmul(left, lora[:, 2, b * P:(b + 1) * P], rw_p[:, 13, LEFT], start=True, stop=True)
                pe.matmul(right, lora[:, 2, b * P:(b + 1) * P], rw_p[:, 13, RIGHT], start=True, stop=True)\
                  .then_inc(rw_g, 1)

        def scalar_rwkv(act, turn):
            def tanhs(n):
                act.wait_ge(rw_z, 2 * n + 1)
                act.activation(rw_w[:, :, :], rw_w[:, :, :], ACT.Tanh, scale=0.5).then_inc(rw_th, 1)
                act.wait_ge(rw_z, 2 * n + 2)
                act.activation(rw_a[:, :, :], rw_a[:, :, :], ACT.Tanh, scale=0.5).then_inc(rw_th, 1)

            def exponentials(n):
                act.wait_ge(rw_sum, n + 1)
                act.activation(rw_dn[:, :, :], rw_up[:, :, :], ACT.Exp, scale=-1.0)
                act.activation(rw_up[:, :, :], rw_up[:, :, :], ACT.Exp).then_inc(rw_exp, 1)

            act.wait_ge(rw_shift, RWKV_BLOCKS)
            act.activation(rw_p[0:HS, 12, :], rw_p[0:HS, 12, :], ACT.Tanh)
            act.activation(rw_p[:, 13, :], rw_p[:, 13, :], ACT.Sigmoid).then_inc(rw_tanh, 1)
            for b in range(4):
                act.wait_ge(rw_kraw, b + 1)
                act.activation(rw_ktmp[:, b, :], rw_kk[:, b, :], ACT.Square).then_inc(rw_ksq, 1)
            tanhs(0)
            exponentials(0)
            for b in range(4):
                act.wait_ge(rw_kguard, b + 1)
                last = act.activation(rw_ktmp[:, b, :], rw_ktmp[:, b, :], ACT.Ln)
            turn(last)
            for b in range(4):
                act.activation(rw_ktmp[:, b, :], rw_ktmp[:, b, :], ACT.Exp, scale=-0.5).then_inc(rw_kroot, 1)
            for c in range(NCH):
                act.wait_ge(rw_vt, c + 1)
                act.activation(rw_v[:, c, :], bank(c % 2), ACT.Copy).then_inc(rw_v_ready, 1)

            for n in range(NB):
                for lv in range(LEVELS - 1):
                    if lv == 1 and n + 1 < NB:
                        tanhs(n + 1)
                    if lv == 4 and n + 1 < NB:
                        exponentials(n + 1)
                    if lv == 5:
                        for j, dst in ((0, rw_bn), (1, rw_kn)):
                            act.wait_ge(rw_natp, 2 * n + j + 1)
                            act.activation(dst[:, :, :].rearrange("p a b -> p (a b)"), bank(3 + 4 * j), ACT.Copy)\
                               .then_inc(rw_nat, 1)
                    for g in (1, 0):
                        act.wait_ge(rw_tp[g], (LEVELS - 1) * n + lv + 1)
                        act.activation(rw_tt[:, g, :, :].rearrange("p a b -> p (a b)"), bank(4 * g + 2), ACT.Copy)\
                           .then_inc(rw_tt_ready[g], 1)
                act.wait_ge(rw_rm, n + 1)
                for odd in range(2):
                    ins = act.activation(rw_r[:, odd:8:2, :], grid(bank(2 + odd, 0, 256), 4, HS), ACT.Copy)
                ins.then_inc(rw_r_ready, 1)
                act.wait_ge(rw_um, n + 1)
                act.activation(rw_u[:, :, :].rearrange("p a b -> p (a b)"), bank(0), ACT.Copy).then_inc(rw_u_ready, 1)
            scalar_head_norm(act, turn, 1, mix[:, 4:8, :], rw_tmp)

        def vector_shift(dve, i, u):
            dve.wait_ge(proj_ready, i * 4 + RET_BLOCKS + u + 1)
            s, v = shifted[:, u % 2, :], rw_p[:, i * 4 + u, :]
            mu = par[:, bass.ds(i * 4 + (pat["mu"][0] + u), 1)]
            for lo, hi in ((0, SEQ), (SEQ, NT)):
                dve.tensor_tensor(s[:, lo + 1:hi - 1], v[:, lo:hi - 2], v[:, lo + 2:hi], ALU.add)
                dve.tensor_copy(s[:, lo:lo + 1], v[:, lo + 1:lo + 2])
                last = dve.tensor_copy(s[:, hi - 1:hi], v[:, hi - 2:hi - 1])
            last.then_inc(rw_near, 1)
            dve.wait_ge(rw_near, i * 8 + 2 * u + 1)
            dve.scalar_tensor_tensor(out=s, in0=s, scalar=0.5, in1=v, op0=ALU.mult, op1=ALU.subtract)\
               .then_inc(rw_near, 1)
            dve.wait_ge(rw_near, i * 8 + 2 * u + 2)
            dve.scalar_tensor_tensor(out=v, in0=s, scalar=mu, in1=v, op0=ALU.mult, op1=ALU.add)\
               .then_inc(rw_shift, 1)

        def vector_rwkv(dve, turn):
            def log_decay(n, step):
                d = RW_BATCHES[n][0]
                if step == 0:
                    if n:
                        dve.wait_ge(rw_prep, n)
                    dve.wait_ge(rw_lora, n + 1)
                    dve.tensor_tensor(rw_w[:, :, :], grid(bank(3), 4, P), over(prm("w0", 4 * d, 4), P), ALU.add)\
                       .then_inc(rw_z, 1)
                    dve.tensor_tensor(rw_a[:, :, :], grid(bank(7), 4, P), over(prm("a0", 4 * d, 4), P), ALU.add)\
                       .then_inc(rw_z, 1)
                elif step == 1:
                    dve.wait_ge(rw_th, 2 * n + 1)
                    turn(dve.tensor_scalar(rw_w[:, :, :], rw_w[:, :, :], -DECAY_MAX / 2, -DECAY_MAX / 2,
                                           ALU.mult, ALU.add))
                elif step == 2:
                    for b in range(4):
                        last = dve.tensor_tensor_scan(rw_f[:, b, 1:P + 1], C("ones"), rw_w[:, b, :], 0.0,
                                                      ALU.mult, ALU.add)
                    turn(last)
                else:
                    dve.tensor_tensor(rw_up[:, :, :], rw_f[:, :, :],
                                      rw_f[:, :, P // 2:P // 2 + 1].to_broadcast([P, 4, P + 1]), ALU.subtract)\
                       .then_inc(rw_sum, 1)

            dve.tensor_scalar(rw_neg_ka, prm("k_a", 0, 4), -1.0, None, ALU.mult)
            turn(dve.tensor_scalar(rw_one_ka, prm("k_a", 0, 4), -1.0, 1.0, ALU.mult, ALU.add))
            dve.wait_ge(rw_shift, RWKV_BLOCKS)
            for b in range(4):
                dve.tensor_scalar(rw_kk[:, b, :], rw_p[:, 4 + b, :], prm("k_k", b), None, ALU.mult)\
                   .then_inc(rw_kraw, 1)
            turn(dve.memset(rw_f[:, :, 0:1], 0.0))
            for step in range(4):
                log_decay(0, step)
            for b in range(4):
                dve.wait_ge(rw_ksum, b + 1)
                dve.tensor_scalar(rw_ktmp[:, b, :], pair(b)[2], 1e-24, None, ALU.max).then_inc(rw_kguard, 1)
            for b in range(4):
                dve.wait_ge(rw_kroot, b + 1)
                dve.tensor_tensor(rw_kk[:, b, :], rw_kk[:, b, :], rw_ktmp[:, b, :], ALU.mult).then_inc(rw_kk_ready, 1)
            dve.wait_ge(rw_kk_ready, 4)
            dve.wait_ge(rw_zero, 2)

            def masked(n, g, k):
                mask = C("mask_f") if RW_BATCHES[n][0] == 0 else C("mask_b")
                dve.wait_ge(rw_mm[g], 3 * n + k + 1)
                at = 2048 * g + 1024 * k
                dve.tensor_tensor((rw_mb, rw_mk)[k][:, g, :, :, :].rearrange("p a b c -> p a (b c)"),
                                  grid(ps[:, at:at + 1024], 4, 256), each(mask, 4), ALU.mult)\
                   .then_inc(rw_masked[g], 1)

            def first_level(n):
                d = RW_BATCHES[n][0]
                other, merge = (C("mask_b"), C("merge_f")) if d == 0 else (C("mask_f"), C("merge_b"))
                for g in (1, 0):
                    dve.wait_ge(rw_masked[g], 3 * n + 2)
                    last = dve.tensor_tensor(rw_t[:, g, :, :], rw_mb[:, g, :, 0, :], each(merge[:, 0:P], 4), ALU.mult)
                turn(last)
                for g in (1, 0):
                    dve.tensor_tensor(rw_t[:, g, :, :], rw_t[:, g, :, :], each(C("ident"), 4), ALU.add)\
                       .then_inc(rw_tr[g], 1)
                for g in (1, 0):
                    dve.wait_ge(rw_mm[g], 3 * n + 3)
                    dve.tensor_tensor(rw_abt[:, g, :, :].rearrange("p (a b) c -> p a b c", a=2),
                                      grid(ps[:, 2048 * g:2048 * g + 1024], 2, 4, P)[:, :, 0:2, :],
                                      each(other[:, 0:P], 4).rearrange("p (a b) c -> p a b c", a=2), ALU.mult)\
                       .then_inc(rw_masked[g], 1)

            for g in (1, 0):
                for k in range(2):
                    masked(0, g, k)
            first_level(0)
            for n, (d, i) in enumerate(RW_BATCHES):
                c = ORDER[d][i]
                merge = C("merge_f") if d == 0 else C("merge_b")
                if n + 1 < NB:
                    log_decay(n + 1, 0)
                for lv in range(1, LEVELS):
                    for g in (1, 0):
                        dve.wait_ge(rw_qm[g], (LEVELS - 1) * n + lv)
                        dve.tensor_tensor(rw_q[:, g, :, :], grid(bank(4 * g), 4, P),
                                          each(merge[:, lv * P:(lv + 1) * P], 4), ALU.mult).then_inc(rw_qs[g], 1)
                    if n + 1 < NB and lv < 4:
                        log_decay(n + 1, lv)
                    for g in (1, 0):
                        dve.wait_ge(rw_zm[g], (LEVELS - 1) * n + lv)
                        dve.wait_ge(rw_tr[g], LEVELS * n + lv)
                        dve.tensor_tensor(rw_t[:, g, :, :], rw_t[:, g, :, :], grid(bank(4 * g + 1), 4, P), ALU.add)\
                           .then_inc(rw_tr[g], 1)
                    if lv == 1:
                        if n >= 2:
                            dve.wait_ge(rw_s_ready, n - 1)
                        if i == 1:
                            dve.wait_ge(rw_first, 16 * (d + 1))
                        S = rw_s[:, d, :, :]
                        dve.tensor_tensor(S, S, over(rw_edge[:, n % 2, 0, :], HS), ALU.mult).then_inc(rw_s0, 1)
                dve.wait_ge(rw_y, n + 1)
                for odd in range(2):
                    lo = HS * odd
                    dst = mix[lo:lo + HS, 4:8, chunk(c)]
                    src = grid(bank(1 + odd), 4, P)[lo:lo + HS]
                    seen = [ORDER[e][j] for e, j in RW_BATCHES[:n]]
                    if c in seen:
                        last = dve.tensor_tensor(dst, dst, src, ALU.add)
                    else:
                        last = dve.tensor_copy(dst, src)
                last.then_inc(rw_y_added, 1)
                if n + 1 < NB:
                    masked(n + 1, 1, 0)
                dve.wait_ge(rw_y_added, n + 1)
                dve.wait_ge(rw_sm, n + 1)
                turn(dve.tensor_tensor(S, S, grid(bank(3, 0, 256), 4, HS), ALU.add))
                dve.tensor_tensor(S, S, over(rw_edge[:, n % 2, 1, :], HS), ALU.mult).then_inc(rw_s_ready, 1)
                if n + 1 < NB:
                    masked(n + 1, 1, 1)
                    masked(n + 1, 0, 0)
                    masked(n + 1, 0, 1)
                    first_level(n + 1)
            vector_head_norm(dve, turn, 1, mix[:, 4:8, :], rw_tmp, HS, 64e-5, "ln_w")
            for b in range(4):
                dve.scalar_tensor_tensor(out=rw_p[:, b, :], in0=rw_p[:, b, :], scalar=prm("r_k", b),
                                         in1=rw_p[:, 4 + b, :], op0=ALU.mult, op1=ALU.mult).then_inc(rw_bonus, 1)
            for b in range(4):
                dve.wait_ge(rw_bsum, b + 1)
                turn(dve.tensor_tensor(rw_p[:, 8 + b, :], rw_p[:, 8 + b, :], pair(b)[2], ALU.mult))
                dve.scalar_tensor_tensor(out=mix[:, 4 + b, :], in0=mix[:, 4 + b, :], scalar=prm("ln_b", b),
                                         in1=rw_p[:, 8 + b, :], op0=ALU.add, op1=ALU.add).then_inc(rw_badd, 1)
            for b in range(4):
                dve.wait_ge(rw_g, b + 1)
                last = dve.tensor_tensor(mix[:, 4 + b, :], mix[:, 4 + b, :], pair(b)[2], ALU.mult)
            turn(last)
            dve.sem_inc(mix_ready, 4)

        la = Area(rest, mx.at)
        ml_p = la.take(MLSTM_BLOCKS, NT)
        ll, la = la, Area(w_mem)
        ml_v = la.take(NCH, 4, P + 1)
        ml_kn = la.take(NCH, 4, P)
        ml_b = la.take(NT)
        ml_top = la.take(NT)
        ml_share = la.take(NT)
        ml_floor = la.take(NT)
        ml_left = la.take(NT)
        ml_m = ll.take(NCH)
        ml_last = ll.take(NCH)
        ml_dec = ll.take(NCH)
        ml_mend = ll.take(1)
        ml_g = ll.take(2, NCH, HS)
        lv_ = Area(rest, mx.at + 8 * NT, mx.at + 12 * NT)
        ml_sw = lv_.take(4, P)
        ml_den = lv_.take(4, P)
        ml_bd = lv_.take(2, 4, P)
        ml_w = la.take(2, 4, P)
        ml_q = ll.take(2, 4, P)
        ml_wk = [lv_.take(4, P), rs[:, 0:4 * P].rearrange("p (a b) -> p a b", a=4)]
        ml_c = la.take(2, 4, P + 1)
        ml_decb = ll.take(2 * 4, NCH)
        R = HS

        ml_fg = sem("ml_fg")
        ml_soft = sem("ml_soft")
        ml_rows = sem("ml_rows")
        ml_exps = sem("ml_exps")
        ml_kscaled = sem("ml_kscaled")
        ml_vt = sem("ml_vt")
        ml_kt = sem("ml_kt")
        ml_nat = sem("ml_nat")
        ml_gt = sem("ml_gt")
        ml_g_ready = sem("ml_g_ready")
        ml_spread = sem("ml_spread")
        ml_score = sem("ml_score")
        ml_q_ready = sem("ml_q_ready")
        ml_wk_ready = sem("ml_wk_ready")
        ml_arg = sem("ml_arg")
        ml_w_ready = sem("ml_w_ready")
        ml_bd_ready = sem("ml_bd_ready")
        ml_fed = sem("ml_fed")
        ml_nd = sem("ml_nd")
        ml_added = sem("ml_added")
        ml_abs = sem("ml_abs")
        ml_big = sem("ml_big")
        ml_over = sem("ml_over")
        ml_done = sem("ml_done")
        ml_zero = sem("ml_zero")
        ml_first = sem("ml_first")
        ml_sig = sem("ml_sig")

        def run(d, c):
            lo, hi = c * P, (c + 1) * P
            return slice(lo, hi) if d == 0 else slice(hi - 1, lo - 1 if lo else None, -1)

        def pool_mlstm(pool):
            pool.wait_ge(proj_ready, RET_BLOCKS + RWKV_BLOCKS + MLSTM_BLOCKS)
            for d in range(2):
                pool.memset(ml_c[:, d, :, :], 0.0).then_inc(ml_zero, 1)
            pool.memset(ml_v[:, :, :, P:P + 1], 1.0).then_inc(ml_zero, 1)
            pool.wait_ge(ml_nat, 2 * NCH)
            pool.wait_ge(ml_g_ready, 1)
            for n, (d, i) in enumerate(RW_BATCHES):
                if n >= 2:
                    pool.wait_ge(ml_added, n - 1)
                pool.tensor_tensor(ml_wk[n % 2][:, :, :], ml_kn[:, ORDER[d][i], :, :],
                                   over(ml_g[:, 1, ORDER[d][i], 32 * d:32 * d + 4], P), ALU.mult)\
                    .then_inc(ml_wk_ready, 1)
                if n in (1, 2):
                    e = n - 1
                    pool.wait_ge(ml_done, e + 1)
                    pool.dma_start(outs["mc"][e], ml_c[:, e, :, :]).then_inc(saved, 16)
                    pool.wait_ge(saved, 16 * (5 + e))
                    pool.dma_start(ml_c[:, e, :, :], st["s_mc"][e]).then_inc(ml_first, 16)
            for d in range(2):
                pool.dma_start(outs["m"][d], ml_mend[32 * d:32 * d + 4, :]).then_inc(saved, 16)

        def tensor_mlstm(pe):
            pe.wait_ge(proj_ready, RET_BLOCKS + RWKV_BLOCKS + MLSTM_BLOCKS)
            pe.wait_ge(ml_kscaled, 1)
            for c in range(NCH):
                if c >= 2:
                    pe.wait_ge(ml_nat, 2 * (c - 1))
                for j, go in ((8, ml_vt), (4, ml_kt)):
                    for b in range(4):
                        ins = pe.transpose(bank((j == 4) * 2 + c % 2, b * P, b * P + P), ml_p[:, j + b, chunk(c)],
                                           C("ident"))
                    ins.then_inc(go, 1)
            pe.wait_ge(ml_exps, 1)
            for j, row in ((0, ml_p[:, 12, :]), (1, ml_left)):
                for c in range(NCH):
                    pe.transpose(bank(4 + j, c * HS, c * HS + HS), row[0:R, chunk(c)], C("ident", R)[:, 0:R])

            def spread(out, d, hd, row):
                r = 32 * d + hd
                return pe.matmul(out, C("ident", R)[:, r:r + 1].to_broadcast([R, P]), row, start=True, stop=True)

            for d in range(2):
                for hd in range(4):
                    at = (4 * d + hd) * NCH
                    ins = spread(bank(6, at, at + NCH), d, hd, ml_dec[0:R, :])
            ins.then_inc(ml_gt, 1)
            pe.wait_ge(ml_nat, 2 * NCH)
            pe.wait_ge(ml_g_ready, 1)

            def spread_rows(n):
                d, i = RW_BATCHES[n]
                if n:
                    pe.wait_ge(ml_q_ready, n)
                    pe.wait_ge(ml_bd_ready, n)
                for b, row in ((1, ml_top), (2, ml_share), (3, ml_floor)):
                    for hd in range(4):
                        ins = spread(bank(b, hd * P, hd * P + P), d, hd, row[0:R, chunk(ORDER[d][i])])
                ins.then_inc(ml_spread, 1)

            def scores(n):
                d, i = RW_BATCHES[n]
                c = ORDER[d][i]
                for hd in range(4):
                    ins = pe.matmul(bank(0, hd * P, hd * P + P), ml_p[:, 4 + hd, chunk(c)], ml_p[:, hd, chunk(c)],
                                    start=True, stop=True)
                ins.then_inc(ml_score, 1)

            spread_rows(0)
            scores(0)
            for n, (d, i) in enumerate(RW_BATCHES):
                c = ORDER[d][i]
                if n + 1 < NB:
                    spread_rows(n + 1)
                pe.wait_ge(ml_wk_ready, n + 1)
                pe.wait_ge(ml_fed, n + 1)
                for hd in range(4):
                    pe.matmul(bank(4, hd * P, hd * P + P), ml_v[:, c, hd, 0:P], ml_sw[:, hd, :],
                              start=True, stop=False)
                    pe.matmul(bank(4, hd * P, hd * P + P), ml_c[:, d, hd, 0:P], ml_q[:, n % 2, hd, :],
                              start=False, stop=True)
                for hd in range(4):
                    pe.matmul(bank(5, hd * P, hd * P + P), C("ones"), ml_sw[:, hd, :], start=True, stop=False)
                    ins = pe.matmul(bank(5, hd * P, hd * P + P), ml_c[:, d, hd, P:P + 1].to_broadcast([P, P]),
                                    ml_q[:, n % 2, hd, :], start=False, stop=True)
                ins.then_inc(ml_nd, 1)
                for hd in range(4):
                    at = (P + 1) * (hd % 2)
                    ins = pe.matmul(bank(6 + hd // 2, at, at + P + 1), ml_wk[n % 2][:, hd, :], ml_v[:, c, hd, :],
                                    start=True, stop=True)
                ins.then_inc(ml_added, 1)
                if n + 1 < NB:
                    scores(n + 1)
            pe.wait_ge(ml_done, NB)
            tensor_head_norm(pe, 2, mix[:, 0:4, :], C("ones"), ml_kn.rearrange("p a b c -> p (a b c)")
                             .rearrange("p (a b) -> p a b", a=4))
            pe.wait_ge(hn_ms, 12)

        def scalar_mlstm(act, turn):
            act.activation(ml_p[:, 4:8, :], ml_p[:, 4:8, :], ACT.Copy, scale=float(P) ** -0.5).then_inc(ml_kscaled, 1)
            act.wait_ge(ml_fg, 1)
            t = ml_left[0:R, :]
            turn(act.activation(t, ml_p[0:R, 13, :], ACT.Abs))
            turn(act.activation(t, t, ACT.Exp, scale=-1.0))
            act.activation(t, t, ACT.Ln, bias=1.0).then_inc(ml_soft, 1)
            for c in range(NCH):
                for j, (go, src) in enumerate(((ml_vt, ml_v[:, c, :, 0:P]), (ml_kt, ml_kn[:, c, :, :]))):
                    act.wait_ge(go, c + 1)
                    act.activation(src, grid(bank(2 * j + c % 2), 4, P), ACT.Copy).then_inc(ml_nat, 1)
            act.wait_ge(ml_rows, 1)
            for c in range(NCH):
                act.activation(ml_share[0:R, chunk(c)], ml_top[0:R, chunk(c)], ACT.Exp, scale=-1.0,
                               bias=ml_m[0:R, c:c + 1])
            act.activation(ml_floor[0:R, :], ml_floor[0:R, :], ACT.Exp, scale=-1.0)
            act.activation(ml_dec[0:R, :], ml_dec[0:R, :], ACT.Exp)
            act.activation(ml_left[0:R, :], ml_left[0:R, :], ACT.Exp).then_inc(ml_exps, 1)
            act.wait_ge(ml_gt, 1)
            for j in range(2):
                ins = act.activation(ml_g[:, j, :, :].rearrange("p a b -> p (a b)"), bank(4 + j, 0, NCH * HS), ACT.Copy)
            ins.then_inc(ml_g_ready, 1)

            def weights(n):
                act.wait_ge(ml_spread, n + 1)
                if n >= 2:
                    act.wait_ge(ml_done, n - 1)
                act.activation(ml_bd[:, n % 2, :, :], grid(bank(3), 4, P), ACT.Copy).then_inc(ml_bd_ready, 1)
                act.wait_ge(ml_arg, n + 1)
                act.activation(ml_w[:, n % 2, :, :], ml_w[:, n % 2, :, :], ACT.Exp).then_inc(ml_w_ready, 1)

            weights(0)
            for n in range(NB):
                if n + 1 < NB:
                    weights(n + 1)
                act.wait_ge(ml_nd, n + 1)
                act.activation(ml_den[:, :, :], grid(bank(5), 4, P), ACT.Abs).then_inc(ml_abs, 1)
                act.wait_ge(ml_big, n + 1)
                turn(act.activation(ml_den[:, :, :], ml_den[:, :, :], ACT.Ln))
                act.activation(ml_den[:, :, :], ml_den[:, :, :], ACT.Exp, scale=-1.0).then_inc(ml_over, 1)
            act.activation(ml_p[:, 14:18, :], ml_p[:, 14:18, :], ACT.Sigmoid).then_inc(ml_sig, 1)
            scalar_head_norm(act, turn, 2, mix[:, 0:4, :], ml_kn.rearrange("p a b c -> p (a b c)")
                             .rearrange("p (a b) -> p a b", a=4))

        def vector_mlstm(dve, turn):
            dve.wait_ge(proj_ready, RET_BLOCKS + RWKV_BLOCKS + MLSTM_BLOCKS)
            ig, fg = ml_p[0:R, 12, :], ml_p[0:R, 13, :]
            dve.tensor_scalar(fg, fg, prm("f_bias", rows=R), None, ALU.add).then_inc(ml_fg, 1)
            dve.tensor_scalar(ig, ig, prm("i_bias", rows=R), None, ALU.add)
            dve.memset(ml_b[0:R, :], 0.0)
            dve.memset(ml_top[0:R, :], 0.0)
            dve.memset(ml_last[0:R, :], 0.0)
            turn(dve.memset(ml_m[0:R, :], 0.0))
            for d in range(2):
                rows = slice(32 * d, 32 * d + 4)
                c = ORDER[d][1]
                dve.tensor_copy(ml_m[rows, c:c + 1], par[rows, pat["m_init"][0]:pat["m_init"][1]])
            dve.wait_ge(ml_soft, 1)
            turn(dve.scalar_tensor_tensor(out=fg, in0=fg, scalar=0.0, in1=ml_left[0:R, :], op0=ALU.min,
                                          op1=ALU.subtract))
            for d in range(2):
                rows = slice(32 * d, 32 * d + 4)
                for c in range(NCH):
                    last = dve.tensor_tensor_scan(ml_b[rows, run(d, c)], C("ones")[rows, :],
                                                  ml_p[rows, 13, run(d, c)], 0.0, ALU.mult, ALU.add)
            turn(last)
            turn(dve.tensor_tensor(ig, ig, ml_b[0:R, :], ALU.subtract))
            for i in range(NCH):
                for d in range(2):
                    rows, c = slice(32 * d, 32 * d + 4), ORDER[d][i]
                    g = ml_p[rows, 12, run(d, c)]
                    last = dve.tensor_tensor_scan(ml_top[rows, run(d, c)], g, g, ml_m[rows, c:c + 1],
                                                  ALU.max, ALU.max)
                turn(last)
                for d in range(2):
                    rows, c = slice(32 * d, 32 * d + 4), ORDER[d][i]
                    e = c * P + (P - 1 if d == 0 else 0)
                    last = dve.tensor_copy(ml_last[rows, c:c + 1], ml_top[rows, e:e + 1])
                    if i + 1 < NCH:
                        m = ml_mend[rows, :] if i == 0 else ml_m[rows, ORDER[d][i + 1]:ORDER[d][i + 1] + 1]
                        last = dve.tensor_tensor(m, ml_top[rows, e:e + 1], ml_b[rows, e:e + 1], ALU.add)
                turn(last)
            dve.tensor_tensor(ml_floor[0:R, :], ml_b[0:R, :], ml_top[0:R, :], ALU.add)
            dve.tensor_tensor(ml_dec[0:R, :], ml_m[0:R, :], ml_last[0:R, :], ALU.subtract)
            dve.tensor_tensor(grid(ml_left[0:R, :], NCH, P), grid(ig, NCH, P), over(ml_last[0:R, :], P),
                              ALU.subtract).then_inc(ml_rows, 1)
            dve.wait_ge(ml_g_ready, 1)
            turn(dve.tensor_copy(ml_decb[:, :, :], grid(bank(6, 0, 8 * NCH), 8, NCH)))
            dve.wait_ge(ml_zero, 3)

            def exponents(n):
                d, i = RW_BATCHES[n]
                c, w = ORDER[d][i], ml_w[:, n % 2, :, :]
                if n >= 2:
                    dve.wait_ge(ml_fed, n - 1)
                dve.wait_ge(ml_spread, n + 1)
                turn(dve.scalar_tensor_tensor(out=w, in0=grid(bank(1), 4, P), scalar=-1.0,
                                              in1=over(ml_g[:, 0, c, 32 * d:32 * d + 4], P),
                                              op0=ALU.mult, op1=ALU.add))
                dve.scalar_tensor_tensor(out=w, in0=w, scalar=0.0, in1=each(C(("neg_f", "neg_b")[d]), 4),
                                         op0=ALU.min, op1=ALU.add).then_inc(ml_arg, 1)
                dve.tensor_tensor(ml_q[:, n % 2, :, :], ml_p[:, 0:4, chunk(c)], grid(bank(2), 4, P), ALU.mult)\
                   .then_inc(ml_q_ready, 1)

            def weighed(n):
                if RW_BATCHES[n][1] == 1:
                    dve.wait_ge(ml_first, 16 * (RW_BATCHES[n][0] + 1))
                dve.wait_ge(ml_score, n + 1)
                dve.wait_ge(ml_w_ready, n + 1)
                dve.tensor_tensor(ml_sw[:, :, :], ml_w[:, n % 2, :, :], grid(bank(0), 4, P), ALU.mult)\
                   .then_inc(ml_fed, 1)

            exponents(0)
            weighed(0)
            for n, (d, i) in enumerate(RW_BATCHES):
                c = ORDER[d][i]
                if n + 1 < NB:
                    exponents(n + 1)
                dve.wait_ge(ml_nd, n + 1)
                if n:
                    dve.wait_ge(ml_done, n)
                dve.wait_ge(ml_bd_ready, n + 1)
                dve.wait_ge(ml_abs, n + 1)
                dve.tensor_tensor(ml_den[:, :, :], ml_den[:, :, :], ml_bd[:, n % 2, :, :], ALU.max).then_inc(ml_big, 1)
                dve.wait_ge(ml_added, n + 1)
                for hd in range(4):
                    at, s = (P + 1) * (hd % 2), ml_c[:, d, hd, :]
                    dve.scalar_tensor_tensor(out=s, in0=s, scalar=ml_decb[:, 4 * d + hd, c:c + 1],
                                             in1=bank(6 + hd // 2, at, at + P + 1), op0=ALU.mult, op1=ALU.add)
                dve.wait_ge(ml_over, n + 1)
                dst = mix[:, 0:4, chunk(c)]
                if c in [ORDER[e][j] for e, j in RW_BATCHES[:n]]:
                    turn(dve.tensor_tensor(ml_den[:, :, :], ml_den[:, :, :], grid(bank(4), 4, P), ALU.mult))
                    last = dve.tensor_tensor(dst, dst, ml_den[:, :, :], ALU.add)
                else:
                    last = dve.tensor_tensor(dst, ml_den[:, :, :], grid(bank(4), 4, P), ALU.mult)
                last.then_inc(ml_done, 1)
                if n + 1 < NB:
                    weighed(n + 1)
            dve.wait_ge(ml_done, NB)
            tmp = ml_kn.rearrange("p a b c -> p (a b c)").rearrange("p (a b) -> p a b", a=4)
            vector_head_norm(dve, turn, 2, mix[:, 0:4, :], tmp, P, 1e-5, "mn_w")
            dve.wait_ge(ml_sig, 1)
            turn(dve.tensor_tensor(mix[:, 0:4, :], mix[:, 0:4, :], ml_p[:, 14:18, :], ALU.mult))
            dve.sem_inc(mix_ready, 4)

        aa = Area(rest, mx.at)
        at_p = aa.take(ATT_BLOCKS, NT)
        aa = Area(w_mem)
        at_ck = aa.take(2, PAST)
        at_cv = aa.take(2 * HS)
        at_v = aa.take(NCH, 2 * HS)
        at_tmp = aa.take(6, NT)
        at_rope = aa.take(2, DEC_SEQ)
        at_e = aa.take(3, NT)
        at_t = aa.take(2, NT)
        at_stat = aa.take(3, 4)

        at_sq = sem("at_sq")
        at_ss = sem("at_ss")
        at_ms = sem("at_ms")
        at_root = sem("at_root")
        at_normed = sem("at_normed")
        at_turned = sem("at_turned")
        at_roped = sem("at_roped")
        at_vt = sem("at_vt")
        at_v_ready = sem("at_v_ready")
        at_cached = sem("at_cached")
        at_score = sem("at_score")
        at_max = sem("at_max")
        at_exp = sem("at_exp")
        at_prob = sem("at_prob")
        at_pt = sem("at_pt")
        at_pt_ready = sem("at_pt_ready")
        at_o = sem("at_o")
        at_out = sem("at_out")
        AT_UNITS = [(c, hd) for c in range(NCH) for hd in range(8)]
        NU = len(AT_UNITS)

        def key_pair(s):
            at = 1024 * s + 384
            return ps[:, at:at + P], ps[:, at + P:at + NT], ps[:, at:at + NT]

        def keys_of(c):
            return 1 if c == 0 else NCH

        def pool_attention(pool):
            pool.wait_ge(proj_ready, RET_BLOCKS + RWKV_BLOCKS + MLSTM_BLOCKS + ATT_BLOCKS)
            pool.dma_start(at_ck[:, :, :], st["s_ck"]).then_inc(at_cached, 16)
            pool.dma_start(grid(at_cv, 2, HS), st["s_cv"]).then_inc(at_cached, 16)
            pool.wait_ge(at_normed, 6)
            for g in range(2):
                pool.dma_start(outs["ck"][g], at_p[0:HS, 4 + g, PROMPT]).then_inc(saved, 16)
            pool.wait_ge(at_v_ready, 1)
            pool.dma_start(outs["cv"], at_v[:, 0, :]).then_inc(saved, 16)

        def tensor_attention(pe):
            pe.wait_ge(proj_ready, RET_BLOCKS + RWKV_BLOCKS + MLSTM_BLOCKS + ATT_BLOCKS)
            for b in range(6):
                pe.wait_ge(at_sq, b + 1)
                if b >= 3:
                    pe.wait_ge(at_ms, b - 2)
                left, right, _ = pair(b % 3)
                pe.matmul(left, C("ones64"), at_tmp[:, b, LEFT], start=True, stop=True)
                pe.matmul(right, C("ones64"), at_tmp[:, b, RIGHT], start=True, stop=True).then_inc(at_ss, 1)
            for c in range(NCH):
                ins = pe.transpose(bank(6 + c // 4, c % 4 * P, c % 4 * P + P), at_p[:, 6, chunk(c)], C("ident"))
            ins.then_inc(at_vt, 1)
            pe.wait_ge(at_ms, 6)
            for b in range(6):
                pe.wait_ge(at_normed, b + 1)
                pe.matmul(bank(b), C("turn"), at_p[:, b, SAMPLE], start=True, stop=True).then_inc(at_turned, 1)
            pe.wait_ge(at_roped, 6)
            pe.wait_ge(at_v_ready, 1)
            pe.wait_ge(at_cached, 32)

            def scores(n):
                c, hd = AT_UNITS[n]
                lo, g = HS * (hd % 2), hd // 4
                pr, sa, _ = key_pair(n % 2)
                q = at_p[lo:lo + HS, hd // 2, chunk(c)]
                if n >= 2:
                    pe.wait_ge(at_exp, n - 1)
                if c == 0:
                    pe.matmul(pr, q, at_p[lo:lo + HS, 4 + g, PROMPT], start=True, stop=True).then_inc(at_score, 1)
                else:
                    pe.matmul(pr, q, at_ck[lo:lo + HS, g, :], start=True, stop=True)
                    pe.matmul(sa, q, at_p[lo:lo + HS, 4 + g, SAMPLE], start=True, stop=True).then_inc(at_score, 1)

            def turned(n):
                c, hd = AT_UNITS[n]
                pe.wait_ge(at_prob, n + 1)
                if n >= 1:
                    pe.wait_ge(at_pt_ready, n)
                for j in range(keys_of(c)):
                    ins = pe.transpose(key_pair(2)[2][:, j * P:(j + 1) * P], at_e[:, n % 3, j * P:(j + 1) * P], C("ident"))
                ins.then_inc(at_pt, 1)

            def values(n):
                c, hd = AT_UNITS[n]
                lo, g = HS * (hd % 2), hd // 4
                pe.wait_ge(at_pt_ready, n + 1)
                if n >= 2:
                    pe.wait_ge(at_out, n - 1)
                nk = keys_of(c)
                for j in range(nk):
                    v = at_cv[:, g * HS:(g + 1) * HS] if c and j == 0 else at_v[:, j, g * HS:(g + 1) * HS]
                    ins = pe.matmul(bank(6 + n % 2, 0, P)[lo:lo + HS], v, at_t[:, n % 2, j * P:(j + 1) * P],
                                    start=(j == 0), stop=(j == nk - 1))
                ins.then_inc(at_o, 1)

            for n in range(NU + 3):
                if n < NU:
                    scores(n)
                if 2 <= n <= NU + 1:
                    turned(n - 2)
                if n >= 3:
                    values(n - 3)

        def scalar_attention(act, turn):
            for b in range(6):
                act.activation(at_tmp[:, b, :], at_p[:, b, :], ACT.Square).then_inc(at_sq, 1)
            act.wait_ge(at_vt, 1)
            act.activation(at_v[:, 0:4, :].rearrange("p a b -> p (a b)"), bank(6), ACT.Copy)
            act.activation(at_v[:, 4, :], bank(7, 0, P), ACT.Copy).then_inc(at_v_ready, 1)
            for b in range(6):
                act.wait_ge(at_ms, b + 1)
                last = act.activation(at_tmp[:, b, :], at_tmp[:, b, :], ACT.Ln)
            turn(last)
            for b in range(6):
                act.activation(at_tmp[:, b, :], at_tmp[:, b, :], ACT.Exp, scale=-0.5).then_inc(at_root, 1)
            for n in range(NU + 3):
                if n < NU:
                    c, hd = AT_UNITS[n]
                    w = keys_of(c) * P
                    act.wait_ge(at_max, n + 1)
                    if n >= 3:
                        act.wait_ge(at_pt, n - 2)
                    act.activation(at_e[:, n % 3, 0:w], key_pair(n % 2)[2][:, 0:w], ACT.Exp, scale=HS ** -0.5,
                                   bias=at_stat[:, n % 3, 1:2], accum_out=at_stat[:, n % 3, 2:3]).then_inc(at_exp, 1)
                if 2 <= n <= NU + 1:
                    c, hd = AT_UNITS[n - 2]
                    w = keys_of(c) * P
                    act.wait_ge(at_pt, n - 1)
                    if n >= 4:
                        act.wait_ge(at_o, n - 3)
                    act.activation(at_t[:, n % 2, 0:w], key_pair(2)[2][:, 0:w], ACT.Copy).then_inc(at_pt_ready, 1)
                if n >= 3:
                    c, hd = AT_UNITS[n - 3]
                    lo = HS * (hd % 2)
                    act.wait_ge(at_o, n - 2)
                    act.activation(mix[lo:lo + HS, 4 + hd // 2, chunk(c)], bank(6 + (n - 3) % 2, 0, P)[lo:lo + HS],
                                   ACT.Copy).then_inc(at_out, 1)

        def vector_attention(dve, turn):
            for b in range(6):
                dve.wait_ge(at_ss, b + 1)
                dve.tensor_scalar(at_tmp[:, b, :], pair(b % 3)[2], 1.0 / HS, EPS, ALU.mult, ALU.add)\
                   .then_inc(at_ms, 1)
            for b in range(6):
                dve.wait_ge(at_root, b + 1)
                dve.scalar_tensor_tensor(out=at_p[:, b, :], in0=at_p[:, b, :],
                                         scalar=prm("q_gain" if b < 4 else "k_gain"), in1=at_tmp[:, b, :],
                                         op0=ALU.mult, op1=ALU.mult).then_inc(at_normed, 1)
            dve.wait_ge(at_normed, 6)
            for b in range(6):
                rope(dve, turn, at_p[:, b, SAMPLE], bank(b), at_rope[:, b % 2, :], at_turned, b + 1, at_roped)
            for n in range(NU + 1):
                if n < NU:
                    c, hd = AT_UNITS[n]
                    dve.wait_ge(at_score, n + 1)
                    turn(dve.tensor_reduce(at_stat[:, n % 3, 0:1], key_pair(n % 2)[2][:, 0:keys_of(c) * P], AX.X, ALU.max))
                    dve.tensor_scalar(at_stat[:, n % 3, 1:2], at_stat[:, n % 3, 0:1], -HS ** -0.5, None, ALU.mult)\
                       .then_inc(at_max, 1)
                if n >= 1:
                    m = n - 1
                    c, hd = AT_UNITS[m]
                    w = keys_of(c) * P
                    dve.wait_ge(at_exp, m + 1)
                    turn(dve.reciprocal(at_stat[:, m % 3, 3:4], at_stat[:, m % 3, 2:3]))
                    dve.tensor_scalar(at_e[:, m % 3, 0:w], at_e[:, m % 3, 0:w], at_stat[:, m % 3, 3:4], None,
                                      ALU.mult).then_inc(at_prob, 1)
            dve.wait_ge(at_out, NU)
            dve.wait_ge(saved, 16 * 11)
            dve.sem_inc(mix_ready, 4)


        block = ctx.enter_context(nc.Block())

        @block.sync
        def _(sp):
            sp.dma_start(par[:, :], params_in).then_inc(par_loaded, 16)

            def stream(src, n0, n, cols):
                def one(i, u):
                    at = src[i * RING + u]
                    sp.wait_ge(split_ready, i * RING + n0 + u + 1)
                    r = (n0 + u) % RING
                    sp.dma_start(ring[:, r, 0:cols], at).then_inc(land[r], 16)
                looped(sp, n, one)

            for layer in range(DEPTH):
                for name, blocks, k in stages_of_layer(layer):
                    if name in ("rwkv", "att", "out"):
                        sp.wait_ge(mix_ready, 4 * (1 + (name == "out")) + 8 * layer)
                        if name != "out":
                            sp.wait_ge(saved, 16 * (2 if layer == 0 else 8))
                    if k:
                        stream(w[layer][name], tile0[layer, name], blocks, k * P)
            for k in range(DB):
                sp.wait_ge(y_ready, k + 1)
                sp.dma_start(outs["y"][:, k, :], y[:, k, :]).then_inc(stored, 16)
            sp.wait_ge(stored, 16 * DB)


        @block.tensor
        def _(pe):
            pe.sem_inc(tiles_done, SPLITS)

            def pairs_read(layer, name):
                pe.wait_ge(free_dve, free0[layer, name]["dve"])
                pe.wait_ge(free_act, free0[layer, name]["act"])

            def linear(layer, name, n, k_blocks, hi, lo, last_k=None, ready=None):
                b0, n0 = blk0[layer, name], tile0[layer, name]
                pairs_read(layer, name)
                reader, f0 = (free_act, free0[layer, name]["act"]) if name in PROJECTIONS else \
                             (free_dve, free0[layer, name]["dve"])

                def one(i, u):
                    left, right, _ = pair((b0 + u) % SETS)
                    s = (n0 + u) % SPLITS
                    pe.wait_ge(reader, i * 4 + f0 + u + 1 - SETS)
                    pe.wait_ge(split_ready, i * 4 + RING + n0 + u + 1)
                    for k in range(k_blocks):
                        if ready is not None and u == 0:
                            pe.wait_ge(ready[0], ready[1] + k + 1)
                        if last_k is not None and k == k_blocks - 1:
                            pe.wait_ge(gated_ready, last_k)
                        w_h, w_l = w_hi[:, s, k * P:(k + 1) * P], w_lo[:, s, k * P:(k + 1) * P]
                        first, last = k == 0, k == k_blocks - 1
                        for weights, acts in ((w_h, hi), (w_h, lo), (w_l, hi)):
                            start, stop = first and weights is w_h and acts is hi, last and weights is w_l
                            pe.matmul(left, weights, acts[:, k, LEFT], start=start, stop=stop)
                            mm = pe.matmul(right, weights, acts[:, k, RIGHT], start=start, stop=stop)
                    mm.then_inc(tiles_done, 1)
                looped(pe, n, one)

            def ada(layer):
                n0 = tile0[layer, "ada"]
                pairs_read(layer, "ada")
                pe.wait_ge(cond_ready, 1)

                def group(i, u):
                    pe.wait_ge(ada_row_ready, i * 4 + N_MOD * layer + u + 1)
                    for k in range(DB):
                        n = n0 + u * DB + k
                        r = n % RING
                        pe.wait_ge(land[r], i * (4 * DB // RING * 16) + 16 * (n // RING + 1))
                        for half in range(2):
                            at = u % 2 * D_MODEL + half * 512
                            mm = pe.matmul(ps[0:2, at:at + 512], scond[:, k, :],
                                           ring[:, r, half * 512:(half + 1) * 512],
                                           start=(k == 0), stop=(k == DB - 1))
                        mm.then_inc(tiles_done, 1)
                looped(pe, N_MOD, group)
                pe.wait_ge(ada_row_ready, N_MOD * (layer + 1) + 2)
                pe.wait_ge(loaded, 48)

                for b in range(N_MOD * DB):
                    ins = pe.transpose(bank(4, 2 * b, 2 * b + 2), ada_row[:, b * P:(b + 1) * P], C("ident", 2)[:, 0:2])
                ins.then_inc(ada_turned, 1)

            norms = [0]

            def norm(layer, name):
                left, right, _ = pair(blk0[layer, name] % SETS)
                pairs_read(layer, name)
                for k in range(DB):
                    pe.wait_ge(sq_ready, norms[0] * DB + k + 1)
                    pe.matmul(left, C("ones"), squares(name)[:, k, LEFT], start=(k == 0), stop=(k == DB - 1))
                    mm = pe.matmul(right, C("ones"), squares(name)[:, k, RIGHT], start=(k == 0), stop=(k == DB - 1))
                mm.then_inc(norm_ready, 1)
                norms[0] += 1

            halves = 0
            for layer in range(DEPTH):
                ada(layer)
                for j in range(3):
                    norm(layer, f"norm{j}")
                    ready = (h_ready, DB * (norms[0] - 1))
                    if j != 1:
                        for half in "ab":
                            linear(layer, f"up{j // 2}{half}", 2 * HALF_F, DB, h_hi, h_lo, ready=ready)
                            halves += 1
                            pe.wait_ge(gated_ready, HALF_F * halves + 1)
                            linear(layer, f"down{j // 2}{half}", DB, HALF_F, g_hi, g_lo, HALF_F * halves + 2)
                    elif layer == 0:
                        linear(layer, "ret", RET_BLOCKS, DB, h_hi, h_lo, ready=ready)
                        tensor_retention(pe)
                        linear(layer, "rwkv", RWKV_BLOCKS, DB, h_hi, h_lo)
                        tensor_rwkv(pe)
                    else:
                        linear(layer, "mlstm", MLSTM_BLOCKS, DB, h_hi, h_lo, ready=ready)
                        tensor_mlstm(pe)
                        linear(layer, "att", ATT_BLOCKS, DB, h_hi, h_lo)
                        tensor_attention(pe)
                    if j == 1:
                        linear(layer, "out", DB, DB, h_hi, h_lo, ready=(mix_split, DB * layer))
            norm(DEPTH, "norm")


        @block.scalar
        def _(act):
            turn = Order(act, act_chain)
            act.wait_ge(par_loaded, 16)
            act.activation(scond[:, :, :], grid(prm("cond", 0, 2 * DB), DB, 2), ACT.Silu).then_inc(cond_ready, 1)
            act.sem_inc(ada_row_ready, 2)
            act.sem_inc(free_act, SETS)

            norms, fblocks, projected = [0], [0], [0]

            def parts(layer, name):
                for n in parts_first(act, tile0[layer, name]):
                    high_part(act, n)

            def only_parts(layer, name, n):
                n0 = tile0[layer, name]
                parts(layer, name)

                def one(i, u, split_ahead):
                    act.wait_ge(tiles_done, i * 4 + SPLITS + n0 + u + 1)
                    split_ahead()
                stepped(act, n0, n, high_part, one)

            def ada(layer):
                n0 = tile0[layer, "ada"]

                def row(i, u):
                    act.wait_ge(tiles_done, i * 4 * DB + SPLITS + n0 + (u + 1) * DB)
                    act.activation(ada_row[:, bass.ds(i * 4 * D_MODEL + u * D_MODEL, D_MODEL)],
                                   ps[0:2, u % 2 * D_MODEL:(u % 2 + 1) * D_MODEL], ACT.Copy)\
                       .then_inc(ada_row_ready, 1)
                looped(act, N_MOD, row)
                act.sem_inc(high_ready, N_MOD * DB)
                parts(layer, "up0a")

            def norm(layer, name, shift):
                q = norms[0]
                for k in range(DB):
                    if q:
                        act.wait_ge(x_ready, x0[layer, name] - DB + k + 1)
                    act.activation(squares(name)[:, k, :], x[:, k, :], ACT.Square).then_inc(sq_ready, 1)
                act.wait_ge(ms_ready, q + 1)
                turn(act.activation(rs[:, :], rs[:, :], ACT.Ln))
                act.activation(rs[:, :], rs[:, :], ACT.Exp, scale=-0.5).then_inc(root_ready, 1)
                if shift is not None:
                    for k in range(DB):
                        act.wait_ge(scaled, DB * q + k + 1)
                        act.activation(h_hi[:, k, PROMPT], normed[:, k % 2, PROMPT], ACT.Identity,
                                       bias=mod[:, shift * DB + k, 0:1])
                        act.activation(h_hi[:, k, SAMPLE], normed[:, k % 2, SAMPLE], ACT.Identity,
                                       bias=mod[:, shift * DB + k, 1:2]).then_inc(h_high, 1)
                norms[0] += 1

            def up(layer, name):
                b0, n0, g0 = blk0[layer, name], tile0[layer, name], fblocks[0]

                def one(i, u, split_ahead):
                    act.wait_ge(tiles_done, i * 4 + SPLITS + n0 + u + 1)
                    split_ahead()
                    f = u // 2
                    if u % 2 == 0:
                        act.activation(silu[:, f % 2, :], pair((b0 + u) % SETS)[2], ACT.Silu).then_inc(silu_ready, 1)
                    else:
                        act.wait_ge(prod_ready, i * 2 + g0 + f + 1)
                        act.activation(g_hi[:, i * 2 + f, :], prod[:, f % 2, :], ACT.Copy).then_inc(g_high, 1)
                stepped(act, n0, 2 * HALF_F, high_part, one)
                fblocks[0] += HALF_F

            def project(layer, name, n, dst):
                b0, n0, p0 = blk0[layer, name], tile0[layer, name], projected[0]
                parts(layer, name)

                def one(i, u, split_ahead):
                    act.wait_ge(tiles_done, i * 4 + SPLITS + n0 + u + 1)
                    split_ahead()
                    act.activation(dst[:, i * 4 + u, :], pair((b0 + u) % SETS)[2], ACT.Copy)\
                       .then_inc(proj_ready, 1)
                    act.wait_ge(proj_ready, i * 4 + p0 + u + 1)
                    act.sem_inc(free_act, 1)
                stepped(act, n0, n, high_part, one)
                projected[0] += n

            for layer in range(DEPTH):
                ada(layer)
                act.wait_ge(loaded, 48)
                act.wait_ge(mod_ready, layer + 1)
                for j in range(3):
                    norm(layer, f"norm{j}", 3 * j)
                    if j != 1:
                        for half in "ab":
                            up(layer, f"up{j // 2}{half}")
                            only_parts(layer, f"down{j // 2}{half}", DB)
                        continue
                    if layer == 0:
                        project(layer, "ret", RET_BLOCKS, rt_p)
                        scalar_retention(act, turn)
                        act.wait_ge(mix_ready, 4)
                        act.wait_ge(saved, 32)
                        project(layer, "rwkv", RWKV_BLOCKS, rw_p)
                        scalar_rwkv(act, turn)
                    else:
                        project(layer, "mlstm", MLSTM_BLOCKS, ml_p)
                        scalar_mlstm(act, turn)
                        act.wait_ge(mix_ready, 12)
                        act.wait_ge(saved, 16 * 8)
                        project(layer, "att", ATT_BLOCKS, at_p)
                        scalar_attention(act, turn)
                    act.wait_ge(mix_ready, 8 * (layer + 1))
                    for k in range(DB):
                        act.activation(h_hi[:, k, :], mix[:, k, :], ACT.Copy).then_inc(mix_high, 1)
                    only_parts(layer, "out", DB)
            norm(DEPTH, "norm", None)


        @block.vector
        def _(dve):
            turn = Order(dve, dve_chain)
            dve.sem_inc(free_dve, SETS)
            dve.sem_inc(gated_ready, 2)
            dve.sem_inc(split_ready, RING)

            norms, fblocks = [0], [0]

            def parts(layer, name):
                for n in parts_first(dve, tile0[layer, name]):
                    low_part(dve, n)

            def only_parts(layer, name, n, then=None):
                parts(layer, name)

                def one(i, u, split_ahead):
                    split_ahead()
                    if then is not None:
                        then(i, u)
                stepped(dve, tile0[layer, name], n, low_part, one)

            def modulation(layer):
                def free(i, u):
                    dve.wait_ge(tiles_done, i * 4 + SPLITS + tile0[layer, "ada"] + u + 1)
                    dve.sem_inc(split_ready, 1)
                looped(dve, N_MOD * DB, free)
                parts(layer, "up0a")
                dve.wait_ge(ada_turned, layer + 1)
                dve.wait_ge(par_loaded, 16)
                dve.wait_ge(loaded, 48)
                src = grid(bank(4, 0, 2 * N_MOD * DB), N_MOD * DB, 2)
                turn(dve.tensor_tensor(mod[:, :, :], src, over(prm("ada_b", layer * N_MOD * DB, N_MOD * DB), 2),
                                       ALU.add))
                dve.sem_inc(free_dve, 1)
                for g in (2, 8):
                    m = mod[:, g * DB:(g + 1) * DB, :]
                    turn(dve.tensor_scalar(m, m, 0.5, None, ALU.mult))
                for j in range(3):
                    last = dve.scalar_tensor_tensor(out=gs[:, j, :, :], in0=mod[:, (3 * j + 1) * DB:(3 * j + 2) * DB, :],
                                                    scalar=1.0, in1=over(prm("norm_g", (3 * layer + j) * DB, DB), 2),
                                                    op0=ALU.add, op1=ALU.mult)
                turn(last)
                dve.sem_inc(mod_ready, 1)

            def norm(layer, name, j):
                q = norms[0]
                dve.wait_ge(norm_ready, q + 1)
                dve.tensor_scalar(rs[:, :], pair(blk0[layer, name] % SETS)[2], 1.0 / D_MODEL, EPS, ALU.mult, ALU.add)\
                   .then_inc(ms_ready, 1)
                dve.wait_ge(root_ready, q + 1)
                dve.sem_inc(free_dve, 1)

                def low(k):
                    dve.wait_ge(h_high, DB * q + k + 1)
                    for part, cond in ((PROMPT, 0), (SAMPLE, 1)):
                        shift = mod[:, 3 * j * DB + k, cond:cond + 1]
                        ins = dve.scalar_tensor_tensor(out=h_lo[:, k, part], in0=normed[:, k % 2, part], scalar=shift,
                                                       in1=h_hi[:, k, part].bitcast(F32),
                                                       op0=ALU.add, op1=ALU.subtract)
                    ins.then_inc(h_ready, 1)

                for k in range(DB):
                    if j is None:
                        dve.scalar_tensor_tensor(out=y[:, k, :], in0=x[:, k, :], scalar=prm("final", k),
                                                 in1=rs[:, :], op0=ALU.mult, op1=ALU.mult).then_inc(y_ready, 1)
                        continue
                    if k >= 2:
                        dve.wait_ge(h_ready, DB * q + k - 1)
                    for part, cond in ((PROMPT, 0), (SAMPLE, 1)):
                        ins = dve.scalar_tensor_tensor(out=normed[:, k % 2, part], in0=x[:, k, part],
                                                       scalar=gs[:, j, k, cond:cond + 1], in1=rs[:, part],
                                                       op0=ALU.mult, op1=ALU.mult)
                    ins.then_inc(scaled, 1)
                    if k:
                        low(k - 1)
                if j is not None:
                    low(DB - 1)
                norms[0] += 1

            def up(layer, name):
                b0, n0, g0 = blk0[layer, name], tile0[layer, name], fblocks[0]

                def one(i, u, split_ahead):
                    dve.wait_ge(tiles_done, i * 4 + SPLITS + n0 + u + 1)
                    split_ahead()
                    f = u // 2
                    if u % 2:
                        dve.wait_ge(silu_ready, i * 2 + g0 + f + 1)
                        dve.wait_ge(gated_ready, i * 2 + g0 + f + 1)
                        dve.tensor_tensor(prod[:, f % 2, :], silu[:, f % 2, :], pair((b0 + u) % SETS)[2], ALU.mult)\
                           .then_inc(prod_ready, 1)
                        dve.wait_ge(g_high, i * 2 + g0 + f + 1)
                        dve.sem_inc(free_dve, 2)
                        dve.tensor_tensor(g_lo[:, i * 2 + f, :], prod[:, f % 2, :],
                                          g_hi[:, i * 2 + f, :].bitcast(F32), ALU.subtract).then_inc(gated_ready, 1)
                stepped(dve, n0, 2 * HALF_F, low_part, one)
                fblocks[0] += HALF_F

            def residual(layer, name, gate):
                b0, n0, xn = blk0[layer, name], tile0[layer, name], x0[layer, name]
                parts(layer, name)

                def one(i, u, split_ahead):
                    dve.wait_ge(tiles_done, i * 4 + SPLITS + n0 + u + 1)
                    split_ahead()
                    src = pair((b0 + u) % SETS)[2]
                    for part, cond in ((PROMPT, 0), (SAMPLE, 1)):
                        xb = x[:, i * 4 + u, part]
                        ins = dve.scalar_tensor_tensor(out=xb, in0=src[:, part],
                                                       scalar=mod[:, i * 4 + (gate * DB + u), cond:cond + 1],
                                                       in1=xb, op0=ALU.mult, op1=ALU.add)
                    ins.then_inc(x_ready, 1)
                    dve.wait_ge(x_ready, i * 4 + xn + u + 1)
                    dve.sem_inc(free_dve, 1)
                stepped(dve, n0, DB, low_part, one)

            for layer in range(DEPTH):
                modulation(layer)
                for j in range(3):
                    norm(layer, f"norm{j}", j)
                    if j != 1:
                        for half in "ab":
                            up(layer, f"up{j // 2}{half}")
                            residual(layer, f"down{j // 2}{half}", 2 + 3 * j)
                        continue
                    if layer == 0:
                        only_parts(layer, "ret", RET_BLOCKS)
                        vector_retention(dve, turn)
                        only_parts(layer, "rwkv", RWKV_BLOCKS, lambda i, u: vector_shift(dve, i, u))
                        vector_rwkv(dve, turn)
                    else:
                        only_parts(layer, "mlstm", MLSTM_BLOCKS)
                        vector_mlstm(dve, turn)
                        only_parts(layer, "att", ATT_BLOCKS)
                        vector_attention(dve, turn)
                    for k in range(DB):
                        dve.wait_ge(mix_high, DB * layer + k + 1)
                        dve.tensor_tensor(h_lo[:, k, :], mix[:, k, :], h_hi[:, k, :].bitcast(F32), ALU.subtract)\
                           .then_inc(mix_split, 1)
                    residual(layer, "out", 5)
            norm(DEPTH, "norm", None)


        @block.gpsimd
        def _(pool):
            pool.dma_start(cst[:, :], consts_in).then_inc(loaded, 16)
            pool.dma_start(x[:, :, :], x_in).then_inc(loaded, 16)
            pool.dma_start(lora[:, :, :], lora_in).then_inc(loaded, 16)
            pool_retention(pool)
            pool_rwkv(pool)
            pool_mlstm(pool)
            pool_attention(pool)
            pool.wait_ge(saved, 16 * 11)



def _tiles(a, k):
    r, c = a.shape
    t = a.reshape(r // (k * P), k, P, c // P, P).transpose(3, 0, 2, 1, 4)
    return np.ascontiguousarray(t.reshape(-1, P, k * P))


def _cols(v):
    return np.ascontiguousarray(v).reshape(-1, P).T


def kernel(**inputs):
    import concourse.bacc as _bacc
    from concourse.bass_utils import run_bass_kernel_spmd as _run

    v = {k: np.asarray(a) for k, a in inputs.items()}
    f = np.float32
    arrays = {}
    tok = np.concatenate([v["x_prompt"][0], v["x_sample"][0]], 0)
    arrays["x_in"] = np.ascontiguousarray(tok.T.reshape(DB, P, NT).transpose(1, 0, 2))
    at, table = const_layout()
    arrays["consts"] = table

    for layer in range(DEPTH):
        arrays[f"w{layer}_ada"] = np.ascontiguousarray(
            v["ada_w"][layer].reshape(DB, P, N_MOD, D_MODEL).transpose(2, 0, 1, 3).reshape(-1, P, D_MODEL))
        for j in range(2):
            w1 = v["ffn_w1"][layer, j].reshape(D_MODEL, 2, FB, P).transpose(0, 2, 1, 3).reshape(D_MODEL, -1)
            for half in range(2):
                cols = slice(half * 2 * HALF_F * P, (half + 1) * 2 * HALF_F * P)
                arrays[f"w{layer}_up{j}{'ab'[half]}"] = _tiles(w1[:, cols], DB)
            for half in range(2):
                rows_ = slice(half * HALF_F * P, (half + 1) * HALF_F * P)
                arrays[f"w{layer}_down{j}{'ab'[half]}"] = _tiles(v["ffn_w2"][layer, j][rows_], HALF_F)
    even, odd = v["w_in_even"][0], v["w_in_odd"][0]
    arrays["w0_ret"] = _tiles(even[:, :RET_BLOCKS * P], DB)
    arrays["w0_rwkv"] = _tiles(even[:, RET_BLOCKS * P:], DB)
    arrays["w0_out"] = _tiles(v["w_out_even"][0], DB)
    gates = np.zeros((2, D_MODEL, P), f)
    for g in range(2):
        for d in range(2):
            gates[g, :, 32 * d:32 * d + 4] = odd[:, 1536 + 8 * g + 4 * d:1536 + 8 * g + 4 * d + 4]
    arrays["w1_mlstm"] = _tiles(np.concatenate([odd[:, :1536], gates[0], gates[1], odd[:, 1552:2064]], 1), DB)
    q, k0, k1, vv = odd[:, 2064:2576], odd[:, 2576:2640], odd[:, 2640:2704], odd[:, 2704:2832]
    arrays["w1_att"] = _tiles(np.concatenate([q, k0, k0, k1, k1, vv], 1), DB)
    arrays["w1_out"] = _tiles(v["w_out_odd"][0], DB)

    pat, npar = param_layout()
    par = np.zeros((P, npar), f)

    def put(name, a):
        par[:a.shape[0], pat[name][0]:pat[name][0] + a.shape[1]] = a

    def rows(a):
        r = np.zeros((P, 1), f)
        r[0:4, 0], r[32:36, 0] = a[0], a[1]
        return r

    for name, key in (("norm_g", "norm_g"), ("final", "final_norm"), ("ada_b", "ada_b"), ("gn_w", "ret_gn_w"),
                      ("mu", "rwkv_mu"), ("w0", "rwkv_w0"), ("a0", "rwkv_a0"), ("k_k", "rwkv_k_k"),
                      ("k_a", "rwkv_k_a"), ("r_k", "rwkv_r_k"), ("ln_w", "rwkv_ln_w"), ("ln_b", "rwkv_ln_b"),
                      ("mn_w", "mlstm_norm_w")):
        put(name, _cols(v[key]))
    put("q_gain", np.tile(v["attn_qk_norm"][0, 0], 2)[:, None])
    put("k_gain", np.tile(v["attn_qk_norm"][0, 1], 2)[:, None])
    lg = v["ret_log_decay"][0]
    put("lg_head", np.tile(lg.reshape(1, 8), (P, 1)))
    put("lg_part", np.repeat(lg.reshape(2, 2, 2), HS, axis=2).reshape(4, P).T)
    put("m_init", rows(v["state_mlstm_m"][0, 0]))
    put("i_bias", rows(v["mlstm_i_bias"][0]))
    put("f_bias", rows(v["mlstm_f_bias"][0]))
    cond = np.stack([v["c_ctx"], v["c"][0]], 1)
    put("cond", cond.reshape(DB, P, 2).transpose(1, 0, 2).reshape(P, 2 * DB))
    arrays["params"] = par
    lora = np.zeros((P, 3, 512), f)
    for d in range(2):
        lora[:HS, d], lora[HS:, d] = v["rwkv_w2"][0, d], v["rwkv_a2"][0, d]
    lora[:, 2] = v["rwkv_g2"][0]
    arrays["lora_in"] = lora

    arrays["s_ret"] = v["state_ret"][0, 0].reshape(2, 2, P, P).transpose(0, 2, 1, 3)
    arrays["s_rwkv"] = v["state_rwkv"][0, 0].transpose(0, 1, 3, 2).reshape(2, 4, P, HS).transpose(0, 2, 1, 3)
    arrays["s_mc"] = np.concatenate([v["state_mlstm_c"][0, 0], v["state_mlstm_n"][0, 0][..., None]], -1)\
        .transpose(0, 2, 1, 3)
    ck = v["cache_k"][0, 0].transpose(2, 0, 1)
    arrays["s_ck"] = np.concatenate([ck, ck], 0)
    arrays["s_cv"] = v["cache_v"][0, 0].transpose(1, 0, 2)

    nc = _bacc.Bacc("TRN2", target_bir_lowering=False, num_devices=1)
    arrays = {k: np.ascontiguousarray(a) for k, a in arrays.items()}
    ap = {k: nc.dram_tensor(k, a.shape, F32, kind="ExternalInput").ap() for k, a in arrays.items()}
    shapes = {"y": (P, DB, NT), "ret": (2, P, 2, P), "rwkv": (2, P, 4, HS), "mc": (2, P, 4, P + 1),
              "m": (2, 4, 1), "ck": (2, HS, P), "cv": (P, P)}
    outs = {k: nc.dram_tensor(f"out_{k}", s, F32, kind="ExternalOutput").ap() for k, s in shapes.items()}
    w = [{n: ap[f"w{layer}_{n}"] for n, _, k in stages_of_layer(layer) if k} for layer in range(DEPTH)]
    st = {k: ap[k] for k in ("s_ret", "s_rwkv", "s_mc", "s_ck", "s_cv")}
    build(nc, w, ap["x_in"], ap["consts"], ap["params"], ap["lora_in"], st, outs)
    r = _run(nc, [arrays], core_ids=[0]).results[0]
    y = r["out_y"].transpose(2, 1, 0).reshape(NT, D_MODEL)
    ret = r["out_ret"].transpose(0, 2, 1, 3).reshape(1, 1, 2, 4, HS, P)
    rwkv = r["out_rwkv"].transpose(0, 2, 1, 3).reshape(2, 8, HS, HS).transpose(0, 1, 3, 2)[None, None]
    mc = r["out_mc"].transpose(0, 2, 1, 3)
    out = (y[None, :SEQ], y[None, SEQ:], ret, rwkv, mc[None, None, ..., :P], mc[None, None, ..., P],
           r["out_m"].reshape(1, 1, 2, 4), r["out_ck"].transpose(0, 2, 1)[None, None],
           r["out_cv"].reshape(P, 2, HS).transpose(1, 0, 2)[None, None])
    return tuple(np.ascontiguousarray(a) for a in out)
```
